# Optimizing a Trainium2 kernel written in Bass

```python
import math
import jax, jax.numpy as jnp
from jax import lax
import numpy as np

D_MODEL = 1024
BATCH = 1
SEQ = 256
DEPTH = 2

GLA_HEADS = 4
GLA_DK = 64
GLA_DV = 128
GLA_RANK = 16
GLA_TAU = 16.0
GLA_CHUNK = 64
DIFF_HEADS = 4
DIFF_DH = 64
DIFF_DV = 2 * DIFF_DH
Q_BLOCK = 128
A_QK = GLA_HEADS * GLA_DK
A_V = GLA_HEADS * GLA_DV
B_QK = DIFF_HEADS * 2 * DIFF_DH
B_V = DIFF_HEADS * DIFF_DV
EVEN_IN = 2 * A_QK + 2 * A_V + GLA_RANK + 2 * B_QK + B_V
EVEN_MIX = A_V + B_V
DIL_PATTERNS = ((128, 1), (512, 4), (2048, 16))
DIL_GROUPS = 3
DIL_HEADS = 4
DIL_DH = 128
ODD_IN = DIL_GROUPS * 3 * DIL_HEADS * DIL_DH
ODD_MIX = DIL_HEADS * DIL_DH
D_FF = 2816
CONV_W = 3
EPS = 1e-6
N_EVEN = (DEPTH + 1) // 2
N_ODD = DEPTH // 2


def rmsnorm(x, g):
    xf = x.astype(jnp.float32)
    y = xf * lax.rsqrt(jnp.mean(xf * xf, axis=-1, keepdims=True) + EPS)
    return (y * g.astype(jnp.float32)).astype(x.dtype)

def gla(q, k, v, log_a):
    B, S, H, dk = q.shape
    dv = v.shape[-1]
    C = GLA_CHUNK
    N = S // C
    f32 = jnp.float32

    def chunk(t):
        return t.astype(f32).reshape(B, N, C, H, t.shape[-1]).transpose(0, 3, 1, 2, 4)

    qc, kc, vc, lc = chunk(q * (dk ** -0.5)), chunk(k), chunk(v), chunk(log_a)
    b = jnp.cumsum(lc, axis=3)
    b_last = b[:, :, :, -1:, :]
    q_d = qc * jnp.exp(b)
    k_d = kc * jnp.exp(-b)
    causal = jnp.tril(jnp.ones((C, C), dtype=bool))
    att = jnp.where(causal, jnp.einsum('bhnik,bhnjk->bhnij', q_d, k_d), 0.0)
    o_intra = jnp.einsum('bhnij,bhnjv->bhniv', att, vc)
    kv = jnp.einsum('bhnjk,bhnjv->bhnkv', kc * jnp.exp(b_last - b), vc)
    decay = jnp.exp(b_last[:, :, :, 0, :])

    def step(state, inp):
        kv_n, dec_n = inp
        return dec_n[..., None] * state + kv_n, state

    s0 = jnp.zeros((B, H, dk, dv), f32)
    _, states = lax.scan(step, s0, (jnp.moveaxis(kv, 2, 0), jnp.moveaxis(decay, 2, 0)))
    states = jnp.moveaxis(states, 0, 2)
    o = o_intra + jnp.einsum('bhnik,bhnkv->bhniv', q_d, states)
    return o.transpose(0, 2, 3, 1, 4).reshape(B, S, H, dv).astype(v.dtype)

def diff_attention(q, k, v, lam):
    B, S, H, _, dh = q.shape
    dv = v.shape[-1]
    nb = S // Q_BLOCK
    qb = (q * (dh ** -0.5)).reshape(B, nb, Q_BLOCK, H, 2, dh).transpose(1, 0, 3, 4, 2, 5)
    kt = k.transpose(0, 2, 3, 1, 4)
    vt = v.transpose(0, 2, 1, 3)
    kpos = jnp.arange(S)

    def block(args):
        qblk, n = args
        s = jnp.einsum('bhcqd,bhckd->bhcqk', qblk, kt).astype(jnp.float32)
        qpos = n * Q_BLOCK + jnp.arange(Q_BLOCK)
        s = jnp.where(kpos[None, :] <= qpos[:, None], s, -jnp.inf)
        p = jax.nn.softmax(s, axis=-1)
        w = p[:, :, 0] - lam * p[:, :, 1]
        return jnp.einsum('bhqk,bhkv->bhqv', w.astype(vt.dtype), vt)

    o = lax.map(block, (qb, jnp.arange(nb)))
    return o.transpose(1, 0, 3, 2, 4).reshape(B, S, H, dv)

def dilated_branch(q, k, v, dilation, wc):
    B, S, H, dh = q.shape
    L = S // dilation
    nb = -(-L // wc)
    Lp = nb * wc

    def to_class(t):
        t = t.reshape(B, L, dilation, H, dh).transpose(0, 2, 3, 1, 4)
        t = jnp.pad(t, ((0, 0), (0, 0), (0, 0), (0, Lp - L), (0, 0)))
        return t.reshape(B, dilation, H, nb, wc, dh)

    def band(t):
        prev = jnp.pad(t, ((0, 0),) * 3 + ((1, 0), (0, 0), (0, 0)))[:, :, :, :-1]
        return jnp.concatenate([prev, t], axis=-2)

    qc = to_class(q)
    kb = band(to_class(k))
    vb = band(to_class(v))
    s = jnp.einsum('brhnqd,brhnkd->brhnqk', qc, kb).astype(jnp.float32) * (dh ** -0.5)
    i = jnp.arange(wc)[:, None]
    j = jnp.arange(2 * wc)[None, :]
    dist = i + wc - j
    blk = jnp.arange(nb)[:, None, None]
    valid = (dist >= 0) & (dist <= wc) & ((blk > 0) | (j >= wc))
    s = jnp.where(valid, s, -jnp.inf)
    lse = jax.nn.logsumexp(s, axis=-1)
    p = jnp.exp(s - lse[..., None])
    o = jnp.einsum('brhnqk,brhnkd->brhnqd', p.astype(vb.dtype), vb)
    o = o.reshape(B, dilation, H, Lp, dh)[:, :, :, :L].transpose(0, 3, 1, 2, 4).reshape(B, S, H, dh)
    lse = lse.reshape(B, dilation, H, Lp)[..., :L].transpose(0, 3, 1, 2).reshape(B, S, H)
    return o, lse

def even_mixer(h, w_in, w_a2, b_a, gla_gain, dq_gain, dk_gain, lq1, lk1, lq2, lk2, diff_gain, w_out, lambda_init):
    B, S, _ = h.shape
    z = h @ w_in
    sizes = [A_QK, A_QK, A_V, A_V, GLA_RANK, B_QK, B_QK]
    aq, ak, av, ag, ar, bq, bk, bv = jnp.split(z, [int(c) for c in np.cumsum(sizes)], axis=-1)
    log_a = jax.nn.log_sigmoid((ar @ w_a2 + b_a).astype(jnp.float32)) / GLA_TAU
    oa = gla(aq.reshape(B, S, GLA_HEADS, GLA_DK), ak.reshape(B, S, GLA_HEADS, GLA_DK),
             av.reshape(B, S, GLA_HEADS, GLA_DV), log_a.reshape(B, S, GLA_HEADS, GLA_DK))
    oa = rmsnorm(oa, gla_gain) * jax.nn.silu(ag.reshape(B, S, GLA_HEADS, GLA_DV))
    bq = rmsnorm(bq.reshape(B, S, DIFF_HEADS, 2, DIFF_DH), dq_gain)
    bk = rmsnorm(bk.reshape(B, S, DIFF_HEADS, 2, DIFF_DH), dk_gain)
    f32 = jnp.float32
    lam = (jnp.exp(jnp.sum(lq1.astype(f32) * lk1.astype(f32)))
           - jnp.exp(jnp.sum(lq2.astype(f32) * lk2.astype(f32))) + lambda_init)
    ob = diff_attention(bq, bk, bv.reshape(B, S, DIFF_HEADS, DIFF_DV), lam)
    ob = rmsnorm(ob, diff_gain) * (1.0 - lambda_init)
    o = jnp.concatenate([oa.reshape(B, S, A_V), ob.reshape(B, S, B_V)], axis=-1)
    return o @ w_out

def odd_mixer(h, w_in, q_gain, k_gain, w_out):
    B, S, _ = h.shape
    z = (h @ w_in).reshape(B, S, DIL_GROUPS, 3, DIL_HEADS, DIL_DH)
    q = rmsnorm(z[:, :, :, 0], q_gain)
    k = rmsnorm(z[:, :, :, 1], k_gain)
    v = z[:, :, :, 2]
    outs, lses = [], []
    for g, (window, dilation) in enumerate(DIL_PATTERNS):
        o_g, lse_g = dilated_branch(q[:, :, g], k[:, :, g], v[:, :, g], dilation, window // dilation)
        outs.append(o_g)
        lses.append(lse_g)
    wts = jax.nn.softmax(jnp.stack(lses, axis=0), axis=0)
    o = jnp.sum(wts[..., None].astype(v.dtype) * jnp.stack(outs, axis=0), axis=0)
    return o.reshape(B, S, ODD_MIX) @ w_out

def conv_ffn(h, w_up, conv_w, conv_b, w_down):
    u = h @ w_up
    u = lax.conv_general_dilated(u, conv_w, window_strides=(1,), padding=[(CONV_W - 1, 0)],
                                 dimension_numbers=('NWC', 'WIO', 'NWC'),
                                 feature_group_count=2 * D_FF) + conv_b
    gate, val = jnp.split(u, 2, axis=-1)
    return (jax.nn.silu(gate) * val) @ w_down

def first_inputs(seed: int = 0) -> dict:
    key = jax.random.key(seed)
    ks = iter(jax.random.split(key, 32))
    nrm = lambda shape, scale: jax.random.normal(next(ks), shape, jnp.float32) * scale
    gain = lambda shape: 1.0 + nrm(shape, 0.02)
    return {
        "x": nrm((BATCH, SEQ, D_MODEL), 1.0),
        "norm_mix": gain((DEPTH, D_MODEL)),
        "norm_ffn": gain((DEPTH, D_MODEL)),
        "ev_w_in": nrm((N_EVEN, D_MODEL, EVEN_IN), D_MODEL ** -0.5),
        "ev_w_a2": nrm((N_EVEN, GLA_RANK, A_QK), GLA_RANK ** -0.5),
        "ev_b_a": nrm((N_EVEN, A_QK), 0.1),
        "ev_gla_gain": gain((N_EVEN, GLA_DV)),
        "ev_dq_gain": gain((N_EVEN, DIFF_DH)),
        "ev_dk_gain": gain((N_EVEN, DIFF_DH)),
        "ev_lq1": nrm((N_EVEN, DIFF_DH), 0.1),
        "ev_lk1": nrm((N_EVEN, DIFF_DH), 0.1),
        "ev_lq2": nrm((N_EVEN, DIFF_DH), 0.1),
        "ev_lk2": nrm((N_EVEN, DIFF_DH), 0.1),
        "ev_diff_gain": gain((N_EVEN, DIFF_DV)),
        "ev_w_out": nrm((N_EVEN, EVEN_MIX, D_MODEL), EVEN_MIX ** -0.5),
        "od_w_in": nrm((N_ODD, D_MODEL, ODD_IN), D_MODEL ** -0.5),
        "od_q_gain": gain((N_ODD, DIL_DH)),
        "od_k_gain": gain((N_ODD, DIL_DH)),
        "od_w_out": nrm((N_ODD, ODD_MIX, D_MODEL), ODD_MIX ** -0.5),
        "ffn_w_up": nrm((DEPTH, D_MODEL, 2 * D_FF), D_MODEL ** -0.5),
        "ffn_conv_w": nrm((DEPTH, CONV_W, 1, 2 * D_FF), CONV_W ** -0.5),
        "ffn_conv_b": nrm((DEPTH, 2 * D_FF), 0.01),
        "ffn_w_down": nrm((DEPTH, D_FF, D_MODEL), D_FF ** -0.5),
    }

def first_block(x, norm_mix, norm_ffn, ev_w_in, ev_w_a2, ev_b_a, ev_gla_gain, ev_dq_gain, ev_dk_gain,
              ev_lq1, ev_lk1, ev_lq2, ev_lk2, ev_diff_gain, ev_w_out, od_w_in, od_q_gain, od_k_gain,
              od_w_out, ffn_w_up, ffn_conv_w, ffn_conv_b, ffn_w_down):
    for i in range(DEPTH):
        h = rmsnorm(x, norm_mix[i])
        if i % 2 == 0:
            e = i // 2
            lambda_init = 0.8 - 0.6 * math.exp(-0.3 * i)
            x = x + even_mixer(h, ev_w_in[e], ev_w_a2[e], ev_b_a[e], ev_gla_gain[e], ev_dq_gain[e],
                               ev_dk_gain[e], ev_lq1[e], ev_lk1[e], ev_lq2[e], ev_lk2[e],
                               ev_diff_gain[e], ev_w_out[e], lambda_init)
        else:
            o = i // 2
            x = x + odd_mixer(h, od_w_in[o], od_q_gain[o], od_k_gain[o], od_w_out[o])
        x = x + conv_ffn(rmsnorm(x, norm_ffn[i]), ffn_w_up[i], ffn_conv_w[i], ffn_conv_b[i], ffn_w_down[i])
    return x


HEAD_DIM = 64
D_MIX = D_MODEL
DN_HEADS = 6
DN_WIDTH = DN_HEADS * HEAD_DIM
FX_HEADS = 6
FX_WIDTH = FX_HEADS * HEAD_DIM
POOL_GROUPS = 4
POOL_WIDTH = D_MIX - DN_WIDTH - FX_WIDTH
POOL_GROUP_DIM = POOL_WIDTH // POOL_GROUPS
POOL_WINDOWS = (2, 4, 8, 16)
CONV_WIDTH = 4
DN_CHUNK = 64
FX_BLOCK = 128
N_EXPERTS = 8
TOP_K = 2
D_FF_EXPERT = 1536
N_DENSE = (DEPTH + 1) // 2
N_MOE = DEPTH // 2
N_IN = 4 * DN_WIDTH + 2 * DN_HEADS + 3 * FX_WIDTH + FX_HEADS + POOL_WIDTH


F32 = jnp.float32

def rmsnorm_2(x, g):
    xf = x.astype(F32)
    y = xf * lax.rsqrt(jnp.mean(xf * xf, axis=-1, keepdims=True) + EPS)
    return (y * g.astype(F32)).astype(x.dtype)

def l2norm(x):
    return x * lax.rsqrt(jnp.sum(x * x, axis=-1, keepdims=True) + EPS)

def causal_conv(x, w):
    c = x.shape[-1]
    return lax.conv_general_dilated(x, w.astype(x.dtype)[:, None, :], window_strides=(1,),
                                    padding=[(CONV_WIDTH - 1, 0)],
                                    dimension_numbers=('NWC', 'WIO', 'NWC'),
                                    feature_group_count=c)

def chunk_gated_delta_rule(q, k, v, g, beta):
    B, T, H, Dk = q.shape
    Dv = v.shape[-1]
    C = DN_CHUNK
    N = T // C

    def to_chunks(a):
        a = a.reshape((B, N, C, H) + a.shape[3:])
        return jnp.moveaxis(a, 3, 1)

    q, k, v, g, beta = (to_chunks(a) for a in (q, k, v, g, beta))
    G = jnp.cumsum(g, axis=-1)
    causal = jnp.tril(jnp.ones((C, C), bool))
    strict = jnp.tril(jnp.ones((C, C), bool), -1)
    diff = G[..., :, None] - G[..., None, :]
    decay = jnp.where(causal, jnp.exp(jnp.where(causal, diff, 0.0)), 0.0)
    kb = k * beta[..., None]
    a_mat = jnp.where(strict, jnp.einsum('bhnid,bhnjd->bhnij', kb, k) * decay, 0.0)
    eye = jnp.eye(C, dtype=q.dtype)
    rhs = jnp.concatenate([v * beta[..., None], kb * jnp.exp(G)[..., None]], axis=-1)
    uw = lax.linalg.triangular_solve(a_mat + eye, rhs, left_side=True, lower=True,
                                     transpose_a=False, conjugate_a=False, unit_diagonal=True)
    u, w = uw[..., :Dv], uw[..., Dv:]
    qk = jnp.where(causal, jnp.einsum('bhnid,bhnjd->bhnij', q, k) * decay, 0.0)
    q_dec = q * jnp.exp(G)[..., None]
    k_dec = k * jnp.exp(G[..., -1:] - G)[..., None]
    last = jnp.exp(G[..., -1])

    def step(S, xs):
        u_n, w_n, qk_n, q_n, k_n, l_n = xs
        v_new = u_n - jnp.einsum('bhck,bhkv->bhcv', w_n, S)
        o_n = jnp.einsum('bhck,bhkv->bhcv', q_n, S) + jnp.einsum('bhij,bhjv->bhiv', qk_n, v_new)
        S = S * l_n[..., None, None] + jnp.einsum('bhck,bhcv->bhkv', k_n, v_new)
        return S, o_n

    xs = tuple(jnp.moveaxis(a, 2, 0) for a in (u, w, qk, q_dec, k_dec, last))
    S0 = jnp.zeros((B, H, Dk, Dv), q.dtype)
    _, o = lax.scan(step, S0, xs)
    return jnp.transpose(o, (1, 0, 3, 2, 4)).reshape(B, T, H, Dv)

def gated_deltanet(q, k, v, z, a, b, conv_w, a_log, dt_bias, onorm_g):
    B, T, _ = q.shape
    dt = q.dtype
    qkv = jax.nn.silu(causal_conv(jnp.concatenate([q, k, v], axis=-1), conv_w)).astype(F32)
    q, k, v = jnp.split(qkv, 3, axis=-1)
    heads = lambda t: t.reshape(B, T, DN_HEADS, HEAD_DIM)
    q = l2norm(heads(q)) * (HEAD_DIM ** -0.5)
    k = l2norm(heads(k))
    v = heads(v)
    beta = jax.nn.sigmoid(b.astype(F32))
    g = -jnp.exp(a_log.astype(F32)) * jax.nn.softplus(a.astype(F32) + dt_bias.astype(F32))
    o = chunk_gated_delta_rule(q, k, v, g, beta)
    o = rmsnorm_2(o, onorm_g) * jax.nn.silu(heads(z).astype(F32))
    return o.reshape(B, T, DN_WIDTH).astype(dt)

def forgetting_attention(q, k, v, f, qnorm_g, knorm_g, f_bias):
    B, T, _ = q.shape
    dt = q.dtype
    heads = lambda t: t.reshape(B, T, FX_HEADS, HEAD_DIM).transpose(0, 2, 1, 3)
    q = rmsnorm_2(heads(q), qnorm_g)
    k = rmsnorm_2(heads(k), knorm_g)
    v = heads(v)
    logf = jax.nn.log_sigmoid(f.astype(F32) + f_bias.astype(F32))
    c = jnp.cumsum(logf, axis=1).transpose(0, 2, 1)
    scale = HEAD_DIM ** -0.5
    outs = []
    for i in range(T // FX_BLOCK):
        lo, hi = i * FX_BLOCK, (i + 1) * FX_BLOCK
        s = jnp.einsum('bhqd,bhkd->bhqk', q[:, :, lo:hi], k[:, :, :hi]).astype(F32) * scale
        s = s + c[:, :, lo:hi, None] - c[:, :, None, :hi]
        q_pos = jnp.arange(lo, hi)[:, None]
        k_pos = jnp.arange(hi)[None, :]
        s = jnp.where(k_pos <= q_pos, s, -jnp.inf)
        p = jax.nn.softmax(s, axis=-1).astype(dt)
        outs.append(jnp.einsum('bhqk,bhkd->bhqd', p, v[:, :, :hi]))
    o = jnp.concatenate(outs, axis=2)
    return o.transpose(0, 2, 1, 3).reshape(B, T, FX_WIDTH)

def pool_mixer(xp, pool_w, pool_scale):
    B, T, _ = xp.shape
    xg = xp.reshape(B, T, POOL_GROUPS, POOL_GROUP_DIM).astype(F32)
    cs = jnp.concatenate([jnp.zeros((B, 1, POOL_GROUPS, POOL_GROUP_DIM), F32),
                          jnp.cumsum(xg, axis=1)], axis=1)
    win = jnp.array(POOL_WINDOWS, jnp.int32)
    t1 = jnp.arange(1, T + 1, dtype=jnp.int32)[:, None]
    start = jnp.maximum(t1 - win[None, :], 0)
    count = (t1 - start).astype(F32)
    gidx = jnp.arange(POOL_GROUPS)[None, :]
    window_sum = cs[:, 1:] - cs[:, start, gidx]
    y = (window_sum / count[..., None] - xg).astype(xp.dtype)
    y = jnp.einsum('btgc,gcd->btgd', y, pool_w)
    return y.reshape(B, T, POOL_WIDTH) * pool_scale

def hybrid_mixer(h, w_in, dn_conv, dn_a_log, dn_dt_bias, dn_onorm, fx_qnorm, fx_knorm, fx_f_bias,
                 pool_w, pool_scale, w_out):
    proj = h @ w_in
    sizes = (DN_WIDTH, DN_WIDTH, DN_WIDTH, DN_WIDTH, DN_HEADS, DN_HEADS,
             FX_WIDTH, FX_WIDTH, FX_WIDTH, FX_HEADS, POOL_WIDTH)
    (dn_q, dn_k, dn_v, dn_z, dn_a, dn_b, fx_q, fx_k, fx_v, fx_f, pl_x) = jnp.split(
        proj, np.cumsum(sizes)[:-1].tolist(), axis=-1)
    o_dn = gated_deltanet(dn_q, dn_k, dn_v, dn_z, dn_a, dn_b, dn_conv, dn_a_log, dn_dt_bias, dn_onorm)
    o_fx = forgetting_attention(fx_q, fx_k, fx_v, fx_f, fx_qnorm, fx_knorm, fx_f_bias)
    o_pl = pool_mixer(pl_x, pool_w, pool_scale)
    return jnp.concatenate([o_dn, o_fx, o_pl], axis=-1) @ w_out

def swiglu(h, w_gate, w_up, w_down):
    return (jax.nn.silu(h @ w_gate) * (h @ w_up)) @ w_down

def moe_swiglu(h, router, w_gate, w_up, w_down):
    B, T, D = h.shape
    ht = h.reshape(B * T, D)
    probs = jax.nn.softmax((ht @ router).astype(F32), axis=-1)
    top_p, top_i = lax.top_k(probs, TOP_K)
    top_p = top_p / jnp.sum(top_p, axis=-1, keepdims=True)
    gates = jnp.sum(jax.nn.one_hot(top_i, N_EXPERTS, dtype=F32) * top_p[..., None], axis=1).astype(h.dtype)
    out = jnp.zeros_like(ht)
    for e in range(N_EXPERTS):
        out = out + gates[:, e:e + 1] * swiglu(ht, w_gate[e], w_up[e], w_down[e])
    return out.reshape(B, T, D)

def second_inputs(seed: int = 0) -> dict:
    key = jax.random.key(seed)
    ks = list(jax.random.split(key, 32))
    counter = [0]

    def nk():
        counter[0] += 1
        return ks[counter[0] - 1]

    def nrm(shape, scale):
        return scale * jax.random.normal(nk(), shape, F32)

    def gain(shape):
        return 1.0 + nrm(shape, 0.05)

    L = DEPTH
    x = nrm((BATCH, SEQ, D_MODEL), 1.0)
    norm1 = gain((L, D_MODEL))
    w_in = nrm((L, D_MODEL, N_IN), D_MODEL ** -0.5)
    dn_conv = nrm((L, CONV_WIDTH, 3 * DN_WIDTH), CONV_WIDTH ** -0.5)
    dn_a_log = jnp.log(jax.random.uniform(nk(), (L, DN_HEADS), F32, 1.0, 16.0))
    dt0 = jnp.exp(jax.random.uniform(nk(), (L, DN_HEADS), F32, math.log(1e-3), math.log(1e-1)))
    dn_dt_bias = dt0 + jnp.log(-jnp.expm1(-dt0))
    dn_onorm = gain((L, HEAD_DIM))
    fx_qnorm = gain((L, HEAD_DIM))
    fx_knorm = gain((L, HEAD_DIM))
    fx_f_bias = 2.0 + nrm((L, FX_HEADS), 0.5)
    pool_w = nrm((L, POOL_GROUPS, POOL_GROUP_DIM, POOL_GROUP_DIM), POOL_GROUP_DIM ** -0.5)
    pool_scale = 1.0 + nrm((L, POOL_WIDTH), 0.1)
    w_out = nrm((L, D_MIX, D_MODEL), 0.5 * D_MIX ** -0.5)
    norm2 = gain((L, D_MODEL))
    ffn_gate = nrm((N_DENSE, D_MODEL, D_FF), D_MODEL ** -0.5)
    ffn_up = nrm((N_DENSE, D_MODEL, D_FF), D_MODEL ** -0.5)
    ffn_down = nrm((N_DENSE, D_FF, D_MODEL), 0.5 * D_FF ** -0.5)
    router = nrm((N_MOE, D_MODEL, N_EXPERTS), D_MODEL ** -0.5)
    moe_gate = nrm((N_MOE, N_EXPERTS, D_MODEL, D_FF_EXPERT), D_MODEL ** -0.5)
    moe_up = nrm((N_MOE, N_EXPERTS, D_MODEL, D_FF_EXPERT), D_MODEL ** -0.5)
    moe_down = nrm((N_MOE, N_EXPERTS, D_FF_EXPERT, D_MODEL), 0.5 * D_FF_EXPERT ** -0.5)
    return {'x': x, 'norm1': norm1, 'w_in': w_in, 'dn_conv': dn_conv, 'dn_a_log': dn_a_log,
            'dn_dt_bias': dn_dt_bias, 'dn_onorm': dn_onorm, 'fx_qnorm': fx_qnorm, 'fx_knorm': fx_knorm,
            'fx_f_bias': fx_f_bias, 'pool_w': pool_w, 'pool_scale': pool_scale, 'w_out': w_out,
            'norm2': norm2, 'ffn_gate': ffn_gate, 'ffn_up': ffn_up, 'ffn_down': ffn_down,
            'router': router, 'moe_gate': moe_gate, 'moe_up': moe_up, 'moe_down': moe_down}

def second_block(x, norm1, w_in, dn_conv, dn_a_log, dn_dt_bias, dn_onorm, fx_qnorm, fx_knorm, fx_f_bias,
              pool_w, pool_scale, w_out, norm2, ffn_gate, ffn_up, ffn_down, router, moe_gate, moe_up,
              moe_down):
    for layer in range(DEPTH):
        h = rmsnorm_2(x, norm1[layer])
        x = x + hybrid_mixer(h, w_in[layer], dn_conv[layer], dn_a_log[layer], dn_dt_bias[layer],
                             dn_onorm[layer], fx_qnorm[layer], fx_knorm[layer], fx_f_bias[layer],
                             pool_w[layer], pool_scale[layer], w_out[layer])
        h = rmsnorm_2(x, norm2[layer])
        j = layer // 2
        if layer % 2 == 0:
            x = x + swiglu(h, ffn_gate[j], ffn_up[j], ffn_down[j])
        else:
            x = x + moe_swiglu(h, router[j], moe_gate[j], moe_up[j], moe_down[j])
    return x


def setup_inputs(seed=0):
    out = dict(first_inputs(seed))
    for name, value in second_inputs(seed + 1).items():
        if name != "x":
            out[name + "_2"] = value
    return out


def reference(
    x, norm_mix, norm_ffn, ev_w_in, ev_w_a2, ev_b_a, ev_gla_gain, ev_dq_gain, ev_dk_gain,
    ev_lq1, ev_lk1, ev_lq2, ev_lk2, ev_diff_gain, ev_w_out, od_w_in, od_q_gain, od_k_gain,
    od_w_out, ffn_w_up, ffn_conv_w, ffn_conv_b, ffn_w_down, norm1_2, w_in_2, dn_conv_2,
    dn_a_log_2, dn_dt_bias_2, dn_onorm_2, fx_qnorm_2, fx_knorm_2, fx_f_bias_2, pool_w_2,
    pool_scale_2, w_out_2, norm2_2, ffn_gate_2, ffn_up_2, ffn_down_2, router_2, moe_gate_2,
    moe_up_2, moe_down_2,
):
    x = first_block(
        x, norm_mix, norm_ffn, ev_w_in, ev_w_a2, ev_b_a, ev_gla_gain, ev_dq_gain, ev_dk_gain,
        ev_lq1, ev_lk1, ev_lq2, ev_lk2, ev_diff_gain, ev_w_out, od_w_in, od_q_gain, od_k_gain,
        od_w_out, ffn_w_up, ffn_conv_w, ffn_conv_b, ffn_w_down,
    )
    return second_block(
        x, norm1_2, w_in_2, dn_conv_2, dn_a_log_2, dn_dt_bias_2, dn_onorm_2, fx_qnorm_2,
        fx_knorm_2, fx_f_bias_2, pool_w_2, pool_scale_2, w_out_2, norm2_2, ffn_gate_2, ffn_up_2,
        ffn_down_2, router_2, moe_gate_2, moe_up_2, moe_down_2,
    )


_drawn_inputs = setup_inputs


def setup_inputs(seed=0):
    import zlib

    import numpy as np

    out = dict(_drawn_inputs(seed))
    spreads = {}
    factors = {'ev_gla_gain': 4.326,
     'ev_dq_gain': 3.449,
     'ev_dk_gain': 3.798,
     'ev_lq1': 3.946,
     'ev_lk1': 8.0,
     'ev_diff_gain': 3.469,
     'od_q_gain': 8.0,
     'od_k_gain': 8.0,
     'ffn_conv_b': 4.644,
     'dn_onorm_2': 4.983,
     'fx_qnorm_2': 7.998,
     'fx_knorm_2': 8.0,
     'ev_lk2': 3.254,
     'pool_scale_2': 4.501,
     'norm2_2': 3.708}
    for name, (base, spread) in spreads.items():
        noise = np.random.default_rng([zlib.crc32(name.encode()), seed]).standard_normal(out[name].shape)
        drawn = base * np.exp(spread * noise) if base else spread * noise
        out[name] = __import__('jax').numpy.asarray(drawn.astype(out[name].dtype))
    for name, factor in factors.items():
        out[name] = (out[name] * factor).astype(out[name].dtype)
    return out
```

```python
import numpy as np

P = 128
S = 256
NT = S // P
D = 1024
KC = D // P
TW = 256
RING = 6
EPS = 1e-6
NEG = -1e30
D_FF, D_FFE, N_EXP = 2816, 1536, 8
G_FFN = D_FF // TW
G_EXP = D_FFE // TW
PASSES = 2
CH = 64
NCH = S // CH
DN_H, FX_H = 6, 6
LAMBDA_INIT = 0.8 - 0.6
POOL_WINDOWS = (2, 4, 8, 16)

M2_SUMS = {1: 7, 3: 0, 4: 1, 5: 2, 6: 4, 8: 5, 9: 6}
M2_SUM_ORDER = [7, 0, 1, 2, 4, 5, 6]
M2_SUM_HALVES = {7: (0,), 0: (0, 1), 1: (0, 1), 2: (0, 1), 4: (1,), 5: (0, 1), 6: (0, 1)}

EV_IN, EV_OUT = 13, 4
OD_IN, OD_OUT = 18, 2
M2_IN, M2_OUT = 12, 4
SIZES = [("ev_in", EV_IN), ("ev_out", EV_OUT), ("ffn0", 3 * G_FFN), ("od_in", OD_IN), ("od_out", OD_OUT),
         ("ffn1", 3 * G_FFN), ("m0_in", M2_IN), ("m0_out", M2_OUT), ("ffn2", 3 * G_FFN), ("m1_in", M2_IN),
         ("m1_out", M2_OUT), ("moe", 3 * G_EXP * N_EXP)]
BASE = {}
N_TILES = 0
for _n, _k in SIZES:
    BASE[_n] = N_TILES
    N_TILES += _k

PRM_W = [("norm", 8 * KC), ("ba", 2), ("wa2", 256), ("gla_gain", 128), ("dq", 1), ("dk", 1), ("lq", 128), ("lk", 128),
         ("diff_gain", 128), ("odq", 1), ("odk", 1), ("conv0", 44 * 4), ("conv1", 44 * 4), ("router", KC * N_EXP)]
for _l in (0, 1):
    PRM_W += [(f"dnconv{_l}", 9 * 4), (f"alog{_l}", 1), (f"dtb{_l}", 1), (f"fb{_l}", 1), (f"onorm{_l}", 64),
              (f"fxq{_l}", 1), (f"fxk{_l}", 1), (f"poolw{_l}", 128), (f"pscale{_l}", 2)]
PRM = {}
N_PRM = 0
for _n, _k in PRM_W:
    PRM[_n] = (N_PRM, _k)
    N_PRM += _k

CST_W = [("ident", 128), ("blk64", 128), ("ones", 256), ("eps", 1), ("one", 1), ("cmask", 384), ("dmask", 3 * 384),
         ("glamask", 128), ("gdneg", 128), ("offd", 6 * 128), ("reset", 512), ("pool", 2 * 4 * 256), ("before", 64),
         ("earlier", 128), ("iota", 128)]
CST = {}
N_CST = 0
for _n, _k in CST_W:
    CST[_n] = (N_CST, _k)
    N_CST += _k
SEL_W = [("sel6", 6 * 256), ("selhp", 3 * 128)]
SEL = {}
N_SEL = 0
for _n, _k in SEL_W:
    SEL[_n] = (N_SEL, _k)
    N_SEL += _k


def constants():
    c = np.zeros((P, N_CST), np.float32)

    def put(name, a):
        o, w = CST[name]
        c[:, o:o + w] = np.asarray(a, np.float32).reshape(P, w)

    p = np.arange(P)[:, None]
    f = np.arange(P)[None, :]
    put("ident", p == f)
    put("blk64", p // 64 == f // 64)
    put("ones", np.ones((P, 256)))
    put("eps", np.full((P, 1), EPS))
    put("one", np.ones((P, 1)))
    causal = np.where(f <= p, 0.0, NEG)
    zero = np.zeros((P, P))
    put("cmask", np.concatenate([causal, zero, causal], 1))
    near = (p - f)
    dm = []
    for dil in (1, 4, 16):
        diag = np.where((near >= 0) & (near % dil == 0), 0.0, NEG)
        far = np.where(((near + P) % dil == 0) & (near + P <= 128 * dil), 0.0, NEG)
        dm.append(np.concatenate([diag, far, diag], 1))
    put("dmask", np.stack(dm, 1))
    same = p // CH == f // CH
    put("glamask", same & (f >= p))
    put("gdneg", np.where(same & (f >= p), 0.0, NEG))
    off = []
    for b in (1, 2, 4, 8, 16, 32):
        off.append((f // (2 * b) == p // (2 * b)) & (f % (2 * b) >= b) & (p % (2 * b) < b))
    put("offd", np.stack(off, 1))
    put("reset", np.broadcast_to(np.arange(512) % CH != 0, (P, 512)))
    pool = np.zeros((P, 2, 4, 256))
    for g, w in enumerate(POOL_WINDOWS):
        for tt in range(2):
            src = tt * P + np.arange(P)[:, None]
            dst = np.arange(256)[None, :]
            pool[:, tt, g] = ((dst - src >= 0) & (dst - src < w)) / np.minimum(dst + 1, w) - (src == dst)
    put("pool", pool)
    put("before", np.broadcast_to((np.arange(8)[None, :] < np.arange(8)[:, None]).reshape(1, 64), (P, 64)))
    put("earlier", p < f)
    put("iota", np.broadcast_to(f, (P, P)))
    s = np.zeros((8, N_SEL), np.float32)
    o = SEL["sel6"][0]
    for h in range(6):
        s[h, o + h * 256:o + (h + 1) * 256] = 1
    o = SEL["selhp"][0]
    for h in range(6):
        s[h, o + (h // 2) * 128 + (h % 2) * 64:o + (h // 2) * 128 + (h % 2) * 64 + 64] = 1
    return c, s


def build(nc, w_dram, x_dram, prm_dram, cst_dram, sel_dram, out_dram, stop=None):
    import concourse.bass as bass
    from concourse import mybir
    F32 = mybir.dt.float32
    ALU = mybir.AluOpType
    ACT = mybir.ActivationFunctionType
    AX = mybir.AxisListType
    ADD, SUB, MUL, MAX, MIN = ALU.add, ALU.subtract, ALU.mult, ALU.max, ALU.min

    X = nc.alloc_sbuf_tensor("X", [P, NT, D], F32)
    HN = nc.alloc_sbuf_tensor("HN", [P, NT, D], F32)
    HT = nc.alloc_sbuf_tensor("HT", [P, KC, S], F32)
    OT = nc.alloc_sbuf_tensor("OT", [P, KC, S], F32)
    W = nc.alloc_sbuf_tensor("W", [P, RING, KC * TW], F32)
    PR = nc.alloc_sbuf_tensor("PR", [P, N_PRM], F32)
    CS = nc.alloc_sbuf_tensor("CS", [P, N_CST], F32)
    SL = nc.alloc_sbuf_tensor("SL", [8, N_SEL], F32)
    ST_ = nc.alloc_sbuf_tensor("STAT", [P, 640], F32)
    ARENA_N = 21632
    AR = nc.alloc_sbuf_tensor("ARENA", [P, ARENA_N], F32)
    PS = [nc.alloc_psum_tensor(f"PS{b}", [P, 512], F32) for b in range(8)]

    def prm(name):
        o, w = PRM[name]
        return PR[:, o:o + w]

    def cst(name):
        o, w = CST[name]
        return CS[:, o:o + w]

    def sel(name):
        o, w = SEL[name]
        return SL[:, o:o + w]

    class Carve:
        def __init__(self):
            self.at = 0

        def __call__(self, n):
            self.at += n
            assert self.at <= ARENA_N, self.at
            return AR[:, self.at - n:self.at]

    class Stats:
        at = 0

        @classmethod
        def get(cls, n):
            cls.at += n
            assert cls.at <= 640, cls.at
            return ST_[:, cls.at - n:cls.at]

    Stats.at = 0
    ident, ones, blk64 = cst("ident"), cst("ones")[:, 0:P], cst("blk64")
    eps, one = cst("eps"), cst("one")

    sems = {}

    def sem(name):
        if name not in sems:
            sems[name] = nc.alloc_semaphore(name)
        return sems[name]

    w_full = [sem(f"w_full{i}") for i in range(RING)]
    w_used = sem("w_used")
    full = [sem(f"bank_full{b}") for b in range(8)]
    free = [sem(f"bank_free{b}") for b in range(8)]
    s_in, s_const, s_out = sem("x_in"), sem("const_in"), sem("out_done")

    uses = {}
    n_use = [0] * 8
    n_full = [0] * 8

    def plan(key, bank, tile=None):
        if tile is None:
            n_full[bank] += 1
            uses[key] = (bank, n_use[bank], full[bank], n_full[bank])
        else:
            uses[key] = (bank, n_use[bank], w_used, tile + 1)
        n_use[bank] += 1

    class Rot:
        def __init__(self, banks):
            self.banks, self.k = banks, 0

        def __call__(self, key, tile=None):
            plan(key, self.banks[self.k % len(self.banks)], tile)
            self.k += 1

    def bank(key):
        return PS[uses[key][0]]

    def await_full(eng, key):
        eng.wait_ge(uses[key][2], uses[key][3])

    def release(ins, key):
        ins.then_inc(free[uses[key][0]], 1)

    def await_free_of(eng, key):
        eng.wait_ge(free[uses[key][0]], uses[key][1] + 1)

    def claim(pe, key):
        b, k = uses[key][:2]
        if k:
            pe.wait_ge(free[b], k)

    def plan_norm(n):
        for b in range(4):
            plan(("norm", n, b), 4 + b)

    def plan_y(n, tile):
        for b in range(4):
            plan(("y", n, b), b, tile)

    def plan_attn(name, units, groups, combine, rot):
        heads = units // combine
        for i in range(heads + 2):
            if i < heads:
                for c in range(combine):
                    for g in range(groups):
                        rot((name, "s", i * combine + c, g))
            if 1 <= i <= heads:
                for g in range(groups):
                    rot((name, "t", i - 1, g))

    def plan_out_t(name, chunks, rot):
        for j in range((chunks + 1) // 2):
            rot((name, "oT", j))

    def plan_even():
        t0 = BASE["ev_in"]
        rot = Rot([0, 1, 2, 3, 4, 5, 6, 7])
        rot(("ev", "ar"), t0)
        rot(("ev", "aq"), t0 + 1)
        rot(("ev", "ak"), t0 + 2)
        rot(("ev", "la"))
        for j in range(2):
            rot(("ev", "av", j), t0 + 3 + j)
        for j in range(2):
            rot(("ev", "ag", j), t0 + 5 + j)
        for j in range(4):
            rot(("ev", "bqk", j), t0 + 7 + j)
            if j:
                rot(("ev", "ss", j - 1))
        rot(("ev", "bv", 0), t0 + 11)
        rot(("ev", "ss", 3))
        rot(("ev", "bv", 1), t0 + 12)
        rot = Rot([2, 3, 4, 5, 6, 7])
        rot(("ev", "kwT"))
        for r in range(2):
            rot(("ev", "att", r))
        for n in range(NCH - 1):
            rot(("ev", "kv", n))
        for t in range(NT):
            plan(("ev", "o", t), t)
        for n in range(NT):
            plan(("evd", "o", n), n)
        plan_attn("evd", 8, 1, 2, rot)
        plan_out_t("ev", 8, Rot([4, 5, 6, 7]))
        plan_y("ev", BASE["ev_out"] + EV_OUT - 1)

    def plan_odd():
        t0 = BASE["od_in"]
        rot = Rot([0, 1, 2, 3, 4, 5, 6, 7])
        for g in range(3):
            for j in range(4):
                rot(("od", "qk", g, j), t0 + 6 * g + j)
                if j:
                    rot(("od", "ss", g, j - 1))
            rot(("od", "v", g, 0), t0 + 6 * g + 4)
            rot(("od", "ss", g, 3))
            rot(("od", "v", g, 1), t0 + 6 * g + 5)
        for n in range(NT):
            plan(("od", "o", n), n)
        plan_attn("od", 4, 3, 1, Rot([2, 3, 4, 5, 6, 7]))
        plan_out_t("od", 4, Rot([4, 5, 6, 7]))
        plan_y("od", BASE["od_out"] + OD_OUT - 1)

    GD_STEPS = 5
    PAIRS = [(t, h) for r in range(2) for t in range(NT) for h in range(r, 6, 2)]

    def plan_m2(m):
        t0 = BASE[f"{m}_in"]
        rot = Rot([0, 1, 2, 3, 4, 5, 6, 7])
        rot((m, "ab"))
        rot((m, "in", 7), t0)
        for j in range(M2_IN - 1):
            jj = j if j < 7 else j + 1
            rot((m, "in", jj), t0 + 1 + j)
            if jj in M2_SUMS:
                rot((m, "ss", M2_SUMS[jj]))
        rot((m, "py"))
        rot((m, "pz"))
        rot((m, "rowT"))
        for j in range(2):
            rot((m, "gb", j))
        for j in range(2):
            rot((m, "bb", j))
        for t in range(NT):
            rot((m, "kT", t))
        for t in range(NT):
            rot((m, "vT", t))
        for q in range(3):
            rot((m, "dec", q))
        for q in range(3):
            rot((m, "kk", q))
        for q in range(3):
            rot((m, "qk", q))
        for q in range(3):
            rot((m, "M", 0, q))
        for s in range(1, GD_STEPS + 1):
            for q in range(3):
                rot((m, "M", s, q))
            for q in range(3):
                if s < GD_STEPS:
                    rot((m, "X", s, q))
                rot((m, "Y", s, q))
        rot = Rot([2, 3, 4, 5, 6, 7])
        for t in range(NT):
            rot((m, "u", t))
            rot((m, "w", t))
        for t in range(NT):
            plan((m, "o", t), t)
        for n in range(NCH):
            if n:
                rot((m, "vp", n))
            if n < NCH - 1:
                rot((m, "kv", n))
        for n in range(NT):
            plan((m + "f", "o", n), n)
        plan_attn(m + "f", 6, 1, 1, rot)
        plan_out_t(m, 6, Rot([4, 5, 6, 7]))
        plan_y(m, BASE[f"{m}_out"] + M2_OUT - 1)

    ffn_k0 = {}

    def plan_ffn(n, groups):
        ffn_k0[n] = list(n_use)
        for g in range(groups):
            n_use[4 + 2 * (g % 2)] += 1
            n_use[5 + 2 * (g % 2)] += 1
        plan_y(n, BASE[n] + 3 * groups - 1)

    MOE_GROUPS = G_EXP * N_EXP
    MOE_TILES = 3 * MOE_GROUPS
    moe_name = ["moe", "moe_more"]

    def plan_moe(p):
        rot = Rot([4, 5, 6, 7])
        for j in range(4):
            rot(("moe", p, "selT", j))
        for j in range(16):
            rot(("moe", p, "gx", j))
        for b in range(4):
            plan(("y", moe_name[p], b), b)
        ffn_k0[moe_name[p]] = list(n_use)
        for b in (6, 7):
            n_use[b] += MOE_GROUPS // 2
        for b in (4, 5):
            n_use[b] += N_EXP

    order = [("norm", 0), ("even",), ("norm", 1), ("ffn", "ffn0", G_FFN, "conv"),
             ("norm", 2), ("odd",), ("norm", 3), ("ffn", "ffn1", G_FFN, "conv"),
             ("norm", 4), ("m2", "m0", 0), ("norm", 5), ("ffn", "ffn2", G_FFN, "glu"),
             ("norm", 6), ("m2", "m1", 1), ("norm", 7), ("router",), ("moe",)]
    if stop is not None:
        order = order[:stop]
    for st in order:
        if st[0] == "norm":
            plan_norm(st[1])
        elif st[0] == "even":
            plan_even()
        elif st[0] == "odd":
            plan_odd()
        elif st[0] == "m2":
            plan_m2(st[1])
        elif st[0] == "router":
            plan(("router", "logits"), 4)
            plan(("router", "place"), 5)
        elif st[0] == "moe":
            for p in range(PASSES):
                plan_moe(p)
        else:
            plan_ffn(st[1], st[2])
    n_tiles = N_TILES
    last_stage = order[-1]
    if stop is not None and last_stage[0] != "moe":
        n_tiles = {"even": BASE["ffn0"], "odd": BASE["ffn1"]}.get(last_stage[0])
        if n_tiles is None:
            names = [n for n, _ in SIZES]
            if last_stage[0] == "m2":
                n_tiles = BASE[last_stage[1] + "_out"] + M2_OUT
            elif last_stage[0] == "ffn":
                k = names.index(last_stage[1])
                n_tiles = BASE[names[k]] + SIZES[k][1]

    def v3(ap, a):
        return ap.rearrange("p (a b) -> p a b", a=a)

    class NS:
        pass

    ev = NS()
    a = Carve()
    ev.arT = a(256)
    ev.T1, ev.MN, ev.B, ev.EB, ev.ENB, ev.EW, ev.QD, ev.KD, ev.KW = [a(512) for _ in range(9)]
    ev.KWT = v3(a(512), 2)
    ev.V = v3(a(1024), 2)
    ev.GG = v3(a(1024), 2)
    ev.ATT = v3(a(1024), 8)
    ev.ST = a(3 * 512).rearrange("p (n c r v) -> p n c r v", n=3, c=2, r=2)
    ev.SQ = v3(a(1024), 2)
    ev.RS = v3(a(1024), 2)
    ev.QK = a(2048).rearrange("p (j c t) -> p j c t", j=4, c=2)
    ev.BV = v3(a(1024), 2)
    ev.SM = a(2 * 384).rearrange("p (u g k) -> p u g k", u=2, g=1)
    ev.EX = a(4 * 384).rearrange("p (u g k) -> p u g k", u=4, g=1)
    ev.WC = a(2 * 384).rearrange("p (u g k) -> p u g k", u=2, g=1)
    ev.PT = a(2 * 384).rearrange("p (u g k) -> p u g k", u=2, g=1)
    od = NS()
    a = Carve()
    od.QK = a(24 * 256).rearrange("p (g j c t) -> p g j c t", g=3, j=4, c=2)
    od.V = a(3 * 1024).rearrange("p (g t n) -> p g t n", g=3, t=2)
    od.SQ = v3(a(1024), 2)
    od.RS = v3(a(1024), 2)
    od.SM = a(2 * 1152).rearrange("p (u g k) -> p u g k", u=2, g=3)
    od.EX = a(2 * 1152).rearrange("p (u g k) -> p u g k", u=2, g=3)
    od.PT = a(2 * 1152).rearrange("p (u g k) -> p u g k", u=2, g=3)
    m2 = NS()
    a = Carve()
    Yf = a(9 * 256)
    m2.Y = v3(Yf, 9)
    m2.QKN = v3(a(6 * 256), 6)
    m2.QD = v3(a(768), 3)
    m2.KB = v3(a(768), 3)
    m2.EGB = v3(a(768), 3)
    KBGf = a(768)
    m2.KBG = v3(KBGf, 2)
    m2.KDEC = v3(a(768), 2)
    m2.VB = v3(a(768), 2)
    m2.FQK = OT[:, 0:6, :]
    m2.FV = v3(a(768), 2)
    m2.ZG = v3(a(768), 2)
    m2.DEC = v3(a(1536), 12)
    m2.OF = m2.DEC
    m2.AT = v3(a(1536), 12)
    m2.ATQ = v3(a(1536), 12)
    DIf, M1f = a(1536), a(1536)
    m2.DI, m2.M1 = v3(DIf, 12), v3(M1f, 12)
    m2.UI = v3(a(1536), 12)
    SQf = a(1024)
    m2.SQ = v3(SQf, 2)
    RSf = a(1024)
    m2.RS = v3(RSf, 2)
    m2.S = RSf[:, 0:768].rearrange("p (b c v) -> p b c v", b=2, c=3)
    m2.SN = v3(a(384), 3)
    m2.XP = v3(KBGf[:, 0:512], 2)
    m2.ROW = HN[0:8, 0, :].rearrange("p (r t) -> p r t", t=256)
    m2.ROW2 = HN[0:8, 1, :].rearrange("p (r t) -> p r t", t=256)
    m2.WT = Yf[:, 0:768].rearrange("p (c t) -> p c t", c=3)
    m2.UU = Yf[:, 768:1536].rearrange("p (t n) -> p t n", t=2)
    m2.PX = M1f[:, 0:512].rearrange("p (c t) -> p c t", c=2)
    m2.SM = M1f[:, 0:768].rearrange("p (u g k) -> p u g k", u=2, g=1)
    m2.EX = M1f[:, 768:1536].rearrange("p (u g k) -> p u g k", u=2, g=1)
    m2.PT = DIf[:, 0:768].rearrange("p (u g k) -> p u g k", u=2, g=1)
    ff = NS()
    a = Carve()
    ff.GH = a(2 * 512).rearrange("p (b c t) -> p b c t", b=2, c=2)
    ff.SG = a(2 * 512).rearrange("p (b c t) -> p b c t", b=2, c=2)
    ff.YG = a(2 * 512).rearrange("p (b c t) -> p b c t", b=2, c=2)
    ff.YV = a(2 * 512).rearrange("p (b c t) -> p b c t", b=2, c=2)
    mo = NS()
    a = Carve()
    mo.GH = a(2 * 256).rearrange("p (b n) -> p b n", b=2)
    mo.SG = a(2 * 256).rearrange("p (b n) -> p b n", b=2)
    mo.YE = a(D)
    mo.XG = a(KC * N_EXP * P).rearrange("p (k e s) -> p k e s", k=KC, e=N_EXP)
    mo.SEL = a(NT * N_EXP * P).rearrange("p (t e s) -> p t e s", t=NT, e=N_EXP)
    mo.GSEL = a(NT * N_EXP * P).rearrange("p (t e s) -> p t e s", t=NT, e=N_EXP)
    mo.SELT = a(N_EXP * S).rearrange("p (e t) -> p e t", e=N_EXP)
    mo.GS = a(S)
    mo.LG, mo.EX, mo.PB, mo.MASK, mo.GATE, mo.POS = [a(16) for _ in range(6)]
    mo.GTR, mo.EQ = a(128), a(128)
    mo.MOST = a(1)

    MORE = nc.alloc_sbuf_tensor("MORE", [1, 1], mybir.dt.int32)

    st_ss, st_rs = Stats.get(2), Stats.get(2)
    st_gain = Stats.get(4)
    st_lam, st_nlam = Stats.get(2), Stats.get(1)
    st_lamp, st_dg = Stats.get(128), Stats.get(128)
    st_nea = Stats.get(2)
    st_o, st_or = Stats.get(16), Stats.get(16)
    st_mx, st_sum, st_ri = Stats.get(24), Stats.get(24), Stats.get(24)
    st_rl = Stats.get(2)
    st_tm = Stats.get(36).rearrange("p (t j h) -> p t j h", t=2, j=3)
    st_beg = Stats.get(12).rearrange("p (t h) -> p t h", t=2)

    def bc(ap, axis, n):
        ap = ap.unsqueeze(axis)
        shape = list(ap.shape)
        shape[axis] = n
        return ap.broadcast_to(shape)

    def bank4(key, n=4):
        return bank(key)[:, 0:n * P].rearrange("p (a b) -> p a b", a=n)

    y_names = {"even": "ev", "odd": "od"}
    resid_of = {}
    prev = None
    for st in order:
        if st[0] == "norm":
            resid_of[st[1]] = prev
        elif st[0] != "router":
            prev = y_names.get(st[0], st[1] if len(st) > 1 else st[0])
    last_resid = prev

    def tile_ap(t):
        return W[:, t % RING, :]

    def in_tile(t):
        return tile_ap(t).rearrange("p (k n) -> p k n", k=KC)

    def out_tile(t):
        return tile_ap(t).rearrange("p (c n) -> p c n", c=2)

    def more_tokens(eng):
        eng.wait_ge(sem("more"), 1)
        return eng.value_load(MORE[0:1, 0:1], min_val=0, max_val=1)

    def moe_loop(eng, group, expert_out, w0):
        group(0, 0, True)
        group(1, 0)
        with eng.Fori(0, N_EXP - 1) as i:
            for gs in range(2, 2 + G_EXP):
                group(gs, i)
                if gs == G_EXP:
                    expert_out(0, i, w0 + 3 * (G_EXP - 1) + 4)
        for gs in range(2 + (N_EXP - 1) * G_EXP, MOE_GROUPS):
            group(gs, 0)
        expert_out(N_EXP - 1, 0, w0 + MOE_TILES - 1)

    block = nc.Block()
    block.__enter__()

    @block.sync
    def _(sp):
        sp.dma_start(X[:, :, :], x_dram.rearrange("b (t p) d -> p (b t) d", p=P)).then_inc(s_in, 16)

        def load(t, slot):
            src = w_dram[t] if isinstance(t, int) else w_dram[bass.ds(t, 1), :, :].rearrange("a p n -> (a p) n")
            sp.dma_start(W[:, slot, :], src).then_inc(w_full[slot], 16)

        for t in range(RING):
            load(t, t)
        rounds = (n_tiles - RING) // RING
        with sp.Fori(0, rounds) as i:
            for u in range(RING):
                sp.wait_ge(w_used, RING * i + (u + 1))
                load(RING * i + (RING + u), u)
        for t in range(RING * (rounds + 1), n_tiles):
            sp.wait_ge(w_used, t - RING + 1)
            load(t, t % RING)
        for b in range(4):
            await_free_of(sp, ("y", last_resid, b))
        if last_resid == "moe":
            with sp.If(more_tokens(sp) > 0):
                n_body = RING
                with sp.Fori(0, MOE_TILES // n_body) as i:
                    for u in range(n_body):
                        sp.wait_ge(w_used, n_body * i + (n_tiles + u - RING + 1))
                        load(n_body * i + (n_tiles - MOE_TILES + u), (n_tiles + u) % RING)
                for b in range(4):
                    await_free_of(sp, ("y", moe_name[1], b))
        sp.dma_start(out_dram.rearrange("b (t p) d -> p (b t) d", p=P), X[:, :, :]).then_inc(s_out, 16)
        sp.wait_ge(s_out, 16)

    @block.gpsimd
    def _(pool):
        pool.dma_start(CS[:, :], cst_dram).then_inc(s_const, 16)
        pool.dma_start(PR[:, :], prm_dram).then_inc(s_const, 16)
        pool.dma_start(SL[:, :], sel_dram).then_inc(s_const, 16)
        pool.wait_ge(s_const, 48)
        offd = v3(cst("offd"), 6)
        for st in order:
            if st[0] != "m2":
                continue
            m = st[1]
            for q in range(3):
                await_free_of(pool, (m, "kk", q))
                await_free_of(pool, (m, "qk", q))
            for s in range(GD_STEPS + 1):
                if s:
                    for q in range(3):
                        await_full(pool, (m, "M", s - 1, q))
                if s == 1:
                    pool.wait_ge(sem(m + "_ui"), 1)
                pool.tensor_tensor(m2.OF, m2.AT, bc(offd[:, s, :], 1, 12), MUL).then_inc(sem(m + "_of"), 1)

    @block.tensor
    def _(pe):
        mm = pe.matmul

        fences = [0]

        def fence(ins):
            fences[0] += 1
            ins.then_inc(sem("pe_fence"), 1)
            pe.wait_ge(sem("pe_fence"), fences[0])

        def await_tile(t):
            pe.wait_ge(w_full[t % RING], 16 * (t // RING + 1))

        def norm(n):
            for b in range(4):
                claim(pe, ("norm", n, b))
                pe.wait_ge(sem("hn"), n + 1)
                for k in range(2):
                    for t in range(NT):
                        c = 2 * b + k
                        ins = pe.transpose(bank(("norm", n, b))[:, k * 256 + t * P:k * 256 + (t + 1) * P],
                                           HN[:, t, c * P:(c + 1) * P], ident)
                ins.then_inc(full[4 + b], 1)

        def hT_ready(n):
            for b in range(4):
                await_free_of(pe, ("norm", n, b))

        def in_channel(t, key, units=((0, 128), (128, 128)), done=True):
            claim(pe, key)
            await_tile(t)
            for c, (o, m) in enumerate(units):
                for k in range(KC):
                    ins = mm(bank(key)[0:m, c * 256:(c + 1) * 256], in_tile(t)[:, k, o:o + m], HT[:, k, :],
                             start=(k == 0), stop=(k == KC - 1))
            if done:
                ins.then_inc(w_used, 1)

        def in_token(t, key):
            claim(pe, key)
            await_tile(t)
            for tt in range(NT):
                for k in range(KC):
                    ins = mm(bank(key)[:, tt * 256:(tt + 1) * 256], HT[:, k, tt * P:(tt + 1) * P], in_tile(t)[:, k, :],
                             start=(k == 0), stop=(k == KC - 1))
            ins.then_inc(w_used, 1)

        def done(ins, key):
            ins.then_inc(uses[key][2], 1)

        def sums(key, sq, sqname, n, mat, o=0, w=512):
            claim(pe, key)
            pe.wait_ge(sem(sqname), n)
            done(mm(bank(key)[:, o:o + w], mat, sq[:, o:o + w], start=True, stop=True), key)

        def attn(name, heads, groups, combine, scores, src, values, dv):
            for i in range(heads + 2):
                if i < heads:
                    for c in range(combine):
                        u = i * combine + c
                        for g in range(groups):
                            key = (name, "s", u, g)
                            claim(pe, key)
                            done(scores(bank(key), u, g), key)
                if 1 <= i <= heads:
                    h = i - 1
                    pe.wait_ge(sem(name + ("_w" if combine > 1 else "_e")), h + 1)
                    for g in range(groups):
                        key = (name, "t", h, g)
                        claim(pe, key)
                        for b in range(3):
                            ins = pe.transpose(bank(key)[:, b * P:(b + 1) * P], src[:, h % 2, g, b * P:(b + 1) * P], ident)
                        done(ins, key)
                if i >= 2:
                    h = i - 2
                    for g in range(groups):
                        await_free_of(pe, (name, "t", h, g))
                    if h == 0:
                        for n in range(NT):
                            claim(pe, (name, "o", n))
                    for n in range(NT):
                        o = bank((name, "o", n))[:, h * dv:(h + 1) * dv]
                        steps = [(g, kt) for g in range(groups) for kt in range(n + 1)]
                        for j, (g, kt) in enumerate(steps):
                            ins = values(o, h, g, n, kt, j == 0, j == len(steps) - 1)
                        if h == heads - 1:
                            done(ins, (name, "o", n))

        def out_transposes(name, chunks, outputs):
            for key in outputs:
                await_free_of(pe, key)
            for j in range((chunks + 1) // 2):
                key = (name, "oT", j)
                claim(pe, key)
                for k in range(2):
                    for t in range(NT):
                        c = 2 * j + k
                        ins = pe.transpose(bank(key)[:, k * 256 + t * P:k * 256 + (t + 1) * P],
                                           HN[:, t, c * P:(c + 1) * P], ident)
                done(ins, key)

        def out_proj(name, tiles, oT_banks):
            t0 = BASE[name + "_out"]
            for j in range(tiles):
                await_tile(t0 + j)
                if j == 0:
                    for i in range(oT_banks):
                        await_free_of(pe, (name, "oT", i))
                    for b in range(4):
                        claim(pe, ("y", name, b))
                for c in range(2):
                    for tt in range(NT):
                        for hf in range(2):
                            ins = mm(PS[2 * tt + hf][:, :], OT[:, 2 * j + c, tt * P:(tt + 1) * P],
                                     out_tile(t0 + j)[:, c, hf * 512:(hf + 1) * 512],
                                     start=(j == 0 and c == 0), stop=(j == tiles - 1 and c == 1))
                ins.then_inc(w_used, 1)

        def even():
            t0 = BASE["ev_in"]
            hT_ready(0)
            in_channel(t0, ("ev", "ar"), units=((0, 16),))
            in_channel(t0 + 1, ("ev", "aq"))
            in_channel(t0 + 2, ("ev", "ak"))
            claim(pe, ("ev", "la"))
            await_free_of(pe, ("ev", "ar"))
            wa2 = prm("wa2")
            for c in range(2):
                ins = mm(bank(("ev", "la"))[:, c * 256:(c + 1) * 256], wa2[0:16, c * P:(c + 1) * P], ev.arT[0:16, :],
                         start=True, stop=True)
            done(ins, ("ev", "la"))
            for j in range(2):
                in_token(t0 + 3 + j, ("ev", "av", j))
            for j in range(2):
                in_token(t0 + 5 + j, ("ev", "ag", j))
            for j in range(4):
                in_channel(t0 + 7 + j, ("ev", "bqk", j))
                if j:
                    sums(("ev", "ss", j - 1), ev.SQ[:, (j - 1) % 2, :], "ev_sq", j, blk64)
            in_token(t0 + 11, ("ev", "bv", 0))
            sums(("ev", "ss", 3), ev.SQ[:, 1, :], "ev_sq", 4, blk64)
            in_token(t0 + 12, ("ev", "bv", 1))
            key = ("ev", "kwT")
            claim(pe, key)
            await_free_of(pe, ("ev", "ak"))
            await_free_of(pe, ("ev", "aq"))
            for t in range(NT):
                for c in range(2):
                    ins = pe.transpose(bank(key)[:, (t * 2 + c) * P:(t * 2 + c + 1) * P],
                                       ev.KW[:, c * 256 + t * P:c * 256 + (t + 1) * P], ident)
            done(ins, key)
            for r in range(2):
                key = ("ev", "att", r)
                claim(pe, key)
                rp = slice(64 * r, 64 * r + 64)
                for t in range(NT):
                    for c in range(2):
                        cc = slice(c * 256 + t * P, c * 256 + (t + 1) * P)
                        ins = mm(bank(key)[:, (2 * t + c) * P:(2 * t + c + 1) * P], ev.KD[rp, cc], ev.QD[rp, cc], start=True, stop=True)
                done(ins, key)
            await_free_of(pe, ("ev", "kwT"))
            await_free_of(pe, ("ev", "av", 1))
            await_free_of(pe, ("ev", "av", 0))
            for n in range(NCH - 1):
                key = ("ev", "kv", n)
                claim(pe, key)
                rp = slice(64 * (n % 2), 64 * (n % 2) + 64)
                for c in range(2):
                    ins = mm(bank(key)[:, c * 256:(c + 1) * 256], ev.KWT[rp, n // 2, c * P:(c + 1) * P],
                             ev.V[rp, n // 2, c * 256:(c + 1) * 256], start=True, stop=True)
                done(ins, key)
            for r in range(2):
                await_free_of(pe, ("ev", "att", r))
            for t in range(NT):
                key = ("ev", "o", t)
                claim(pe, key)
                for h in range(4):
                    mm(bank(key)[:, h * P:(h + 1) * P], ev.ATT[:, 4 * (h % 2) + 2 * t + h // 2, :], ev.V[:, t, h * P:(h + 1) * P],
                       start=(h == 0), stop=False, skip_group_check=True)
                for n in (2 * t, 2 * t + 1):
                    if n == 0:
                        continue
                    await_free_of(pe, ("ev", "kv", n - 1))
                    for c in range(2):
                        ins = mm(bank(key)[64 * (n % 2):64 * (n % 2) + 64, c * 256:(c + 1) * 256],
                                 ev.QD[:, c * 256 + n * CH:c * 256 + (n + 1) * CH],
                                 ev.ST[:, n - 1, c].rearrange("p r v -> p (r v)"), start=False, stop=(n == 2 * t + 1 and c == 1),
                                 skip_group_check=True)
                done(ins, key)
            for j in range(4):
                await_free_of(pe, ("ev", "bqk", j))
            await_free_of(pe, ("ev", "bv", 0))
            await_free_of(pe, ("ev", "bv", 1))

            def scores(bk, u, g):
                h, c = u // 2, u % 2
                r = slice(64 * c, 64 * c + 64)
                q, k = ev.QK[r, h // 2, h % 2, :], ev.QK[r, 2 + h // 2, h % 2, :]
                mm(bk[:, 0:P], q[:, 0:P], k[:, 0:P], start=True, stop=True)
                return mm(bk[:, P:P + 256], q[:, P:256], k[:, 0:256], start=True, stop=True)

            def values(o, h, g, n, kt, first, last):
                b = 0 if n == 0 else 1 + kt
                return mm(o, ev.PT[:, h % 2, 0, b * P:(b + 1) * P], ev.BV[:, kt, h * P:(h + 1) * P], start=first, stop=last)

            attn("evd", 4, 1, 2, scores, ev.WC, values, 128)
            out_transposes("ev", 8, [("ev", "o", 0), ("ev", "o", 1), ("evd", "o", 0), ("evd", "o", 1)])
            out_proj("ev", EV_OUT, 4)

        def odd():
            t0 = BASE["od_in"]
            hT_ready(2)
            for g in range(3):
                for j in range(4):
                    in_channel(t0 + 6 * g + j, ("od", "qk", g, j))
                    if j:
                        sums(("od", "ss", g, j - 1), od.SQ[:, (j - 1) % 2, :], "od_sq", 4 * g + j, ones)
                in_token(t0 + 6 * g + 4, ("od", "v", g, 0))
                sums(("od", "ss", g, 3), od.SQ[:, 1, :], "od_sq", 4 * g + 4, ones)
                in_token(t0 + 6 * g + 5, ("od", "v", g, 1))
            for g in range(3):
                for j in range(4):
                    await_free_of(pe, ("od", "qk", g, j))
                for j in range(2):
                    await_free_of(pe, ("od", "v", g, j))

            def scores(bk, h, g):
                q, k = od.QK[:, g, h // 2, h % 2, :], od.QK[:, g, 2 + h // 2, h % 2, :]
                mm(bk[:, 0:P], q[:, 0:P], k[:, 0:P], start=True, stop=True)
                return mm(bk[:, P:P + 256], q[:, P:256], k[:, 0:256], start=True, stop=True)

            def values(o, h, g, n, kt, first, last):
                b = 0 if n == 0 else 1 + kt
                return mm(o, od.PT[:, h % 2, g, b * P:(b + 1) * P], od.V[:, g, kt, h * P:(h + 1) * P], start=first, stop=last)

            attn("od", 4, 3, 1, scores, od.EX, values, 128)
            out_transposes("od", 4, [("od", "o", 0), ("od", "o", 1)])
            out_proj("od", OD_OUT, 2)

        def mixer2(m, l):
            t0 = BASE[f"{m}_in"]
            hT_ready(4 + 2 * l)
            ab = (m, "ab")
            claim(pe, ab)
            await_tile(t0)
            for j in range(2):
                for k in range(KC):
                    ins = mm(bank(ab)[0:6, j * 256:(j + 1) * 256], in_tile(t0)[:, k, 128 + 6 * j:134 + 6 * j], HT[:, k, :],
                             start=(k == 0), stop=(k == KC - 1))
            done(ins, ab)
            in_channel(t0, (m, "in", 7), units=((0, 128), (140, 6)))
            for j in range(M2_IN - 1):
                jj = j if j < 7 else j + 1
                (in_channel if jj < 8 else in_token)(t0 + 1 + j, (m, "in", jj))
                if jj in M2_SUMS:
                    i = M2_SUMS[jj]
                    k = M2_SUM_ORDER.index(i)
                    hv = M2_SUM_HALVES[i]
                    sums((m, "ss", i), m2.SQ[:, k % 2, :], m + "_sq", k + 1, blk64, 256 * hv[0], 256 * len(hv))
            key = (m, "py")
            claim(pe, key)
            await_free_of(pe, (m, "in", 11))
            pm = cst("pool").rearrange("p (t g n) -> p t g n", t=2, g=4)
            for g in range(4):
                r = slice(64 * (g % 2), 64 * (g % 2) + 64)
                for tt in range(NT):
                    ins = mm(bank(key)[r, (g // 2) * 256:(g // 2 + 1) * 256], m2.XP[:, tt, g * 64:(g + 1) * 64],
                             pm[:, tt, g, :], start=(tt == 0), stop=(tt == NT - 1))
            done(ins, key)
            key = (m, "pz")
            claim(pe, key)
            await_free_of(pe, (m, "py"))
            pw = v3(prm(f"poolw{l}"), 2)
            for g in range(4):
                r = slice(64 * (g % 2), 64 * (g % 2) + 64)
                ins = mm(bank(key)[r, (g // 2) * 256:(g // 2 + 1) * 256], pw[r, g // 2, :], m2.PX[r, g // 2, :],
                         start=True, stop=True)
            done(ins, key)
            key = (m, "rowT")
            claim(pe, key)
            pe.wait_ge(sem(m + "_rows"), 1)
            G_, GL_, BT_, NG_ = m2.ROW[0:6, 0, :], m2.ROW[0:6, 1, :], m2.ROW[0:6, 2, :], m2.ROW[0:6, 3, :]
            for t in range(NT):
                for j, src in enumerate((G_, GL_, BT_)):
                    ins = pe.transpose(bank(key)[:, (t * 3 + j) * 6:(t * 3 + j) * 6 + 6], src[:, t * P:(t + 1) * P], ident[0:6, 0:6])
            done(ins, key)
            hp = v3(sel("selhp"), 3)
            for name, src in (("gb", G_), ("bb", BT_)):
                for j in range(2):
                    key = (m, name, j)
                    claim(pe, key)
                    for c in range(2 - j):
                        ins = mm(bank(key)[:, c * 256:(c + 1) * 256], hp[0:6, 2 * j + c, :], src, start=True, stop=True)
                    done(ins, key)
            pe.wait_ge(sem(m + "_qk"), 1)
            pe.wait_ge(sem(m + "_v"), 2)
            for t in range(NT):
                key = (m, "kT", t)
                claim(pe, key)
                for c in range(3):
                    ins = pe.transpose(bank(key)[:, c * P:(c + 1) * P], m2.QKN[:, 3 + c, t * P:(t + 1) * P], ident)
                done(ins, key)
            for t in range(NT):
                key = (m, "vT", t)
                claim(pe, key)
                for c in range(3):
                    ins = pe.transpose(bank(key)[:, c * P:(c + 1) * P], m2.Y[:, 6 + c, t * P:(t + 1) * P], ident)
                done(ins, key)
            s6 = v3(sel("sel6"), 6)
            for q in range(3):
                key = (m, "dec", q)
                claim(pe, key)
                for i in range(4):
                    t, h = PAIRS[4 * q + i]
                    o = bank(key)[:, i * P:(i + 1) * P]
                    mm(o, s6[0:6, h, 0:P], G_[:, t * P:(t + 1) * P], start=True, stop=False)
                    mm(o, NG_[:, t * P:(t + 1) * P], s6[0:6, h, 0:P], start=False, stop=False)
                    ins = mm(o, ident, cst("gdneg"), start=False, stop=True)
                done(ins, key)
            for j in range(2):
                await_free_of(pe, (m, "bb", j))
            for name, src, base in (("kk", m2.KB, 0), ("qk", m2.QKN, 0)):
                for q in range(3):
                    key = (m, name, q)
                    claim(pe, key)
                    for i in range(4):
                        t, h = PAIRS[4 * q + i]
                        r = slice(64 * (h % 2), 64 * (h % 2) + 64)
                        if q == 1 and i == 2:
                            fence(ins)
                        ins = mm(bank(key)[:, i * P:(i + 1) * P], m2.QKN[r, 3 + h // 2, t * P:(t + 1) * P],
                                 src[r, h // 2, t * P:(t + 1) * P], start=True, stop=True)
                    done(ins, key)
            for s in range(GD_STEPS + 1):
                for q in range(3):
                    key = (m, "M", s, q)
                    claim(pe, key)
                    pe.wait_ge(sem(m + "_of"), s + 1)
                    if s == 1:
                        await_free_of(pe, (m, "M", 0, q))
                    elif s:
                        await_free_of(pe, (m, "X", s - 1, q))
                    for i in range(4):
                        z = 4 * q + i
                        ins = mm(bank(key)[:, i * P:(i + 1) * P], m2.OF[:, z, :], ident if s == 0 else m2.DI[:, z, :],
                                 start=True, stop=True)
                    done(ins, key)
                if s == 0:
                    continue
                for q in range(3):
                    await_free_of(pe, (m, "M", s, q))
                    if s == 1:
                        pe.wait_ge(sem(m + "_ui"), 1)
                    else:
                        await_free_of(pe, (m, "Y", s - 1, q))
                    if s < GD_STEPS:
                        key = (m, "X", s, q)
                        claim(pe, key)
                        for i in range(4):
                            z = 4 * q + i
                            ins = mm(bank(key)[:, i * P:(i + 1) * P], m2.UI[:, z, :], m2.M1[:, z, :], start=True, stop=True)
                        done(ins, key)
                    key = (m, "Y", s, q)
                    claim(pe, key)
                    for i in range(4):
                        z = 4 * q + i
                        ins = mm(bank(key)[:, i * P:(i + 1) * P], m2.M1[:, z, :], m2.UI[:, z, :], start=True, stop=True)
                    done(ins, key)
            for q in range(3):
                await_free_of(pe, (m, "Y", GD_STEPS, q))
            for t in range(NT):
                await_free_of(pe, (m, "kT", t))
                await_free_of(pe, (m, "vT", t))
            for t in range(NT):
                key = (m, "u", t)
                claim(pe, key)
                for h in range(6):
                    ins = mm(bank(key)[:, h * 64:(h + 1) * 64], m2.UI[:, PAIRS.index((t, h)), :], m2.VB[:, t, h * 64:(h + 1) * 64],
                             start=True, stop=True)
                done(ins, key)
                key = (m, "w", t)
                claim(pe, key)
                for h in range(6):
                    ins = mm(bank(key)[64 * (h % 2):64 * (h % 2) + 64, (h // 2) * P:(h // 2 + 1) * P],
                             m2.KBG[:, t, h * 64:(h + 1) * 64], m2.UI[:, PAIRS.index((t, h)), :], start=True, stop=True)
                done(ins, key)
            pe.wait_ge(sem(m + "_qd"), 1)
            for q in range(3):
                await_free_of(pe, (m, "qk", q))
            for n in range(NCH):
                t, p0 = n // 2, 64 * (n % 2)
                rp = slice(p0, p0 + 64)
                cols = slice(n * CH, (n + 1) * CH)
                await_free_of(pe, (m, "u", t))
                if n:
                    key = (m, "vp", n)
                    claim(pe, key)
                    await_free_of(pe, (m, "kv", n - 1))
                    await_free_of(pe, (m, "w", t))
                    for c in range(3):
                        ins = mm(bank(key)[rp, c * P:(c + 1) * P], m2.WT[:, c, cols], m2.S[:, n % 2, c, :], start=True, stop=True)
                    done(ins, key)
                key = (m, "o", t)
                if p0 == 0:
                    claim(pe, key)
                for c in range(3):
                    mm(bank(key)[rp, c * P:(c + 1) * P], m2.QD[:, c, cols], m2.S[:, n % 2, c, :], start=(c == 0), stop=False,
                       skip_group_check=True)
                if n:
                    await_free_of(pe, (m, "vp", n))
                if n < NCH - 1:
                    key = (m, "kv", n)
                    claim(pe, key)
                    for c in range(3):
                        ins = mm(bank(key)[:, c * P:(c + 1) * P], m2.KDEC[rp, t, c * P:(c + 1) * P], m2.UU[rp, t, c * P:(c + 1) * P],
                                 start=True, stop=True)
                    done(ins, key)
                if p0:
                    key = (m, "o", t)
                    for h in range(6):
                        ins = mm(bank(key)[:, h * 64:(h + 1) * 64], m2.ATQ[:, PAIRS.index((t, h)), :], m2.UU[:, t, h * 64:(h + 1) * 64],
                                 start=False, stop=(h == 5), skip_group_check=True)
                    done(ins, key)
            for j in (4, 5, 6, 7):
                await_free_of(pe, (m, "in", j))
            pe.wait_ge(sem(m + "_frow"), 1)
            C_, NC_ = m2.ROW2[0:6, 2, :], m2.ROW2[0:6, 3, :]
            await_free_of(pe, (m, "in", 9))
            await_free_of(pe, (m, "in", 10))

            def scores(bk, h, g):
                r = slice(64 * (h % 2), 64 * (h % 2) + 64)
                q, k = m2.FQK[r, h // 2, :], m2.FQK[r, 3 + h // 2, :]
                for n, (o, w) in enumerate(((0, P), (P, 256))):
                    qs = slice(n * P, (n + 1) * P)
                    mm(bk[:, o:o + w], q[:, qs], k[:, 0:w], start=True, stop=False)
                    mm(bk[:, o:o + w], C_[:, qs], s6[0:6, h, 0:w], start=False, stop=False)
                    ins = mm(bk[:, o:o + w], s6[0:6, h, 0:P], NC_[:, 0:w], start=False, stop=True)
                return ins

            def values(o, h, g, n, kt, first, last):
                b = 0 if n == 0 else 1 + kt
                return mm(o, m2.PT[:, h % 2, 0, b * P:(b + 1) * P], m2.FV[:, kt, h * 64:(h + 1) * 64], start=first, stop=last)

            attn(m + "f", 6, 1, 1, scores, m2.EX, values, 64)
            out_transposes(m, 6, [(m, "o", 0), (m, "o", 1), (m + "f", "o", 0), (m + "f", "o", 1)])
            await_free_of(pe, (m, "pz"))
            out_proj(m, M2_OUT, 3)

        def router():
            hT_ready(7)
            key = ("router", "logits")
            claim(pe, key)
            rt = v3(prm("router"), KC)
            for t in range(NT):
                for k in range(KC):
                    ins = mm(bank(key)[:, t * 8:(t + 1) * 8], HT[:, k, t * P:(t + 1) * P], rt[:, k, :],
                             start=(k == 0), stop=(k == KC - 1))
            done(ins, key)
            key = ("router", "place")
            claim(pe, key)
            pe.wait_ge(sem("chosen"), 1)
            m3 = mo.MASK.rearrange("p (t e) -> p t e", t=NT)
            earlier = cst("earlier")
            mm(bank(key)[:, 0:8], earlier, m3[:, 0, :], start=True, stop=True)
            mm(bank(key)[:, 8:16], ones, m3[:, 0, :], start=True, stop=False)
            mm(bank(key)[:, 8:16], earlier, m3[:, 1, :], start=False, stop=True)
            mm(bank(key)[:, 16:24], ones, m3[:, 0, :], start=True, stop=False)
            done(mm(bank(key)[:, 16:24], ones, m3[:, 1, :], start=False, stop=True), key)

        def moe(p):
            name = moe_name[p]
            w0, k0 = BASE["moe"] + p * MOE_TILES, ffn_k0[name]
            pe.wait_ge(sem("moe_sel"), p + 1)
            for j in range(4):
                key = ("moe", p, "selT", j)
                claim(pe, key)
                for k in range(2):
                    for t in range(NT):
                        ins = pe.transpose(bank(key)[:, k * 256 + t * P:k * 256 + (t + 1) * P], mo.GSEL[:, t, 2 * j + k, :], ident)
                done(ins, key)
            for c in range(KC):
                for hf in range(2):
                    key = ("moe", p, "gx", 2 * c + hf)
                    claim(pe, key)
                    for t in range(NT):
                        ins = mm(bank(key)[:, :], HN[:, t, c * P:(c + 1) * P],
                                 mo.SEL[:, t, 4 * hf:4 * hf + 4, :].rearrange("p e s -> p (e s)"), start=(t == 0), stop=(t == 1))
                    done(ins, key)
            for b in range(4):
                claim(pe, ("y", name, b))
                mm(PS[b][:, :], ident, X[:, b // 2, (b % 2) * 512:(b % 2 + 1) * 512], start=True, stop=False, skip_group_check=True)
            for j in range(12, 16):
                await_free_of(pe, ("moe", p, "gx", j))
            for j in range(4):
                await_free_of(pe, ("moe", p, "selT", j))

            def await_moe_tile(ts, i):
                pe.wait_ge(w_full[ts % RING], 16 * (ts // RING + 1) + 16 * (3 * G_EXP // RING) * i)

            def up(gs, i, first=False):
                b, e = 6 + gs % 2, gs // G_EXP
                pe.wait_ge(free[b], k0[b] + gs // 2 + (G_EXP // 2) * i)
                for half in range(2):
                    ts = w0 + half if first else w0 + 3 * gs - 1 + half
                    await_moe_tile(ts, i)
                    for c in range(2):
                        for kk in range(KC):
                            x = mo.XG[:, kk, e, :] if isinstance(i, int) else mo.XG[:, kk, bass.ds(i + e, 1), :].rearrange("p e s -> p (e s)")
                            o = half * 256 + c * P
                            ins = mm(PS[b][:, o:o + P], in_tile(ts)[:, kk, c * P:(c + 1) * P], x, start=(kk == 0), stop=(kk == KC - 1))
                    ins.then_inc(w_used, 1)

            def down(gs, i, ts):
                await_moe_tile(ts, i)
                b = 6 + gs % 2
                pe.wait_ge(free[b], k0[b] + gs // 2 + 1 + (G_EXP // 2) * i)
                if gs % G_EXP == 0:
                    for b in (4, 5):
                        pe.wait_ge(free[b], k0[b] + gs // G_EXP + i)
                for c in range(2):
                    for hf in range(2):
                        ins = mm(PS[4 + hf][:, :], mo.GH[:, gs % 2, c * P:(c + 1) * P], out_tile(ts)[:, c, hf * 512:(hf + 1) * 512],
                                 start=(gs % G_EXP == 0 and c == 0), stop=(gs % G_EXP == G_EXP - 1 and c == 1), skip_group_check=True)
                ins.then_inc(w_used, 1)

            def scatter(e, i, last=False):
                for b in (4, 5):
                    pe.wait_ge(free[b], k0[b] + e + 1 + i)
                for t in range(NT):
                    for hf in range(2):
                        ins = mm(PS[2 * t + hf][:, :], mo.GS[:, t * P:(t + 1) * P], mo.YE[:, hf * 512:(hf + 1) * 512], start=False, stop=last, skip_group_check=True)
                        if last:
                            done(ins, ("y", name, 2 * t + hf))
                if not last:
                    ins.then_inc(sem("moe_scattered"), 1)

            up(0, 0, True)
            up(1, 0)
            down(0, 0, w0 + 4)
            with pe.Fori(0, N_EXP - 1) as i:
                for u in range(G_EXP):
                    g = 2 + u
                    up(g, i)
                    if g == G_EXP + 1:
                        scatter(0, i)
                    down(g - 1, i, w0 + 3 * (g - 1) + 4)
            for g in range(2 + (N_EXP - 1) * G_EXP, MOE_GROUPS):
                up(g, 0)
                down(g - 1, 0, w0 + 3 * (g - 1) + 4)
            down(MOE_GROUPS - 1, 0, w0 + MOE_TILES - 1)
            scatter(N_EXP - 1, 0, True)

        def ffn(name, groups, kind):
            w0, k0 = BASE[name], ffn_k0[name]
            body = 2

            def up(gs, i, first):
                g = gs + body * i
                for half in range(2):
                    ts = w0 + half if first else w0 + 3 * gs - 1 + half
                    b = 4 + 2 * (gs % 2) + half
                    pe.wait_ge(w_full[ts % RING], 16 * (ts // RING + 1) + 16 * (3 * body // RING) * i)
                    k = k0[b] + gs // 2
                    if not (isinstance(k, int) and k == 0):
                        pe.wait_ge(free[b], k + (body // 2) * i)
                    for c in range(2):
                        for kk in range(KC):
                            ins = mm(PS[b][:, c * 256:(c + 1) * 256], in_tile(ts)[:, kk, c * P:(c + 1) * P], HT[:, kk, :],
                                     start=(kk == 0), stop=(kk == KC - 1))
                    ins.then_inc(w_used, 1)

            def down(gs, i, ts):
                pe.wait_ge(w_full[ts % RING], 16 * (ts // RING + 1) + 16 * (3 * body // RING) * i)
                if kind == "conv":
                    pe.wait_ge(sem(name + "_v"), 7 * (gs + 1) + 7 * body * i)
                else:
                    b = 5 + 2 * (gs % 2)
                    pe.wait_ge(free[b], k0[b] + gs // 2 + 1 + (body // 2) * i)
                if gs == 0:
                    for b in range(4):
                        claim(pe, ("y", name, b))
                for c in range(2):
                    for tt in range(NT):
                        for hf in range(2):
                            ins = mm(PS[2 * tt + hf][:, :], ff.GH[:, gs % 2, c, tt * P:(tt + 1) * P],
                                     out_tile(ts)[:, c, hf * 512:(hf + 1) * 512],
                                     start=(gs == 0 and c == 0), stop=(gs == groups - 1 and c == 1), skip_group_check=True)
                ins.then_inc(w_used, 1)

            hT_ready({"ffn0": 1, "ffn1": 3, "ffn2": 5}[name])
            up(0, 0, True)
            up(1, 0, False)
            down(0, 0, w0 + 4)
            rounds = (groups - 2) // body
            with pe.Fori(0, rounds) as i:
                for u in range(body):
                    g = 2 + u
                    up(g, i, False)
                    down(g - 1, i, w0 + 3 * (g - 1) + 4)
            assert 3 * body % RING == 0 and body % 2 == 0
            for g in range(2 + rounds * body, groups):
                up(g, 0, False)
                down(g - 1, 0, w0 + 3 * (g - 1) + 4)
            down(groups - 1, 0, w0 + 3 * groups - 1)

        pe.wait_ge(s_const, 48)
        for st in order:
            if st[0] == "norm":
                norm(st[1])
            elif st[0] == "even":
                even()
            elif st[0] == "odd":
                odd()
            elif st[0] == "m2":
                mixer2(*st[1:])
            elif st[0] == "router":
                router()
            elif st[0] == "moe":
                moe(0)
                with pe.If(more_tokens(pe) > 0):
                    moe(1)
            else:
                ffn(*st[1:])

    @block.scalar
    def _(act):
        A = act.activation
        chain = [0]
        s_act = sem("act_chain")

        def link(ins):
            chain[0] += 1
            ins.then_inc(s_act, 1)
            act.wait_ge(s_act, chain[0])

        def norm(n):
            if n == 0:
                act.wait_ge(s_in, 16)
            else:
                for b in range(4):
                    await_free_of(act, ("y", resid_of[n], b))
            for t in range(NT):
                ins = A(HT[:, 4 * t:4 * t + 4, :].rearrange("p a b -> p (a b)"), X[:, t, :], ACT.Square,
                        accum_out=st_ss[:, t:t + 1])
            link(ins)
            link(A(st_rs, st_ss, ACT.Ln, scale=1.0 / D, bias=eps))
            A(st_rs, st_rs, ACT.Exp, scale=-0.5).then_inc(sem("rstd"), 1)
            g = prm("norm")
            for b in range(2):
                key = ("norm", n, b)
                await_full(act, key)
                for k in range(2):
                    c = 2 * b + k
                    ins = A(HT[:, c, :], bank(key)[:, k * 256:(k + 1) * 256], ACT.Copy, scale=g[:, n * KC + c:n * KC + c + 1])
                release(ins, key)

        def squares(src, sq, name):
            A(sq, src, ACT.Square).then_inc(sem(name), 1)

        def rsqrt(key, rs, name, scale, o=0, w=512):
            await_full(act, key)
            release(A(rs[:, o:o + w], bank(key)[:, o:o + w], ACT.Ln, scale=scale, bias=eps), key)
            await_free_of(act, key)
            A(rs[:, o:o + w], rs[:, o:o + w], ACT.Exp, scale=-0.5).then_inc(sem(name), 1)

        def attn(name, heads, groups, combine, SM, EX, PT):
            for i in range(heads + 1):
                if i < heads:
                    for c in range(combine):
                        u = i * combine + c
                        act.wait_ge(sem(name + "_mx"), u + 1)
                        if i >= 2 and c == 0:
                            if combine == 1:
                                for g in range(groups):
                                    await_full(act, (name, "t", i - 2, g))
                            else:
                                act.wait_ge(sem(name + "_w"), i - 1)
                        b = u % (2 * combine)
                        for n, sl in enumerate((slice(0, P), slice(P, 384))):
                            j = 2 * u + n
                            ins = A(EX[:, b, :, sl], SM[:, u % 2, :, sl], ACT.Exp, bias=st_mx[:, j:j + 1],
                                    accum_out=st_sum[:, j:j + 1])
                        ins.then_inc(sem(name + "_e"), 1)
                if i >= 1:
                    for g in range(groups):
                        key = (name, "t", i - 1, g)
                        await_full(act, key)
                        release(A(PT[:, (i - 1) % 2, g, :], bank(key)[:, 0:384], ACT.Copy), key)

        def out_norm(name, heads, width, sq, sname):
            for t in range(NT):
                key = (name, "o", t)
                await_full(act, key)
                for h in range(heads):
                    ins = A(sq[:, t, h * width:(h + 1) * width], bank(key)[:, h * width:(h + 1) * width], ACT.Square,
                            accum_out=st_o[:, t * 8 + h:t * 8 + h + 1])
                link(ins)
                o = slice(t * 8, t * 8 + heads)
                link(A(st_or[:, o], st_o[:, o], ACT.Ln, scale=1.0 / width, bias=eps))
                A(st_or[:, o], st_or[:, o], ACT.Exp, scale=-0.5).then_inc(sem(sname), 1)

        def out_T(name, banks):
            for j in range(0, banks, 2):
                key = (name, "oT", j)
                await_full(act, key)
                release(A(OT[:, 2 * j:2 * j + 2, :].rearrange("p a b -> p (a b)"), bank(key)[:, :], ACT.Copy), key)

        def copy_half(dst, key, j):
            await_full(act, key)
            release(A(dst[:, :, j * 256:(j + 1) * 256], v3(bank(key)[:, :], 2), ACT.Copy), key)

        def even():
            key = ("ev", "ar")
            await_full(act, key)
            release(A(ev.arT[0:16, :], bank(key)[0:16, 0:256], ACT.Copy), key)
            key = ("ev", "la")
            await_full(act, key)
            ba = prm("ba")
            for c in range(2):
                ins = A(ev.T1[:, c * 256:(c + 1) * 256], bank(key)[:, c * 256:(c + 1) * 256], ACT.Abs, bias=ba[:, c:c + 1])
            ins.then_inc(sem("ev_a"), 1)
            act.wait_ge(sem("ev_a"), 1)
            link(A(ev.T1, ev.T1, ACT.Exp, scale=-1.0))
            A(ev.T1, ev.T1, ACT.Ln, bias=one).then_inc(sem("ev_a"), 1)
            act.wait_ge(sem("ev_b"), 1)
            A(ev.EB, ev.B, ACT.Exp, scale=1.0 / 16)
            A(ev.ENB, ev.B, ACT.Exp, scale=-1.0 / 16).then_inc(sem("ev_a"), 1)
            act.wait_ge(sem("ev_b"), 2)
            A(ev.EW, ev.EW, ACT.Exp, scale=1.0 / 16).then_inc(sem("ev_a"), 1)
            for j in range(2):
                copy_half(ev.V, ("ev", "av", j), j)
            for j in range(2):
                key = ("ev", "ag", j)
                await_full(act, key)
                release(A(ev.GG[:, :, j * 256:(j + 1) * 256], v3(bank(key)[:, :], 2), ACT.Silu), key)
            for j in range(4):
                key = ("ev", "bqk", j)
                await_full(act, key)
                if j >= 2:
                    await_full(act, ("ev", "ss", j - 2))
                squares(bank(key)[:, :], ev.SQ[:, j % 2, :], "ev_sq")
                if j:
                    if j >= 3:
                        await_free_of(act, ("ev", "bqk", j - 3))
                    rsqrt(("ev", "ss", j - 1), ev.RS[:, (j - 1) % 2, :], "ev_rs", 1.0 / 64)
            copy_half(ev.BV, ("ev", "bv", 0), 0)
            await_free_of(act, ("ev", "bqk", 1))
            rsqrt(("ev", "ss", 3), ev.RS[:, 1, :], "ev_rs", 1.0 / 64)
            copy_half(ev.BV, ("ev", "bv", 1), 1)
            key = ("ev", "kwT")
            await_full(act, key)
            release(A(ev.KWT.rearrange("p a b -> p (a b)"), bank(key)[:, :], ACT.Copy), key)
            out_norm("ev", 4, 128, ev.SQ, "ev_or")
            attn("evd", 4, 1, 2, ev.SM, ev.EX, ev.PT)
            await_free_of(act, ("ev", "o", 1))
            out_norm("evd", 4, 128, ev.SQ, "ev_or")
            out_T("ev", 4)

        def odd():
            k = 0
            for g in range(3):
                for j in range(4):
                    key = ("od", "qk", g, j)
                    await_full(act, key)
                    if k >= 2:
                        await_full(act, ("od", "ss", (k - 2) // 4, (k - 2) % 4))
                    squares(bank(key)[:, :], od.SQ[:, k % 2, :], "od_sq")
                    if j:
                        od_scale(k - 1)
                    k += 1
                copy_half(od.V[:, g], ("od", "v", g, 0), 0)
                od_scale(k - 1)
                copy_half(od.V[:, g], ("od", "v", g, 1), 1)
            attn("od", 4, 3, 1, od.SM, od.EX, od.PT)
            out_T("od", 2)

        def od_scale(k):
            if k >= 2:
                await_free_of(act, ("od", "qk", (k - 2) // 4, (k - 2) % 4))
            rsqrt(("od", "ss", k // 4, k % 4), od.RS[:, k % 2, :], "od_rs", 1.0 / 128)

        def mixer2(m, l):
            key = (m, "ab")
            ra = sem(m + "_ra")
            await_full(act, key)
            RA = m2.ROW2[0:6, 0, :]
            link(A(RA, bank(key)[0:6, 0:256], ACT.Abs, bias=prm(f"dtb{l}")[0:6, :]))
            link(A(RA, RA, ACT.Exp, scale=-1.0))
            A(RA, RA, ACT.Ln, bias=one[0:6, :]).then_inc(ra, 1)
            A(m2.ROW[0:6, 2, :], bank(key)[0:6, 256:512], ACT.Sigmoid).then_inc(ra, 1)
            key = (m, "in", 7)
            RF = m2.ROW2[0:6, 3, :]
            await_full(act, key)
            link(A(RF, bank(key)[0:6, 256:512], ACT.Abs, bias=prm(f"fb{l}")[0:6, :]))
            link(A(RF, RF, ACT.Exp, scale=-1.0))
            A(RF, RF, ACT.Ln, bias=one[0:6, :]).then_inc(ra, 1)
            taps = v3(prm(f"dnconv{l}"), 9)

            def square_of(k):
                j = M2_SUM_ORDER[k]
                if k >= 2:
                    await_full(act, (m, "ss", M2_SUM_ORDER[k - 2]))
                hv = M2_SUM_HALVES[j]
                o, w = 256 * hv[0], 256 * len(hv)
                src = m2.Y[:, 2 * j:2 * j + 2, :].rearrange("p a b -> p (a b)") if j < 3 else bank((m, "in", j))[:, :]
                squares(src[:, o:o + w], m2.SQ[:, k % 2, o:o + w], m + "_sq")

            def scale_of(k):
                j = M2_SUM_ORDER[k]
                if k >= 2:
                    act.wait_ge(sem(m + "_nu"), k - 1)
                hv = M2_SUM_HALVES[j]
                rsqrt((m, "ss", j), m2.RS[:, k % 2, :], m + "_rs", 1.0 if j < 3 else 1.0 / 64, 256 * hv[0], 256 * len(hv))

            square_of(0)
            for j in list(range(7)) + [8, 9, 10, 11]:
                key = (m, "in", j)
                await_full(act, key)
                if j < 5:
                    us = [u for u in (2 * j, 2 * j + 1) if u < 9]
                    for u in us:
                        ins = A(m2.Y[:, u, :], bank(key)[:, (u % 2) * 256:(u % 2) * 256 + 256], ACT.Copy, scale=taps[:, u, 3:4])
                    ins.then_inc(sem(m + "_c0"), 1)
                    act.wait_ge(sem(m + "_c1"), j + 1)
                    for u in us:
                        ins = A(m2.Y[:, u, :], m2.Y[:, u, :], ACT.Silu)
                    if j < 3:
                        link(ins)
                    else:
                        ins.then_inc(sem(m + "_v"), 1)
                elif j == 8:
                    release(A(m2.ZG[:, :, 0:256], v3(bank(key)[:, :], 2), ACT.Silu), key)
                elif j == 9:
                    A(m2.ZG[:, :, 256:384], v3(bank(key)[:, :], 2)[:, :, 0:P], ACT.Silu).then_inc(sem(m + "_z"), 1)
                    release(A(m2.FV[:, :, 0:P], v3(bank(key)[:, :], 2)[:, :, P:256], ACT.Copy), key)
                elif j == 10:
                    release(A(m2.FV[:, :, P:384], v3(bank(key)[:, :], 2), ACT.Copy), key)
                elif j == 11:
                    release(A(m2.XP, v3(bank(key)[:, :], 2), ACT.Copy), key)
                if j in M2_SUM_ORDER:
                    square_of(M2_SUM_ORDER.index(j))
                if j in M2_SUMS:
                    scale_of(M2_SUM_ORDER.index(M2_SUMS[j]))
            key = (m, "py")
            await_full(act, key)
            release(A(m2.PX.rearrange("p a b -> p (a b)"), bank(key)[:, :], ACT.Copy), key)
            key = (m, "rowT")
            await_full(act, key)
            rows = bank(key)[:, 0:36].rearrange("p (t j h) -> p t j h", t=2, j=3)
            A(st_tm[:, :, 0:2, :], rows[:, :, 0:2, :], ACT.Exp)
            release(A(st_tm[:, :, 2, :], rows[:, :, 2, :], ACT.Copy), key)
            for j in range(2):
                key = (m, "gb", j)
                w = 2 - j
                await_full(act, key)
                release(A(m2.EGB[:, 2 * j:2 * j + w, :], bank(key)[:, 0:256 * w].rearrange("p (a b) -> p a b", a=w), ACT.Exp), key)
            for q in range(3):
                key = (m, "dec", q)
                await_full(act, key)
                release(A(m2.DEC[:, 4 * q:4 * q + 4, :], bank4(key), ACT.Exp), key)
            for s in range(1, GD_STEPS + 1):
                for q in range(3):
                    key = (m, "M", s, q)
                    await_full(act, key)
                    if s > 1:
                        await_full(act, (m, "Y", s - 1, q))
                    else:
                        await_full(act, (m, "pz"))
                    release(A(m2.M1[:, 4 * q:4 * q + 4, :], bank4(key), ACT.Copy), key)
            for t in range(NT):
                key = (m, "u", t)
                await_full(act, key)
                release(A(m2.UU[:, t, :], bank(key)[:, 0:384], ACT.Copy), key)
            for t in range(NT):
                key = (m, "o", t)
                await_full(act, key)
                A(m2.SQ[:, t, 0:384], bank(key)[:, 0:384], ACT.Square).then_inc(sem(m + "_osq"), 1)
                act.wait_ge(sem(m + "_oss"), t + 1)
                o = slice(t * 8, t * 8 + 6)
                link(A(st_or[:, o], st_o[:, o], ACT.Ln, scale=1.0 / 64, bias=eps))
                A(st_or[:, o], st_or[:, o], ACT.Exp, scale=-0.5).then_inc(sem(m + "_ors"), 1)
            attn(m + "f", 6, 1, 1, m2.SM, m2.EX, m2.PT)
            out_T(m, 3)

        def router():
            act.wait_ge(sem("r_mx"), 1)
            for t in range(NT):
                ins = A(mo.EX[:, t * 8:t * 8 + 8], mo.LG[:, t * 8:t * 8 + 8], ACT.Exp, bias=st_mx[:, t:t + 1],
                        accum_out=st_sum[:, t:t + 1])
            ins.then_inc(sem("r_e"), 1)

        def moe(p):
            name = moe_name[p]
            w0, k0 = BASE["moe"] + p * MOE_TILES, ffn_k0[name]
            if p:
                await_full(act, ("y", moe_name[0], 3))
            for j in range(4):
                key = ("moe", p, "selT", j)
                await_full(act, key)
                release(A(mo.SELT[:, 2 * j:2 * j + 2, :].rearrange("p e t -> p (e t)"), bank(key)[:, :], ACT.Copy), key)
            g = prm("norm")
            for c in range(KC):
                key = ("moe", p, "gx", 2 * c)
                await_full(act, key)
                release(A(mo.XG[:, c, 0:4, :].rearrange("p e s -> p (e s)"), bank(key)[:, :], ACT.Copy,
                          scale=g[:, 7 * KC + c:7 * KC + c + 1]), key)

            def group(gs, i, first=False):
                hb, b = gs % 2, 6 + gs % 2
                act.wait_ge(w_used, w0 + (1 if first else 3 * gs) + 1 + 3 * G_EXP * i)
                act.wait_ge(free[b], k0[b] + gs // 2 + (G_EXP // 2) * i)
                A(mo.SG[:, hb, :], PS[b][:, 0:256], ACT.Silu).then_inc(sem("moe_silu"), 1)

            def expert_out(e, i, tile):
                act.wait_ge(w_used, tile + 1 + 3 * G_EXP * i)
                if p or e or not isinstance(i, int):
                    act.wait_ge(sem("moe_scattered"), (N_EXP - 1) * p + e + i)
                A(mo.YE[:, 0:512], PS[4][:, :], ACT.Copy).then_inc(free[4], 1)

            moe_loop(act, group, expert_out, w0)

        def ffn(name, groups, kind):
            w0, k0 = BASE[name], ffn_k0[name]
            body = 2
            f = lambda ap: ap.rearrange("p c t -> p (c t)")
            sv, sc = sem(name + "_v"), sem(name + "_a")

            def group(gs, i, first=False):
                hb, b = gs % 2, 4 + 2 * (gs % 2)
                tile = w0 + (0 if first else 3 * gs - 1)
                dt, dk = 3 * body * i, (body // 2) * i
                act.wait_ge(w_used, tile + 1 + dt)
                if kind != "conv":
                    if gs >= 2:
                        act.wait_ge(free[b + 1], k0[b + 1] + gs // 2 + dk)
                    A(f(ff.SG[:, hb]), PS[b][:, :], ACT.Silu).then_inc(free[b], 1)
                    return
                if gs >= 2:
                    act.wait_ge(sv, 7 * (gs - 1) + 7 * body * i)
                off = PRM["conv0" if name == "ffn0" else "conv1"][0]
                for half, dst in enumerate((ff.YG, ff.YV)):
                    if half:
                        act.wait_ge(w_used, tile + 2 + dt)
                    for c in range(2):
                        unit = off + 4 * (22 * half + 2 * gs + c)
                        col = lambda j: PR[:, unit + j:unit + j + 1] if isinstance(i, int) else \
                            PR[:, bass.ds(8 * body * i + (unit + j), 1)]
                        ins = A(dst[:, hb, c, :], PS[b + half][:, c * 256:(c + 1) * 256], ACT.Identity, scale=col(2), bias=col(3))
                ins.then_inc(sc, 1)
                act.wait_ge(sv, 7 * gs + 5 + 7 * body * i)
                act.wait_ge(free[b], k0[b] + gs // 2 + 1 + dk)
                A(f(ff.SG[:, hb]), f(ff.YG[:, hb]), ACT.Silu).then_inc(sc, 1)

            group(0, 0, True)
            group(1, 0)
            rounds = (groups - 2) // body
            with act.Fori(0, rounds) as i:
                for u in range(body):
                    group(2 + u, i)
            for g in range(2 + rounds * body, groups):
                group(g, 0)

        act.wait_ge(s_const, 48)
        A(st_lam, st_lam, ACT.Copy) if False else None
        act.wait_ge(sem("prep"), 1)
        link(A(st_lam, st_lam, ACT.Exp))
        for l in range(2):
            ins = A(st_nea[0:6, l:l + 1], prm(f"alog{l}")[0:6, :], ACT.Exp)
        ins.then_inc(sem("prep_a"), 1)
        for st in order:
            if st[0] == "norm":
                norm(st[1])
            elif st[0] == "even":
                even()
            elif st[0] == "odd":
                odd()
            elif st[0] == "m2":
                mixer2(*st[1:])
            elif st[0] == "router":
                router()
            elif st[0] == "moe":
                moe(0)
                with act.If(more_tokens(act) > 0):
                    moe(1)
            else:
                ffn(*st[1:])

    @block.vector
    def _(dve):
        TT, TS, STT = dve.tensor_tensor, dve.tensor_scalar, dve.scalar_tensor_tensor
        chain = [0]
        s_dve = sem("dve_chain")

        def mark(ins):
            chain[0] += 1
            ins.then_inc(s_dve, 1)
            return chain[0]

        def after(n):
            dve.wait_ge(s_dve, n)

        def link(ins):
            after(mark(ins))

        def prep():
            dve.wait_ge(s_const, 48)
            link(TT(st_lamp, prm("lq"), prm("lk"), MUL))
            dve.tensor_reduce(st_lam, v3(st_lamp, 2), AX.X, ADD).then_inc(sem("prep"), 1)
            TS(st_gain[:, 0:1], prm("dq"), 0.125, None, MUL)
            TS(st_gain[:, 1:2], prm("odq"), 128 ** -0.5, None, MUL)
            for l in range(2):
                TS(st_gain[:, 2 + l:3 + l], prm(f"fxq{l}"), 0.125, None, MUL)
            link(TS(st_dg, prm("diff_gain"), 1.0 - LAMBDA_INIT, None, MUL))
            dve.wait_ge(sem("prep_a"), 1)
            link(TT(st_nlam, st_lam[:, 1:2], st_lam[:, 0:1], SUB))
            link(TS(st_nlam, st_nlam, LAMBDA_INIT, None, SUB))
            link(TS(st_nea[0:6, :], st_nea[0:6, :], -1.0, None, MUL))

        def norm(n):
            dve.wait_ge(sem("rstd"), n + 1)
            for t in range(NT):
                ins = TS(HN[:, t, :], X[:, t, :], st_rs[:, t:t + 1], None, MUL)
            ins.then_inc(sem("hn"), 1)
            g = prm("norm")
            for b in range(2, 4):
                key = ("norm", n, b)
                await_full(dve, key)
                for k in range(2):
                    c = 2 * b + k
                    ins = TS(HT[:, c, :], bank(key)[:, k * 256:(k + 1) * 256], g[:, n * KC + c:n * KC + c + 1], None, MUL)
                release(ins, key)

        def resid(name):
            for b in range(4):
                key = ("y", name, b)
                await_full(dve, key)
                xs = X[:, b // 2, (b % 2) * 512:(b % 2 + 1) * 512]
                release(TT(xs, xs, PS[b][:, :], ADD), key)

        def attn(name, heads, groups, combine, SM, EX, WC, masks):
            for i in range(heads + (combine > 1)):
                if i < heads:
                    for c in range(combine):
                        u = i * combine + c
                        if u >= 2:
                            dve.wait_ge(sem(name + "_e"), u - 1)
                        for g in range(groups):
                            key = (name, "s", u, g)
                            await_full(dve, key)
                            release(TT(SM[:, u % 2, g, :], bank(key)[:, 0:384], masks(g), ADD), key)
                        for g in range(groups):
                            await_free_of(dve, (name, "s", u, g))
                        for n, sl in enumerate((slice(0, P), slice(P, 384))):
                            j = 2 * u + n
                            ins = dve.tensor_reduce(st_mx[:, j:j + 1], SM[:, u % 2, :, sl], AX.XY, MAX, negate=True)
                        ins.then_inc(sem(name + "_mx"), 1)
                if combine > 1 and i >= 1:
                    h = i - 1
                    dve.wait_ge(sem(name + "_e"), 2 * h + 2)
                    if h >= 2:
                        await_full(dve, (name, "t", h - 2, 0))
                    link(dve.reciprocal(st_ri[:, 4 * h:4 * h + 4], st_sum[:, 4 * h:4 * h + 4]))
                    link(TS(st_rl, st_ri[:, 4 * h + 2:4 * h + 4], st_nlam, None, MUL))
                    e = 2 * (h % 2)
                    sls = (slice(0, P), slice(P, 384))
                    for n, sl in enumerate(sls):
                        ins = TS(EX[:, e + 1, 0, sl], EX[:, e + 1, 0, sl], st_rl[:, n:n + 1], None, MUL)
                    link(ins)
                    for n, sl in enumerate(sls):
                        ins = STT(WC[:, h % 2, 0, sl], EX[:, e, 0, sl], st_ri[:, 4 * h + n:4 * h + n + 1], EX[:, e + 1, 0, sl], MUL, ADD)
                    ins.then_inc(sem(name + "_w"), 1)

        def attn_out(name, heads, width, col):
            dve.wait_ge(sem(name + "_e"), heads)
            link(dve.reciprocal(st_ri[:, 0:2 * heads], st_sum[:, 0:2 * heads]))
            for n in range(NT):
                key = (name, "o", n)
                await_full(dve, key)
                o = bank(key)[:, 0:heads * width].rearrange("p (h v) -> p h v", h=heads)
                ri = st_ri[:, 0:2 * heads].rearrange("p (h n) -> p h n", n=2)[:, :, n]
                dst = HN[:, n, col:col + heads * width].rearrange("p (h v) -> p h v", h=heads)
                release(TT(dst, o, bc(ri, 2, width), MUL), key)

        def out_T(name, banks):
            for j in range(1, banks, 2):
                key = (name, "oT", j)
                await_full(dve, key)
                release(dve.tensor_copy(OT[:, 2 * j:2 * j + 2, :].rearrange("p a b -> p (a b)"), bank(key)[:, :]), key)

        def even():
            key = ("ev", "la")
            await_full(dve, key)
            dve.wait_ge(sem("ev_a"), 1)
            ba = prm("ba")
            for c in range(2):
                ins = TS(ev.MN[:, c * 256:(c + 1) * 256], bank(key)[:, c * 256:(c + 1) * 256], ba[:, c:c + 1], 0.0, ADD, MIN)
            release(ins, key)
            await_free_of(dve, key)
            dve.wait_ge(sem("ev_a"), 2)
            link(TT(ev.MN, ev.MN, ev.T1, SUB))
            dve.tensor_tensor_scan(ev.B, cst("reset"), ev.MN, 0.0, MUL, ADD).then_inc(sem("ev_b"), 1)
            dve.wait_ge(sem("ev_b"), 1)
            b3 = v3(ev.B, 8)
            TT(v3(ev.EW, 8), b3[:, :, CH - 1:CH].broadcast_to([P, 8, CH]), b3, SUB).then_inc(sem("ev_b"), 1)
            dve.wait_ge(sem("ev_a"), 3)
            key = ("ev", "aq")
            await_full(dve, key)
            release(STT(ev.QD, bank(key)[:, :], 0.125, ev.EB, MUL, MUL), key)
            key = ("ev", "ak")
            await_full(dve, key)
            TT(ev.KD, bank(key)[:, :], ev.ENB, MUL)
            dve.wait_ge(sem("ev_a"), 4)
            release(TT(ev.KW, bank(key)[:, :], ev.EW, MUL), key)
            await_free_of(dve, ("ev", "ag", 0))
            await_free_of(dve, ("ev", "ag", 1))
            gg = ev.GG.rearrange("p t (h v) -> p (t h) v", v=P)
            link(TT(gg, gg, bc(prm("gla_gain"), 1, 8), MUL))
            for j in range(4):
                key = ("ev", "bqk", j)
                dve.wait_ge(sem("ev_rs"), j + 1)
                gain = st_gain[:, 0:1] if j < 2 else prm("dk")
                release(STT(ev.QK[:, j].rearrange("p c t -> p (c t)"), bank(key)[:, :], gain, ev.RS[:, j % 2, :], MUL, MUL), key)
            for r in range(2):
                key = ("ev", "att", r)
                await_full(dve, key)
                release(TT(ev.ATT[:, 4 * r:4 * r + 4, :], bank4(key), bc(cst("glamask"), 1, 4), MUL), key)
            own = bc(blk64.rearrange("p (r v) -> p r v", r=2)[:, :, 0], 2, P)
            for n in range(NCH - 1):
                key = ("ev", "kv", n)
                await_full(dve, key)
                for c in range(2):
                    ins = TT(ev.ST[:, n, c], bank(key)[:, c * 256:(c + 1) * 256].rearrange("p (r v) -> p r v", r=2), own, MUL)
                if n:
                    link(ins)
                    for c in range(2):
                        e = c * 256 + n * CH + CH - 1
                        f = lambda k: ev.ST[:, k, c].rearrange("p r v -> p (r v)")
                        ins = STT(f(n), f(n - 1), ev.EB[:, e:e + 1], f(n), MUL, ADD)
                release(ins, key)
                await_free_of(dve, key)
            gate(("ev", "ev_or"), lambda t, h: ev.GG[:, t, h * P:(h + 1) * P], 0, 0)
            attn("evd", 4, 1, 2, ev.SM, ev.EX, ev.WC, lambda g: cst("cmask"))
            gate(("evd", "ev_or"), lambda t, h: st_dg, 512, 2)
            out_T("ev", 4)
            resid("ev")

        def gate(names, factor, col, count):
            for t in range(NT):
                key = (names[0], "o", t)
                dve.wait_ge(sem(names[1]), count + t + 1)
                for h in range(4):
                    ins = STT(HN[:, t, col + h * P:col + (h + 1) * P], bank(key)[:, h * P:(h + 1) * P],
                              st_or[:, t * 8 + h:t * 8 + h + 1], factor(t, h), MUL, MUL)
                release(ins, key)

        def odd():
            for k in range(12):
                g, j = divmod(k, 4)
                key = ("od", "qk", g, j)
                dve.wait_ge(sem("od_rs"), k + 1)
                gain = st_gain[:, 1:2] if j < 2 else prm("odk")
                release(STT(od.QK[:, g, j].rearrange("p c t -> p (c t)"), bank(key)[:, :], gain, od.RS[:, k % 2, :], MUL, MUL), key)
            dm = cst("dmask").rearrange("p (g k) -> p g k", g=3)
            attn("od", 4, 3, 1, od.SM, od.EX, None, lambda g: dm[:, g, :])
            attn_out("od", 4, 128, 0)
            out_T("od", 2)
            resid("od")

        def mixer2(m, l):
            ra = sem(m + "_ra")
            G_, GL_, BT_, NG_ = [m2.ROW[0:6, r, :] for r in range(4)]
            R0, R1, R2, R3 = [m2.ROW2[0:6, r, :] for r in range(4)]
            key = (m, "ab")
            dve.wait_ge(ra, 2)
            release(TS(R1, bank(key)[0:6, 0:256], prm(f"dtb{l}")[0:6, :], 0.0, ADD, MAX), key)
            await_free_of(dve, key)
            link(TT(R1, R1, R0, ADD))
            link(TS(R1, R1, st_nea[0:6, l:l + 1], None, MUL))
            link(dve.tensor_tensor_scan(G_, cst("reset")[0:6, 0:256], R1, 0.0, MUL, ADD))
            g3 = G_.rearrange("p (n c) -> p n c", c=CH)
            TT(GL_.rearrange("p (n c) -> p n c", c=CH), g3[:, :, CH - 1:CH].broadcast_to([6, NCH, CH]), g3, SUB)
            TS(NG_, G_, -1.0, None, MUL).then_inc(sem(m + "_rows"), 1)
            key = (m, "in", 7)
            await_full(dve, key)
            dve.wait_ge(ra, 3)
            dve.wait_ge(sem(m + "_sq"), 1)
            link(TS(R1, bank(key)[0:6, 256:512], prm(f"fb{l}")[0:6, :], 0.0, ADD, MIN))
            link(TT(R1, R1, R3, SUB))
            link(dve.tensor_tensor_scan(R2, cst("ones")[0:6, :], R1, 0.0, MUL, ADD))
            TS(R3, R2, -1.0, None, MUL).then_inc(sem(m + "_frow"), 1)
            taps = v3(prm(f"dnconv{l}"), 9)

            def normed(k):
                j = M2_SUM_ORDER[k]
                dve.wait_ge(sem(m + "_rs"), k + 1)
                key = (m, "in", j)
                for c in M2_SUM_HALVES[j]:
                    u = 2 * j + c
                    rs = m2.RS[:, k % 2, c * 256:(c + 1) * 256]
                    if j < 3:
                        ins = STT(m2.QKN[:, u, :], m2.Y[:, u, :], 0.125 if u < 3 else 1.0, rs, MUL, MUL)
                    else:
                        gain = st_gain[:, 2 + l:3 + l] if u < 12 else prm(f"fxk{l}")
                        ins = STT(m2.FQK[:, u - 9, :], bank(key)[:, c * 256:(c + 1) * 256], gain, rs, MUL, MUL)
                n = mark(ins)
                after(n)
                dve.sem_inc(sem(m + "_nu"), 1)
                if j >= 3:
                    dve.sem_inc(free[uses[key][0]], 1)

            for j in list(range(7)) + [8, 9]:
                if j < 5:
                    key = (m, "in", j)
                    dve.wait_ge(sem(m + "_c0"), j + 1)
                    us = [u for u in (2 * j, 2 * j + 1) if u < 9]
                    last = {}
                    for s in (1, 2, 3):
                        for u in us:
                            if s > 1:
                                after(last[u])
                            o = (u % 2) * 256
                            ins = STT(m2.Y[:, u, s:256], bank(key)[:, o:o + 256 - s], taps[:, u, 3 - s:4 - s], m2.Y[:, u, s:256], MUL, ADD)
                            if s < 3 or u != us[-1]:
                                last[u] = mark(ins)
                    ins.then_inc(sem(m + "_c1"), 1)
                    if j < 4:
                        dve.wait_ge(sem(m + "_c1"), j + 1)
                        dve.sem_inc(free[uses[key][0]], 1)
                if j in M2_SUMS:
                    normed(M2_SUM_ORDER.index(M2_SUMS[j]))
            dve.sem_inc(sem(m + "_qk"), 1)
            dve.wait_ge(sem(m + "_z"), 1)
            zg = m2.ZG.rearrange("p t (h v) -> p (t h) v", v=64)
            link(TT(zg, zg, bc(prm(f"onorm{l}"), 1, 12), MUL))
            key = (m, "pz")
            await_full(dve, key)
            ps = prm(f"pscale{l}")
            for c in range(2):
                ins = TS(OT[:, 6 + c, :], bank(key)[:, c * 256:(c + 1) * 256], ps[:, c:c + 1], None, MUL)
            release(ins, key)
            await_free_of(dve, (m, "rowT"))
            link(TT(st_beg, st_tm[:, :, 2, :], st_tm[:, :, 0, :], MUL))
            for j in range(2):
                await_free_of(dve, (m, "gb", j))
            dve.memset(m2.S[:, 0], 0.0)
            TT(m2.QD, m2.QKN[:, 0:3, :], m2.EGB, MUL).then_inc(sem(m + "_qd"), 1)
            dve.wait_ge(sem(m + "_qd"), 1)
            for j in range(2):
                key = (m, "bb", j)
                w = 2 - j
                await_full(dve, key)
                release(TT(m2.KB[:, 2 * j:2 * j + w, :], m2.QKN[:, 3 + 2 * j:3 + 2 * j + w, :],
                           bank(key)[:, 0:256 * w].rearrange("p (a b) -> p a b", a=w), MUL), key)
            h3 = lambda ap: ap.rearrange("p (h v) -> p h v", h=6)
            for t in range(NT):
                key = (m, "kT", t)
                await_full(dve, key)
                TT(h3(m2.KBG[:, t, :]), h3(bank(key)[:, 0:384]), bc(st_beg[:, t, :], 2, 64), MUL)
                release(TT(h3(m2.KDEC[:, t, :]), h3(bank(key)[:, 0:384]), bc(st_tm[:, t, 1, :], 2, 64), MUL), key)
            for t in range(NT):
                key = (m, "vT", t)
                await_full(dve, key)
                release(TT(h3(m2.VB[:, t, :]), h3(bank(key)[:, 0:384]), bc(st_tm[:, t, 2, :], 2, 64), MUL), key)
            for name, dst in (("kk", m2.AT), ("qk", m2.ATQ)):
                for q in range(3):
                    key = (m, name, q)
                    await_full(dve, key)
                    await_free_of(dve, (m, "dec", q))
                    release(TT(dst[:, 4 * q:4 * q + 4, :], bank4(key), m2.DEC[:, 4 * q:4 * q + 4, :], MUL), key)
            dve.wait_ge(sem(m + "_of"), 1)
            TT(m2.UI, bc(ident, 1, 12), m2.OF, SUB).then_inc(sem(m + "_ui"), 1)
            for q in range(3):
                key = (m, "M", 0, q)
                await_full(dve, key)
                release(TT(m2.DI[:, 4 * q:4 * q + 4, :], bc(ident, 1, 4), bank4(key), SUB), key)
            for s in range(1, GD_STEPS + 1):
                for q in range(3):
                    for name, dst in (("X", m2.DI), ("Y", m2.UI)):
                        if name == "X" and s == GD_STEPS:
                            continue
                        key = (m, name, s, q)
                        await_full(dve, key)
                        d = dst[:, 4 * q:4 * q + 4, :]
                        release(TT(d, d, bank4(key), SUB), key)
            for t in range(NT):
                key = (m, "w", t)
                await_full(dve, key)
                release(dve.tensor_copy(m2.WT[:, :, t * P:(t + 1) * P], bank4(key, 3)), key)
            for n in range(NCH):
                t, p0 = n // 2, 64 * (n % 2)
                rp = slice(p0, p0 + 64)
                if n:
                    key = (m, "vp", n)
                    await_full(dve, key)
                    await_free_of(dve, (m, "u", t))
                    release(TT(m2.UU[rp, t, :], m2.UU[rp, t, :], bank(key)[rp, 0:384], SUB), key)
                if n < NCH - 1:
                    key = (m, "kv", n)
                    await_full(dve, key)
                    S1, S0 = m2.S[:, (n + 1) % 2], m2.S[:, n % 2]
                    e = n * CH + CH - 1
                    TT(S1, S0, m2.EGB[:, :, e:e + 1].broadcast_to([P, 3, P]), MUL)
                    link(TT(m2.SN, bank4(key, 3), bc(blk64, 1, 3), MUL))
                    release(TT(S1, S1, m2.SN, ADD), key)
                    await_free_of(dve, key)
            for t in range(NT):
                key = (m, "o", t)
                dve.wait_ge(sem(m + "_osq"), t + 1)
                dve.tensor_reduce(st_o[:, t * 8:t * 8 + 6], h3(m2.SQ[:, t, 0:384]), AX.X, ADD).then_inc(sem(m + "_oss"), 1)
                dve.wait_ge(sem(m + "_ors"), t + 1)
                dst = HN[:, t, 0:384]
                link(TT(h3(dst), h3(bank(key)[:, 0:384]), bc(st_or[:, t * 8:t * 8 + 6], 2, 64), MUL))
                link(TT(dst, dst, m2.ZG[:, t, :], MUL))
                dve.sem_inc(free[uses[key][0]], 1)
            attn(m + "f", 6, 1, 1, m2.SM, m2.EX, None, lambda g: cst("cmask"))
            attn_out(m + "f", 6, 64, 384)
            out_T(m, 3)
            resid(m)

        def router():
            key = ("router", "logits")
            await_full(dve, key)
            LG, EX_, PB, MASK = mo.LG, mo.EX, mo.PB, mo.MASK
            t2 = lambda ap: ap.rearrange("p (t e) -> p t e", t=2)
            release(dve.tensor_copy(LG, bank(key)[:, 0:16]), key)
            await_free_of(dve, key)
            dve.tensor_reduce(st_mx[:, 0:2], t2(LG), AX.X, MAX, negate=True).then_inc(sem("r_mx"), 1)
            dve.wait_ge(sem("r_e"), 1)
            link(dve.reciprocal(st_ri[:, 0:2], st_sum[:, 0:2]))
            link(TT(t2(PB), t2(EX_), bc(st_ri[:, 0:2], 2, 8), MUL))
            mine = bc(t2(PB), 3, 8)
            other = bc(t2(PB), 2, 8)
            four = lambda ap: ap.rearrange("p (t e f) -> p t e f", t=2, e=8)
            GTR, EQ = four(mo.GTR), four(mo.EQ)
            TT(GTR, other, mine, ALU.is_gt)
            link(TT(EQ, other, mine, ALU.is_equal))
            link(TT(EQ, EQ, bc(cst("before").rearrange("p (e f) -> p e f", e=8), 1, 2), MUL))
            link(TT(GTR, GTR, EQ, ADD))
            link(dve.tensor_reduce(t2(MASK), GTR, AX.X, ADD))
            TS(MASK, MASK, 1.5, None, ALU.is_lt).then_inc(sem("chosen"), 1)
            dve.wait_ge(sem("chosen"), 1)
            link(TT(PB, PB, MASK, MUL))
            link(dve.tensor_reduce(st_sum[:, 2:4], t2(PB), AX.X, ADD))
            link(dve.reciprocal(st_ri[:, 2:4], st_sum[:, 2:4]))
            link(TT(t2(mo.GATE), t2(PB), bc(st_ri[:, 2:4], 2, 8), MUL))
            key = ("router", "place")
            await_full(dve, key)
            link(TS(mo.EX, MASK, -4.0 * S, 4.0 * S, MUL, ADD))
            TT(mo.POS, mo.EX, bank(key)[:, 0:16], ADD)
            link(dve.tensor_reduce(mo.MOST, bank(key)[:, 16:24], AX.X, MAX))
            release(TS(MORE[0:1, :], mo.MOST[0:1, :], P + 0.5, None, ALU.is_gt), key)
            await_free_of(dve, key)
            dve.sem_inc(sem("more"), 1)

        def moe(p):
            name = moe_name[p]
            w0, k0 = BASE["moe"] + p * MOE_TILES, ffn_k0[name]
            if p:
                link(TS(mo.POS, mo.POS, -float(P), None, ADD))
            t3 = lambda ap: ap.rearrange("p t e s -> p (t e) s")
            link(TT(t3(mo.SEL), bc(cst("iota"), 1, 16), bc(mo.POS, 2, P), ALU.is_equal))
            TT(t3(mo.GSEL), t3(mo.SEL), bc(mo.GATE, 2, P), MUL).then_inc(sem("moe_sel"), 1)
            g = prm("norm")
            for c in range(KC):
                key = ("moe", p, "gx", 2 * c + 1)
                await_full(dve, key)
                release(TS(mo.XG[:, c, 4:8, :].rearrange("p e s -> p (e s)"), bank(key)[:, :],
                           g[:, 7 * KC + c:7 * KC + c + 1], None, MUL), key)

            def group(gs, i, first=False):
                hb, b = gs % 2, 6 + gs % 2
                dve.wait_ge(sem("moe_silu"), MOE_GROUPS * p + gs + 1 + G_EXP * i)
                TT(mo.GH[:, hb, :], mo.SG[:, hb, :], PS[b][:, 256:512], MUL).then_inc(free[b], 1)

            def expert_out(e, i, tile):
                dve.wait_ge(w_used, tile + 1 + 3 * G_EXP * i)
                if p or e or not isinstance(i, int):
                    dve.wait_ge(sem("moe_scattered"), (N_EXP - 1) * p + e + i)
                gs = mo.SELT[:, e, :] if isinstance(i, int) else mo.SELT[:, bass.ds(i + e, 1), :].rearrange("p e t -> p (e t)")
                dve.tensor_copy(mo.GS, gs)
                dve.tensor_copy(mo.YE[:, 512:1024], PS[5][:, :]).then_inc(free[5], 1)

            for j in range(4):
                await_free_of(dve, ("moe", p, "selT", j))
            moe_loop(dve, group, expert_out, w0)
            for b in range(4):
                key = ("y", name, b)
                await_full(dve, key)
                release(dve.tensor_copy(X[:, b // 2, (b % 2) * 512:(b % 2 + 1) * 512], PS[b][:, :]), key)

        def ffn(name, groups, kind):
            w0, k0 = BASE[name], ffn_k0[name]
            body = 2
            f = lambda ap: ap.rearrange("p c t -> p (c t)")
            sv, sc = sem(name + "_v"), sem(name + "_a")

            def group(gs, i, first=False):
                hb, b = gs % 2, 4 + 2 * (gs % 2)
                tile = w0 + (1 if first else 3 * gs)
                dt, dk = 3 * body * i, (body // 2) * i
                if kind != "conv":
                    dve.wait_ge(free[b], k0[b] + gs // 2 + 1 + dk)
                    sg = ff.SG[:, hb]
                    dve.wait_ge(w_used, tile + 1 + dt)
                    TT(f(ff.GH[:, hb]), f(sg), PS[b + 1][:, :], MUL).then_inc(free[b + 1], 1)
                    return
                off = PRM["conv0" if name == "ffn0" else "conv1"][0]
                n0 = 7 * gs + 7 * body * i
                dve.wait_ge(sc, 2 * gs + 1 + 2 * body * i)
                for s in (1, 2):
                    for half, Y in enumerate((ff.YG, ff.YV)):
                        if s == 2:
                            dve.wait_ge(sv, n0 + 2 + 2 * half)
                        for c in range(2):
                            col = off + 4 * (22 * half + 2 * gs + c) + 2 - s
                            w = PR[:, col:col + 1] if isinstance(i, int) else PR[:, bass.ds(8 * body * i + col, 1)]
                            ins = STT(Y[:, hb, c, s:256], PS[b + half][:, c * 256:c * 256 + 256 - s], w, Y[:, hb, c, s:256], MUL, ADD)
                            if s == 2 and c == 1:
                                ins.then_inc(free[b + half], 1)
                            else:
                                ins.then_inc(sv, 1)
                dve.wait_ge(sv, n0 + 6)
                dve.wait_ge(free[b + 1], k0[b + 1] + gs // 2 + 1 + dk)
                dve.wait_ge(sc, 2 * gs + 2 + 2 * body * i)
                TT(f(ff.GH[:, hb]), f(ff.SG[:, hb]), f(ff.YV[:, hb]), MUL).then_inc(sv, 1)

            group(0, 0, True)
            group(1, 0)
            rounds = (groups - 2) // body
            with dve.Fori(0, rounds) as i:
                for u in range(body):
                    group(2 + u, i)
            for g in range(2 + rounds * body, groups):
                group(g, 0)
            resid(name)

        prep()
        for st in order:
            if st[0] == "norm":
                norm(st[1])
            elif st[0] == "even":
                even()
            elif st[0] == "odd":
                odd()
            elif st[0] == "m2":
                mixer2(*st[1:])
            elif st[0] == "router":
                router()
            elif st[0] == "moe":
                moe(0)
                with dve.If(more_tokens(dve) > 0):
                    moe(1)
            else:
                ffn(*st[1:])

    block.__exit__(None, None, None)
    return n_tiles


def pack_params(v):
    prm = np.zeros((P, N_PRM), np.float32)

    def put(name, a):
        o, w = PRM[name]
        a = np.asarray(a).reshape(-1, w)
        prm[:a.shape[0], o:o + w] = a

    def cols(a, n):
        return np.asarray(a).reshape(n, P).transpose(1, 0)

    def rows(a):
        a = np.asarray(a).reshape(1, -1)
        return np.broadcast_to(a, (P, a.shape[1]))

    def column(a, reps):
        return np.concatenate([np.asarray(a).reshape(-1)] * reps).reshape(P, 1)

    norms = [v["norm_mix"][0], v["norm_ffn"][0], v["norm_mix"][1], v["norm_ffn"][1],
             v["norm1_2"][0], v["norm2_2"][0], v["norm1_2"][1], v["norm2_2"][1]]
    put("norm", np.concatenate([cols(g, KC) for g in norms], 1))
    put("ba", cols(v["ev_b_a"][0], 2))
    put("wa2", v["ev_w_a2"][0])
    put("gla_gain", rows(v["ev_gla_gain"][0]))
    put("dq", column(v["ev_dq_gain"][0], 2))
    put("dk", column(v["ev_dk_gain"][0], 2))
    put("lq", rows(np.concatenate([v["ev_lq1"][0], v["ev_lq2"][0]])))
    put("lk", rows(np.concatenate([v["ev_lk1"][0], v["ev_lk2"][0]])))
    put("diff_gain", rows(v["ev_diff_gain"][0]))
    put("odq", column(v["od_q_gain"][0], 1))
    put("odk", column(v["od_k_gain"][0], 1))
    for i in range(2):
        taps = np.concatenate([v["ffn_conv_w"][i][:, 0, :], v["ffn_conv_b"][i][None, :]], 0)
        put(f"conv{i}", taps.reshape(4, 44, P).transpose(2, 1, 0).reshape(P, 176))
        put(f"dnconv{i}", v["dn_conv_2"][i].reshape(4, 9, P).transpose(2, 1, 0).reshape(P, 36))
        put(f"alog{i}", v["dn_a_log_2"][i].reshape(6, 1))
        put(f"dtb{i}", v["dn_dt_bias_2"][i].reshape(6, 1))
        put(f"fb{i}", v["fx_f_bias_2"][i].reshape(6, 1))
        put(f"onorm{i}", rows(v["dn_onorm_2"][i]))
        put(f"fxq{i}", column(v["fx_qnorm_2"][i], 2))
        put(f"fxk{i}", column(v["fx_knorm_2"][i], 2))
        put(f"poolw{i}", v["pool_w_2"][i].reshape(2, P, 64).transpose(1, 0, 2).reshape(P, 128))
        put(f"pscale{i}", cols(v["pool_scale_2"][i], 2))
    put("router", v["router_2"][0].reshape(KC, P, N_EXP).transpose(1, 0, 2).reshape(P, KC * N_EXP))
    return prm


def pack_weights(v):
    w = np.zeros((N_TILES, P, KC * TW), np.float32)

    def put_in(t, mat, cols, at=0):
        a = mat[:, cols]
        w[t].reshape(P, KC, TW)[:, :, at:at + a.shape[1]] = a.reshape(KC, P, a.shape[1]).transpose(1, 0, 2)

    def put_out(t, mat, j):
        w[t].reshape(P, 2, D)[:] = mat[j * TW:(j + 1) * TW].reshape(2, P, D).transpose(1, 0, 2)

    def span(o, n=TW):
        return slice(o, o + n)

    m, b = v["ev_w_in"][0], BASE["ev_in"]
    put_in(b, m, span(1536, 16))
    for j, o in enumerate([0, 256, 512, 768, 1024, 1280, 1552, 1808, 2064, 2320, 2576, 2832]):
        put_in(b + 1 + j, m, span(o))
    for j in range(EV_OUT):
        put_out(BASE["ev_out"] + j, v["ev_w_out"][0], j)
    for j in range(OD_IN):
        put_in(BASE["od_in"] + j, v["od_w_in"][0], span(j * TW))
    for j in range(OD_OUT):
        put_out(BASE["od_out"] + j, v["od_w_out"][0], j)
    for l in range(2):
        m, b = v["w_in_2"][l], BASE[f"m{l}_in"]
        units = [span(o, P) for o in list(range(0, 1152, P)) + list(range(1548, 2316, P))]
        put_in(b, m, units[14])
        put_in(b, m, span(1536, 12), 128)
        put_in(b, m, span(2700, 6), 140)
        for j in range(7):
            put_in(b + 1 + j, m, units[2 * j])
            put_in(b + 1 + j, m, units[2 * j + 1], P)
        put_in(b + 8, m, span(1152))
        put_in(b + 9, m, span(1408, P))
        put_in(b + 9, m, span(2316, P), P)
        put_in(b + 10, m, span(2444))
        put_in(b + 11, m, span(2706))
        for j in range(M2_OUT):
            put_out(BASE[f"m{l}_out"] + j, v["w_out_2"][l], j)

    def ffn(base, groups, gate, up, down):
        for g in range(groups):
            t = base + (0 if g == 0 else 3 * g - 1)
            put_in(t, *gate(g))
            put_in(t + 1, *up(g))
            put_out(base + (3 * g + 4 if g < groups - 1 else 3 * groups - 1), *down(g))

    for l in range(2):
        u, d = v["ffn_w_up"][l], v["ffn_w_down"][l]
        ffn(BASE[f"ffn{l}"], G_FFN, lambda g: (u, span(g * TW)), lambda g: (u, span(D_FF + g * TW)), lambda g: (d, g))
    ffn(BASE["ffn2"], G_FFN, lambda g: (v["ffn_gate_2"][0], span(g * TW)), lambda g: (v["ffn_up_2"][0], span(g * TW)),
        lambda g: (v["ffn_down_2"][0], g))
    ffn(BASE["moe"], G_EXP * N_EXP, lambda g: (v["moe_gate_2"][0, g // G_EXP], span(g % G_EXP * TW)),
        lambda g: (v["moe_up_2"][0, g // G_EXP], span(g % G_EXP * TW)), lambda g: (v["moe_down_2"][0, g // G_EXP], g % G_EXP))
    return w


STOP = None


def kernel(**inputs):
    import concourse.bacc as _bacc
    from concourse import mybir as _mybir
    from concourse.bass_utils import run_bass_kernel_spmd as _run
    v = {k: np.asarray(a) for k, a in inputs.items()}
    cst, sel = constants()
    arrays = {"weights": pack_weights(v), "x": v["x"], "params": pack_params(v), "consts": cst, "selectors": sel}
    nc = _bacc.Bacc("TRN2", target_bir_lowering=False, num_devices=1)
    f32 = _mybir.dt.float32
    aps = [nc.dram_tensor(f"in_{k}", a.shape, f32, kind="ExternalInput").ap() for k, a in arrays.items()]
    out = nc.dram_tensor("out", (1, S, D), f32, kind="ExternalOutput").ap()
    build(nc, aps[0], aps[1], aps[2], aps[3], aps[4], out, STOP)
    r = _run(nc, [{f"in_{k}": a for k, a in arrays.items()}], core_ids=[0])
    return r.results[0]["out"]
```

```python
import numpy as np

P = 128
S = 256
NT = S // P
D = 1024
KC = D // P
TW = 256
RING = 6
SPLIT = 3
EPS = 1e-6
NEG = -1e30
D_FF, D_FFE, N_EXP = 2816, 1536, 8
G_FFN = D_FF // TW
G_EXP = D_FFE // TW
PASSES = 2
CH = 64
NCH = S // CH
DN_H, FX_H = 6, 6
LAMBDA_INIT = 0.8 - 0.6
POOL_WINDOWS = (2, 4, 8, 16)

M2_SUMS = {1: 7, 3: 0, 4: 1, 5: 2, 6: 4, 8: 5, 9: 6}
M2_SUM_ORDER = [7, 0, 1, 2, 4, 5, 6]
M2_SUM_HALVES = {7: (0,), 0: (0, 1), 1: (0, 1), 2: (0, 1), 4: (1,), 5: (0, 1), 6: (0, 1)}

EV_IN, EV_OUT = 13, 4
OD_IN, OD_OUT = 18, 2
M2_IN, M2_OUT = 12, 4
SIZES = [("ev_in", EV_IN), ("ev_out", EV_OUT), ("ffn0", 3 * G_FFN), ("od_in", OD_IN), ("od_out", OD_OUT),
         ("ffn1", 3 * G_FFN), ("m0_in", M2_IN), ("m0_out", M2_OUT), ("ffn2", 3 * G_FFN), ("m1_in", M2_IN),
         ("m1_out", M2_OUT), ("moe", 3 * G_EXP * N_EXP)]
BASE = {}
N_TILES = 0
for _n, _k in SIZES:
    BASE[_n] = N_TILES
    N_TILES += _k

PRM_W = [("norm", 8 * KC), ("ba", 2), ("wa2", 256), ("gla_gain", 128), ("dq", 1), ("dk", 1), ("lq", 128), ("lk", 128),
         ("diff_gain", 128), ("odq", 1), ("odk", 1), ("conv0", 44 * 4), ("conv1", 44 * 4), ("router", KC * N_EXP)]
for _l in (0, 1):
    PRM_W += [(f"dnconv{_l}", 9 * 4), (f"alog{_l}", 1), (f"dtb{_l}", 1), (f"fb{_l}", 1), (f"onorm{_l}", 64),
              (f"fxq{_l}", 1), (f"fxk{_l}", 1), (f"poolw{_l}", 128), (f"pscale{_l}", 2)]
PRM = {}
N_PRM = 0
for _n, _k in PRM_W:
    PRM[_n] = (N_PRM, _k)
    N_PRM += _k

CST_W = [("ident", 128), ("blk64", 128), ("ones", 256), ("eps", 1), ("one", 1), ("mhalf", 1), ("cmask", 384), ("dmask", 3 * 384),
         ("glamask", 128), ("gdneg", 128), ("offd", 6 * 128), ("reset", 512), ("pool", 2 * 4 * 256), ("before", 64),
         ("earlier", 128), ("iota", 128)]
CST = {}
N_CST = 0
for _n, _k in CST_W:
    CST[_n] = (N_CST, _k)
    N_CST += _k
N_FIRST = CST["cmask"][0]
SEL_W = [("sel6", 6 * 256), ("selhp", 3 * 128)]
SEL = {}
N_SEL = 0
for _n, _k in SEL_W:
    SEL[_n] = (N_SEL, _k)
    N_SEL += _k


def constants():
    c = np.zeros((P, N_CST), np.float32)

    def put(name, a):
        o, w = CST[name]
        c[:, o:o + w] = np.asarray(a, np.float32).reshape(P, w)

    p = np.arange(P)[:, None]
    f = np.arange(P)[None, :]
    put("ident", p == f)
    put("blk64", p // 64 == f // 64)
    put("ones", np.ones((P, 256)))
    put("eps", np.full((P, 1), EPS))
    put("one", np.ones((P, 1)))
    put("mhalf", np.full((P, 1), -0.5))
    causal = np.where(f <= p, 0.0, NEG)
    zero = np.zeros((P, P))
    put("cmask", np.concatenate([causal, zero, causal], 1))
    near = (p - f)
    dm = []
    for dil in (1, 4, 16):
        diag = np.where((near >= 0) & (near % dil == 0), 0.0, NEG)
        far = np.where(((near + P) % dil == 0) & (near + P <= 128 * dil), 0.0, NEG)
        dm.append(np.concatenate([diag, far, diag], 1))
    put("dmask", np.stack(dm, 1))
    same = p // CH == f // CH
    put("glamask", same & (f >= p))
    put("gdneg", np.where(same & (f >= p), 0.0, NEG))
    off = []
    for b in (1, 2, 4, 8, 16, 32):
        off.append((f // (2 * b) == p // (2 * b)) & (f % (2 * b) >= b) & (p % (2 * b) < b))
    put("offd", np.stack(off, 1))
    put("reset", np.broadcast_to(np.arange(512) % CH != 0, (P, 512)))
    pool = np.zeros((P, 2, 4, 256))
    for g, w in enumerate(POOL_WINDOWS):
        for tt in range(2):
            src = tt * P + np.arange(P)[:, None]
            dst = np.arange(256)[None, :]
            pool[:, tt, g] = ((dst - src >= 0) & (dst - src < w)) / np.minimum(dst + 1, w) - (src == dst)
    put("pool", pool)
    put("before", np.broadcast_to((np.arange(8)[None, :] < np.arange(8)[:, None]).reshape(1, 64), (P, 64)))
    put("earlier", p < f)
    put("iota", np.broadcast_to(f, (P, P)))
    s = np.zeros((8, N_SEL), np.float32)
    o = SEL["sel6"][0]
    for h in range(6):
        s[h, o + h * 256:o + (h + 1) * 256] = 1
    o = SEL["selhp"][0]
    for h in range(6):
        s[h, o + (h // 2) * 128 + (h % 2) * 64:o + (h // 2) * 128 + (h % 2) * 64 + 64] = 1
    return c, s


def build(nc, w_dram, x_dram, prm_dram, cst_dram, sel_dram, out_dram, stop=None):
    import concourse.bass as bass
    from concourse import mybir
    F32 = mybir.dt.float32
    F32R = mybir.dt.float32r
    ALU = mybir.AluOpType
    ACT = mybir.ActivationFunctionType
    AX = mybir.AxisListType
    ADD, SUB, MUL, MAX, MIN = ALU.add, ALU.subtract, ALU.mult, ALU.max, ALU.min

    X = nc.alloc_sbuf_tensor("X", [P, NT, D], F32)
    HN = nc.alloc_sbuf_tensor("HN", [P, NT, D], F32)
    HT = nc.alloc_sbuf_tensor("HT", [P, KC, S], F32)
    ht_at = nc.sbuf_base - 4 * KC * S
    OT = nc.alloc_sbuf_tensor("OT", [P, KC, S], F32)
    ot_at = nc.sbuf_base - 4 * KC * S
    W = nc.alloc_sbuf_tensor("W", [P, RING, KC * TW], F32)
    PR = nc.alloc_sbuf_tensor("PR", [P, N_PRM], F32)
    CS = nc.alloc_sbuf_tensor("CS", [P, N_CST], F32)
    SL = nc.alloc_sbuf_tensor("SL", [8, N_SEL], F32)
    ST_ = nc.alloc_sbuf_tensor("STAT", [P, 640], F32)
    ARENA_N = 21632
    AR = nc.alloc_sbuf_tensor("ARENA", [P, ARENA_N], F32)
    arena_at = nc.sbuf_base - 4 * ARENA_N
    HTH = nc.alloc_sbuf_tensor_at("HTH", [P, KC, S], F32R, offset=ht_at)
    HTL = nc.alloc_sbuf_tensor_at("HTL", [P, KC, S], F32R, offset=ot_at)
    ff_n = 4 * 2 * 512
    gh_n, wh_n = 2 * 512, SPLIT * KC * TW
    assert ff_n + 2 * gh_n + 2 * wh_n <= ARENA_N
    GHH = nc.alloc_sbuf_tensor_at("GHH", [P, 2, 2, S], F32R, offset=arena_at + 4 * ff_n)
    GHL = nc.alloc_sbuf_tensor_at("GHL", [P, 2, 2, S], F32R, offset=arena_at + 4 * (ff_n + gh_n))
    WH = nc.alloc_sbuf_tensor_at("WH", [P, SPLIT, KC * TW], F32R, offset=arena_at + 4 * (ff_n + 2 * gh_n))
    WL = nc.alloc_sbuf_tensor_at("WL", [P, SPLIT, KC * TW], F32R, offset=arena_at + 4 * (ff_n + 2 * gh_n + wh_n))
    HNH = nc.alloc_sbuf_tensor_at("HNH", [P, NT, D], F32R, offset=ht_at)
    HNL = nc.alloc_sbuf_tensor_at("HNL", [P, NT, D], F32R, offset=ot_at)
    DH = nc.alloc_sbuf_tensor_at("DH", [P, 2, D], F32R, offset=ht_at)
    DL = nc.alloc_sbuf_tensor_at("DL", [P, 2, D], F32R, offset=ot_at)
    sel_n, gr_n = NT * N_EXP * P, 2 * 256
    SELR = nc.alloc_sbuf_tensor_at("SELR", [P, NT, N_EXP, P], F32R, offset=arena_at)
    GRH = nc.alloc_sbuf_tensor_at("GRH", [P, 2, 256], F32R, offset=arena_at + 4 * sel_n)
    GRL = nc.alloc_sbuf_tensor_at("GRL", [P, 2, 256], F32R, offset=arena_at + 4 * (sel_n + gr_n))
    PS = [nc.alloc_psum_tensor(f"PS{b}", [P, 512], F32) for b in range(8)]

    def prm(name):
        o, w = PRM[name]
        return PR[:, o:o + w]

    def cst(name):
        o, w = CST[name]
        return CS[:, o:o + w]

    def sel(name):
        o, w = SEL[name]
        return SL[:, o:o + w]

    class Carve:
        def __init__(self):
            self.at = 0

        def __call__(self, n):
            self.at += n
            assert self.at <= ARENA_N, self.at
            return AR[:, self.at - n:self.at]

    class Stats:
        at = 0

        @classmethod
        def get(cls, n):
            cls.at += n
            assert cls.at <= 640, cls.at
            return ST_[:, cls.at - n:cls.at]

    Stats.at = 0
    ident, ones, blk64 = cst("ident"), cst("ones")[:, 0:P], cst("blk64")
    eps, one, mhalf = cst("eps"), cst("one"), cst("mhalf")

    sems = {}

    def sem(name):
        if name not in sems:
            sems[name] = nc.alloc_semaphore(name)
        return sems[name]

    w_full = [sem(f"w_full{i}") for i in range(RING)]
    w_used = sem("w_used")
    full = [sem(f"bank_full{b}") for b in range(8)]
    free = [sem(f"bank_free{b}") for b in range(8)]
    s_in, s_const, s_late, s_out = sem("x_in"), sem("const_in"), sem("late_const_in"), sem("out_done")

    uses = {}
    n_use = [0] * 8
    n_full = [0] * 8

    def plan(key, bank, tile=None):
        if tile is None:
            n_full[bank] += 1
            uses[key] = (bank, n_use[bank], full[bank], n_full[bank])
        else:
            uses[key] = (bank, n_use[bank], w_used, tile + 1)
        n_use[bank] += 1

    class Rot:
        def __init__(self, banks):
            self.banks, self.k = banks, 0

        def __call__(self, key, tile=None):
            plan(key, self.banks[self.k % len(self.banks)], tile)
            self.k += 1

    def bank(key):
        return PS[uses[key][0]]

    def await_full(eng, key):
        eng.wait_ge(uses[key][2], uses[key][3])

    def release(ins, key):
        ins.then_inc(free[uses[key][0]], 1)

    def await_free_of(eng, key):
        eng.wait_ge(free[uses[key][0]], uses[key][1] + 1)

    def claim(pe, key):
        b, k = uses[key][:2]
        if k:
            pe.wait_ge(free[b], k)

    def plan_norm(n):
        for b in range(4):
            plan(("norm", n, b), 4 + b)

    def plan_y(n, tile):
        for b in range(4):
            plan(("y", n, b), b, tile if b == 3 else None)

    def plan_attn_step(i, name, heads, groups, combine, rot, parts="st"):
        if i < heads and "s" in parts:
            for c in range(combine):
                for g in range(groups):
                    rot((name, "s", i * combine + c, g))
        if 1 <= i <= heads and "t" in parts:
            for g in range(groups):
                rot((name, "t", i - 1, g))

    def plan_attn(name, heads, groups, combine, rot):
        for i in range(heads + 2):
            plan_attn_step(i, name, heads, groups, combine, rot)

    def plan_out_t(name, chunks, rot):
        for j in range((chunks + 1) // 2):
            rot((name, "oT", j))

    def plan_even():
        t0 = BASE["ev_in"]
        rot = Rot([0, 1, 2, 3, 4, 5, 6, 7])
        rot(("ev", "ar"), t0)
        rot(("ev", "aq"), t0 + 1)
        rot(("ev", "ak"), t0 + 2)
        rot(("ev", "la"))
        for j in range(2):
            rot(("ev", "av", j), t0 + 3 + j)
        for j in range(2):
            rot(("ev", "ag", j), t0 + 5 + j)
        for j in range(4):
            rot(("ev", "bqk", j), t0 + 7 + j)
            if j:
                rot(("ev", "ss", j - 1))
            if j == 0:
                rot(("ev", "kwT"))
                for r in range(2):
                    rot(("ev", "att", r))
            if j == 1:
                for n in range(NCH - 1):
                    rot(("ev", "kv", n))
            if j == 2:
                for t in range(NT):
                    rot(("ev", "o", t))
        plan_attn_step(0, "evd", 4, 1, 2, rot)
        rot(("ev", "bv", 0), t0 + 11)
        rot(("ev", "ss", 3))
        plan_attn_step(1, "evd", 4, 1, 2, rot, "s")
        rot(("ev", "bv", 1), t0 + 12)
        for n in range(NT):
            plan(("evd", "o", n), 4 + n)
        rot = Rot([0, 1, 2, 3, 6, 7])
        for i in range(1, 6):
            if i == 4:
                rot = Rot([6, 7])
                for j in range(2):
                    rot(("ev", "oT", j))
            plan_attn_step(i, "evd", 4, 1, 2, rot, "t" if i == 1 else "st")
        for j in range(2, 4):
            rot(("ev", "oT", j))
        plan_y("ev", BASE["ev_out"] + EV_OUT - 1)

    def plan_odd():
        t0 = BASE["od_in"]
        rot = Rot([0, 1, 2, 3, 4, 5, 6, 7])
        for g in range(3):
            for j in range(4):
                rot(("od", "qk", g, j), t0 + 6 * g + j)
                if j:
                    rot(("od", "ss", g, j - 1))
            rot(("od", "v", g, 0), t0 + 6 * g + 4)
            rot(("od", "ss", g, 3))
            rot(("od", "v", g, 1), t0 + 6 * g + 5)
        for n in range(NT):
            plan(("od", "o", n), n)
        plan_attn("od", 4, 3, 1, Rot([2, 3, 4, 5, 6, 7]))
        plan_out_t("od", 4, Rot([4, 5, 6, 7]))
        plan_y("od", BASE["od_out"] + OD_OUT - 1)

    GD_STEPS = 5
    M2_OT = [(4, 5), (3,), (0, 1), (2,)]
    M2_OUT_CHUNKS = [(6, 7), (4, 5), (2, 3), (0, 1)]
    PAIRS = [(t, h) for r in range(2) for t in range(NT) for h in range(r, 6, 2)]

    def plan_m2(m):
        t0 = BASE[f"{m}_in"]
        rot = Rot([0, 1, 2, 3, 4, 5, 6, 7])
        rot((m, "ab"))
        rot((m, "in", 7), t0)
        for j in range(M2_IN - 1):
            jj = j if j < 7 else j + 1
            rot((m, "in", jj), t0 + 1 + j)
            if jj in M2_SUMS:
                rot((m, "ss", M2_SUMS[jj]))
        rot((m, "py"))
        rot((m, "pz"))
        rot((m, "rowT"))
        for j in range(2):
            rot((m, "gb", j))
        for j in range(2):
            rot((m, "bb", j))
        for t in range(NT):
            rot((m, "kT", t))
        for t in range(NT):
            rot((m, "vT", t))
        for q in range(3):
            rot((m, "dec", q))
        for q in range(3):
            rot((m, "kk", q))
        for q in range(3):
            rot((m, "qk", q))
        fx = (m + "f", FX_H, 1, 1)
        for n in range(NT):
            plan((m + "f", "o", n), 2 + n)
        rot = Rot([0, 1, 4, 5, 6, 7])
        for s in range(GD_STEPS + 1):
            for q in range(3):
                rot((m, "M", s, q))
            plan_attn_step(s, *fx, rot)
            for q in range(3 if s else 0):
                if s < GD_STEPS:
                    rot((m, "X", s, q))
                rot((m, "Y", s, q))
        rot = Rot([6, 7])
        for t in range(NT):
            rot((m, "u", t))
            rot((m, "w", t))
        plan_attn_step(GD_STEPS + 1, *fx, rot)
        for t in range(NT):
            plan((m, "o", t), 4 + t)
        for n in range(NCH):
            if n:
                rot((m, "vp", n))
            if n == 2:
                for j in range(2):
                    rot((m, "oT", j))
            if n < NCH - 1:
                rot((m, "kv", n))
            if n == 0:
                plan_attn_step(GD_STEPS + 2, *fx, rot)
        for j in range(2, 4):
            rot((m, "oT", j))
        plan_y(m, BASE[f"{m}_out"] + M2_OUT - 1)

    ffn_k0 = {}

    def plan_ffn(n, groups):
        ffn_k0[n] = list(n_use)
        for g in range(groups):
            n_use[4 + 2 * (g % 2)] += 1
            n_use[5 + 2 * (g % 2)] += 1
        plan_y(n, BASE[n] + 3 * groups - 1)

    MOE_GROUPS = G_EXP * N_EXP
    MOE_TILES = 3 * MOE_GROUPS
    moe_name = ["moe", "moe_more"]

    def plan_moe(p):
        rot = Rot([4, 5, 6, 7])
        for j in range(16):
            rot(("moe", p, "gx", j))
        for j in range(4):
            rot(("moe", p, "selT", j))
        for b in range(4):
            plan(("y", moe_name[p], b), b)
        ffn_k0[moe_name[p]] = list(n_use)
        for b in (6, 7):
            n_use[b] += MOE_GROUPS // 2
        for b in (4, 5):
            n_use[b] += N_EXP

    order = [("norm", 0), ("even",), ("norm", 1), ("ffn", "ffn0", G_FFN, "conv"),
             ("norm", 2), ("odd",), ("norm", 3), ("ffn", "ffn1", G_FFN, "conv"),
             ("norm", 4), ("m2", "m0", 0), ("norm", 5), ("ffn", "ffn2", G_FFN, "glu"),
             ("norm", 6), ("m2", "m1", 1), ("norm", 7), ("router",), ("moe",)]
    if stop is not None:
        order = order[:stop]
    for st in order:
        if st[0] == "norm":
            plan_norm(st[1])
        elif st[0] == "even":
            plan_even()
        elif st[0] == "odd":
            plan_odd()
        elif st[0] == "m2":
            plan_m2(st[1])
        elif st[0] == "router":
            plan(("router", "logits"), 4)
            plan(("router", "place"), 5)
        elif st[0] == "moe":
            for p in range(PASSES):
                plan_moe(p)
        else:
            plan_ffn(st[1], st[2])
    n_tiles = N_TILES
    last_stage = order[-1]
    if stop is not None and last_stage[0] != "moe":
        n_tiles = {"even": BASE["ffn0"], "odd": BASE["ffn1"]}.get(last_stage[0])
        if n_tiles is None:
            names = [n for n, _ in SIZES]
            if last_stage[0] == "m2":
                n_tiles = BASE[last_stage[1] + "_out"] + M2_OUT
            elif last_stage[0] == "ffn":
                k = names.index(last_stage[1])
                n_tiles = BASE[names[k]] + SIZES[k][1]

    def v3(ap, a):
        return ap.rearrange("p (a b) -> p a b", a=a)

    class NS:
        pass

    ev = NS()
    a = Carve()
    ev.arT = a(256)
    ev.T1, ev.MN, ev.B, ev.EB, ev.ENB, ev.EW, ev.QD, ev.KD, ev.KW = [a(512) for _ in range(9)]
    ev.KWT = v3(a(512), 2)
    ev.V = v3(a(1024), 2)
    ev.GG = v3(a(1024), 2)
    ev.ATT = v3(a(1024), 8)
    ev.ST = a(3 * 512).rearrange("p (n c r v) -> p n c r v", n=3, c=2, r=2)
    ev.SQ = v3(a(1024), 2)
    ev.RS = v3(a(1024), 2)
    ev.QK = a(2048).rearrange("p (j c t) -> p j c t", j=4, c=2)
    ev.BV = v3(a(1024), 2)
    ev.SM = a(2 * 384).rearrange("p (u g k) -> p u g k", u=2, g=1)
    EXf = a(4 * 384)
    ev.EX = EXf.rearrange("p (u g k) -> p u g k", u=4, g=1)
    ev.OSQ = v3(EXf[:, 0:1024], 2)
    ev.WC = a(2 * 384).rearrange("p (u g k) -> p u g k", u=2, g=1)
    ev.PT = a(2 * 384).rearrange("p (u g k) -> p u g k", u=2, g=1)
    od = NS()
    a = Carve()
    od.QK = a(24 * 256).rearrange("p (g j c t) -> p g j c t", g=3, j=4, c=2)
    od.V = a(3 * 1024).rearrange("p (g t n) -> p g t n", g=3, t=2)
    od.SQ = v3(a(1024), 2)
    od.RS = v3(a(1024), 2)
    od.SM = a(2 * 1152).rearrange("p (u g k) -> p u g k", u=2, g=3)
    od.EX = a(2 * 1152).rearrange("p (u g k) -> p u g k", u=2, g=3)
    od.PT = a(2 * 1152).rearrange("p (u g k) -> p u g k", u=2, g=3)
    m2 = NS()
    a = Carve()
    Yf = a(9 * 256)
    m2.Y = v3(Yf, 9)
    QKNf = a(6 * 256)
    m2.QKN = v3(QKNf, 6)
    m2.QD = v3(a(768), 3)
    KBf = a(768)
    m2.KB = v3(KBf, 3)
    m2.EGB = v3(a(768), 3)
    KBGf = a(768)
    m2.KBG = v3(KBGf, 2)
    m2.KDEC = v3(a(768), 2)
    m2.VB = v3(a(768), 2)
    m2.FQK = OT[:, 0:6, :]
    m2.FV = v3(a(768), 2)
    m2.ZG = v3(a(768), 2)
    m2.DEC = v3(a(1536), 12)
    m2.OF = m2.DEC
    m2.AT = v3(a(1536), 12)
    m2.ATQ = v3(a(1536), 12)
    DIf, M1f = a(1536), a(1536)
    m2.DI, m2.M1 = v3(DIf, 12), v3(M1f, 12)
    m2.UI = v3(a(1536), 12)
    SQf = a(1024)
    m2.SQ = v3(SQf, 2)
    RSf = a(1024)
    m2.RS = v3(RSf, 2)
    m2.S = RSf[:, 0:768].rearrange("p (b c v) -> p b c v", b=2, c=3)
    m2.SN = v3(a(384), 3)
    m2.XP = v3(KBGf[:, 0:512], 2)
    m2.ROW = HN[0:8, 0, :].rearrange("p (r t) -> p r t", t=256)
    m2.ROW2 = HN[0:8, 1, :].rearrange("p (r t) -> p r t", t=256)
    m2.WT = Yf[:, 0:768].rearrange("p (c t) -> p c t", c=3)
    m2.UU = Yf[:, 768:1536].rearrange("p (t n) -> p t n", t=2)
    m2.PX = M1f[:, 0:512].rearrange("p (c t) -> p c t", c=2)
    m2.SM = QKNf[:, 0:768].rearrange("p (u g k) -> p u g k", u=2, g=1)
    m2.PT = QKNf[:, 768:1536].rearrange("p (u g k) -> p u g k", u=2, g=1)
    m2.EX = KBf.rearrange("p (u g k) -> p u g k", u=2, g=1)
    ff = NS()
    a = Carve()
    ff.GH = a(2 * 512).rearrange("p (b c t) -> p b c t", b=2, c=2)
    ff.SG = a(2 * 512).rearrange("p (b c t) -> p b c t", b=2, c=2)
    ff.YG = a(2 * 512).rearrange("p (b c t) -> p b c t", b=2, c=2)
    ff.YV = a(2 * 512).rearrange("p (b c t) -> p b c t", b=2, c=2)
    mo = NS()
    a = Carve()
    a(sel_n + 2 * gr_n)
    mo.GH = a(2 * 256).rearrange("p (b n) -> p b n", b=2)
    mo.SG = a(2 * 256).rearrange("p (b n) -> p b n", b=2)
    mo.YE = a(D)
    mo.XG = a(KC * N_EXP * P).rearrange("p (k e s) -> p k e s", k=KC, e=N_EXP)
    mo.GSEL = a(NT * N_EXP * P).rearrange("p (t e s) -> p t e s", t=NT, e=N_EXP)
    mo.SELT = a(N_EXP * S).rearrange("p (e t) -> p e t", e=N_EXP)
    mo.GS = a(S)
    mo.LG, mo.EX, mo.PB, mo.MASK, mo.GATE, mo.POS = [a(16) for _ in range(6)]
    mo.GTR, mo.EQ = a(128), a(128)
    mo.MOST = a(1)

    MORE = nc.alloc_sbuf_tensor("MORE", [1, 1], mybir.dt.int32)

    st_ss, st_rs = Stats.get(2), Stats.get(2)
    st_gain = Stats.get(4)
    st_lam, st_nlam = Stats.get(2), Stats.get(1)
    st_lamp, st_dg = Stats.get(128), Stats.get(128)
    st_nea = Stats.get(2)
    st_o, st_or = Stats.get(16), Stats.get(16)
    st_mx, st_sum, st_ri = Stats.get(24), Stats.get(24), Stats.get(24)
    st_rl = Stats.get(2)
    st_tm = Stats.get(36).rearrange("p (t j h) -> p t j h", t=2, j=3)
    st_beg = Stats.get(12).rearrange("p (t h) -> p t h", t=2)

    def bc(ap, axis, n):
        ap = ap.unsqueeze(axis)
        shape = list(ap.shape)
        shape[axis] = n
        return ap.broadcast_to(shape)

    def bank4(key, n=4):
        return bank(key)[:, 0:n * P].rearrange("p (a b) -> p a b", a=n)

    y_names = {"even": "ev", "odd": "od"}
    resid_of = {}
    prev = None
    for st in order:
        if st[0] == "norm":
            resid_of[st[1]] = prev
        elif st[0] != "router":
            prev = y_names.get(st[0], st[1] if len(st) > 1 else st[0])
    last_resid = prev

    FFN_TILES = 3 * G_FFN
    ffn_of_norm = {1: "ffn0", 3: "ffn1", 5: "ffn2"}
    split_base = {n: FFN_TILES * k for k, n in enumerate(("ffn0", "ffn1", "ffn2"))}
    hi_done, lo_done = sem("hi_done"), sem("lo_done")

    def tile_ap(t):
        return W[:, t % RING, :]

    def in_tile(t):
        return tile_ap(t).rearrange("p (k n) -> p k n", k=KC)

    def out_tile(t):
        return tile_ap(t).rearrange("p (c n) -> p c n", c=2)

    def more_tokens(eng):
        eng.wait_ge(sem("more"), 1)
        return eng.value_load(MORE[0:1, 0:1], min_val=0, max_val=1)

    def moe_loop(eng, group, expert_out, w0):
        group(0, 0, True)
        group(1, 0)
        with eng.Fori(0, N_EXP - 1) as i:
            for gs in range(2, 2 + G_EXP):
                group(gs, i)
                if gs == G_EXP:
                    expert_out(0, i, w0 + 3 * (G_EXP - 1) + 4)
        for gs in range(2 + (N_EXP - 1) * G_EXP, MOE_GROUPS):
            group(gs, 0)
        expert_out(N_EXP - 1, 0, w0 + MOE_TILES - 1)

    block = nc.Block()
    block.__enter__()

    @block.sync
    def _(sp):
        sp.dma_start(X[:, :, :], x_dram.rearrange("b (t p) d -> p (b t) d", p=P)).then_inc(s_in, 16)
        sp.dma_start(CS[:, 0:N_FIRST], cst_dram[:, 0:N_FIRST]).then_inc(s_const, 16)
        sp.dma_start(PR[:, :], prm_dram).then_inc(s_const, 16)

        def load(t, slot):
            src = w_dram[t] if isinstance(t, int) else w_dram[bass.ds(t, 1), :, :].rearrange("a p n -> (a p) n")
            sp.dma_start(W[:, slot, :], src).then_inc(w_full[slot], 16)

        for t in range(RING):
            load(t, t)
        rounds = (n_tiles - RING) // RING
        with sp.Fori(0, rounds) as i:
            for u in range(RING):
                sp.wait_ge(w_used, RING * i + (u + 1))
                load(RING * i + (RING + u), u)
        for t in range(RING * (rounds + 1), n_tiles):
            sp.wait_ge(w_used, t - RING + 1)
            load(t, t % RING)
        for b in range(4):
            await_free_of(sp, ("y", last_resid, b))
        if last_resid == "moe":
            with sp.If(more_tokens(sp) > 0):
                n_body = RING
                with sp.Fori(0, MOE_TILES // n_body) as i:
                    for u in range(n_body):
                        sp.wait_ge(w_used, n_body * i + (n_tiles + u - RING + 1))
                        load(n_body * i + (n_tiles - MOE_TILES + u), (n_tiles + u) % RING)
                for b in range(4):
                    await_free_of(sp, ("y", moe_name[1], b))
        sp.dma_start(out_dram.rearrange("b (t p) d -> p (b t) d", p=P), X[:, :, :]).then_inc(s_out, 16)
        sp.wait_ge(s_out, 16)

    @block.gpsimd
    def _(pool):
        offd = v3(cst("offd"), 6)

        def norm(n):
            if n == 0:
                pool.wait_ge(s_const, 32)
            for t in range(NT):
                pool.wait_ge(sem("mean_sq"), NT * n + t + 1)
                if n:
                    pool.wait_ge(sem("hn"), NT * (n - 1) + t + 1)
                pool.tensor_tensor(st_ss[:, t:t + 1], st_ss[:, t:t + 1], eps, ADD).then_inc(sem("mean_eps"), 1)
                pool.wait_ge(sem("mean_eps"), NT * n + t + 1)
                pool.tensor_tensor(st_rs[:, t:t + 1], st_ss[:, t:t + 1], mhalf, ALU.pow).then_inc(sem("rstd"), 1)

        def late_constants():
            pool.wait_ge(w_used, 1)
            pool.dma_start(CS[:, N_FIRST:N_CST], cst_dram[:, N_FIRST:N_CST]).then_inc(s_late, 16)
            pool.dma_start(SL[:, :], sel_dram).then_inc(s_late, 16)
            pool.wait_ge(s_late, 32)

        def mixer2(m):
            for q in range(3):
                await_free_of(pool, (m, "kk", q))
                await_free_of(pool, (m, "qk", q))
            for s in range(GD_STEPS + 1):
                if s:
                    for q in range(3):
                        await_full(pool, (m, "M", s - 1, q))
                if s == 1:
                    pool.wait_ge(sem(m + "_ui"), 1)
                pool.tensor_tensor(m2.OF, m2.AT, bc(offd[:, s, :], 1, 12), MUL).then_inc(sem(m + "_of"), 1)

        for st in order:
            if st[0] == "norm":
                norm(st[1])
                if st[1] == 0:
                    late_constants()
            elif st[0] == "m2":
                mixer2(st[1])

    @block.tensor
    def _(pe):
        mm = pe.matmul

        fences = [0]

        def fence(ins):
            fences[0] += 1
            ins.then_inc(sem("pe_fence"), 1)
            pe.wait_ge(sem("pe_fence"), fences[0])

        def await_tile(t):
            pe.wait_ge(w_full[t % RING], 16 * (t // RING + 1))

        def norm(n):
            for b in range(4):
                claim(pe, ("norm", n, b))
            for t in range(NT):
                pe.wait_ge(sem("hn"), NT * n + t + 1)
                for b in range(4):
                    for k in range(2):
                        c = 2 * b + k
                        ins = pe.transpose(bank(("norm", n, b))[:, k * 256 + t * P:k * 256 + (t + 1) * P],
                                           HN[:, t, c * P:(c + 1) * P], ident)
                    if t == NT - 1:
                        done(ins, ("norm", n, b))

        def hT_ready(n):
            for b in range(4):
                await_free_of(pe, ("norm", n, b))

        def in_channel(t, key, units=((0, 128), (128, 128)), done=True):
            claim(pe, key)
            await_tile(t)
            for c, (o, m) in enumerate(units):
                for k in range(KC):
                    ins = mm(bank(key)[0:m, c * 256:(c + 1) * 256], in_tile(t)[:, k, o:o + m], HT[:, k, :],
                             start=(k == 0), stop=(k == KC - 1))
            if done:
                ins.then_inc(w_used, 1)

        def in_token(t, key):
            claim(pe, key)
            await_tile(t)
            for tt in range(NT):
                for k in range(KC):
                    ins = mm(bank(key)[:, tt * 256:(tt + 1) * 256], HT[:, k, tt * P:(tt + 1) * P], in_tile(t)[:, k, :],
                             start=(k == 0), stop=(k == KC - 1))
            ins.then_inc(w_used, 1)

        def done(ins, key):
            ins.then_inc(uses[key][2], 1)

        def sums(key, sq, sqname, n, mat, o=0, w=512):
            claim(pe, key)
            pe.wait_ge(sem(sqname), n)
            done(mm(bank(key)[:, o:o + w], mat, sq[:, o:o + w], start=True, stop=True), key)

        def attn_step(i, name, heads, groups, combine, scores, src, values, dv, parts="stv"):
            if i < heads and "s" in parts:
                for c in range(combine):
                    u = i * combine + c
                    for g in range(groups):
                        key = (name, "s", u, g)
                        claim(pe, key)
                        done(scores(bank(key), u, g), key)
            if 1 <= i <= heads and "t" in parts:
                h = i - 1
                pe.wait_ge(sem(name + ("_w" if combine > 1 else "_e")), h + 1)
                for g in range(groups):
                    key = (name, "t", h, g)
                    claim(pe, key)
                    for b in range(3):
                        ins = pe.transpose(bank(key)[:, b * P:(b + 1) * P], src[:, h % 2, g, b * P:(b + 1) * P], ident)
                    done(ins, key)
            if i >= 2 and "v" in parts:
                h = i - 2
                for g in range(groups):
                    await_free_of(pe, (name, "t", h, g))
                if h == 0:
                    for n in range(NT):
                        claim(pe, (name, "o", n))
                for n in range(NT):
                    o = bank((name, "o", n))[:, h * dv:(h + 1) * dv]
                    steps = [(g, kt) for g in range(groups) for kt in range(n + 1)]
                    for j, (g, kt) in enumerate(steps):
                        ins = values(o, h, g, n, kt, j == 0, j == len(steps) - 1)
                    if h == heads - 1:
                        done(ins, (name, "o", n))

        def attn(*args):
            for i in range(args[1] + 2):
                attn_step(i, *args)

        def out_transposes(name, chunks, outputs):
            for key in outputs:
                await_free_of(pe, key)
            for j in range((chunks + 1) // 2):
                key = (name, "oT", j)
                claim(pe, key)
                for k in range(2):
                    for t in range(NT):
                        c = 2 * j + k
                        ins = pe.transpose(bank(key)[:, k * 256 + t * P:k * 256 + (t + 1) * P],
                                           HN[:, t, c * P:(c + 1) * P], ident)
                done(ins, key)

        def transposed(name, j, chunks):
            key = (name, "oT", j)
            claim(pe, key)
            for k, c in enumerate(chunks):
                for t in range(NT):
                    ins = pe.transpose(bank(key)[:, k * 256 + t * P:k * 256 + (t + 1) * P], HN[:, t, c * P:(c + 1) * P], ident)
            done(ins, key)

        def out_chunk(name, j, k, c, first=False, used=False):
            t = BASE[name + "_out"] + j
            await_tile(t)
            if first:
                for b in range(4):
                    claim(pe, ("y", name, b))
            for tt in range(NT):
                for hf in range(2):
                    ins = mm(PS[2 * tt + hf][:, :], OT[:, c, tt * P:(tt + 1) * P], out_tile(t)[:, k, hf * 512:(hf + 1) * 512],
                             start=first, stop=False, skip_group_check=True)
            if used:
                ins.then_inc(w_used, 1)

        def out_last_tile(name, tiles, chunks):
            t = BASE[name + "_out"] + tiles - 1
            await_tile(t)
            for tt in range(NT):
                for k, c in enumerate(chunks):
                    for hf in range(2):
                        ins = mm(PS[2 * tt + hf][:, :], OT[:, c, tt * P:(tt + 1) * P], out_tile(t)[:, k, hf * 512:(hf + 1) * 512],
                                 start=False, stop=(k == 1), skip_group_check=True)
                        if k == 1 and 2 * tt + hf < 3:
                            done(ins, ("y", name, 2 * tt + hf))
            ins.then_inc(w_used, 1)

        def out_proj(name, tiles, oT_banks):
            t0 = BASE[name + "_out"]
            for j in range(tiles):
                await_tile(t0 + j)
                if j == 0:
                    for i in range(oT_banks):
                        await_free_of(pe, (name, "oT", i))
                    for b in range(4):
                        claim(pe, ("y", name, b))
                for tt in range(NT):
                    for c in range(2):
                        for hf in range(2):
                            ins = mm(PS[2 * tt + hf][:, :], OT[:, 2 * j + c, tt * P:(tt + 1) * P],
                                     out_tile(t0 + j)[:, c, hf * 512:(hf + 1) * 512],
                                     start=(j == 0 and c == 0), stop=(j == tiles - 1 and c == 1))
                            if j == tiles - 1 and c == 1 and 2 * tt + hf < 3:
                                done(ins, ("y", name, 2 * tt + hf))
                ins.then_inc(w_used, 1)

        def even():
            t0 = BASE["ev_in"]
            hT_ready(0)
            in_channel(t0, ("ev", "ar"), units=((0, 16),))
            in_channel(t0 + 1, ("ev", "aq"))
            in_channel(t0 + 2, ("ev", "ak"))
            claim(pe, ("ev", "la"))
            await_free_of(pe, ("ev", "ar"))
            wa2 = prm("wa2")
            for c in range(2):
                ins = mm(bank(("ev", "la"))[:, c * 256:(c + 1) * 256], wa2[0:16, c * P:(c + 1) * P], ev.arT[0:16, :],
                         start=True, stop=True)
            done(ins, ("ev", "la"))
            for j in range(2):
                in_token(t0 + 3 + j, ("ev", "av", j))
            for j in range(2):
                in_token(t0 + 5 + j, ("ev", "ag", j))
            def gla_scores():
                key = ("ev", "kwT")
                claim(pe, key)
                await_free_of(pe, ("ev", "ak"))
                await_free_of(pe, ("ev", "aq"))
                for t in range(NT):
                    for c in range(2):
                        ins = pe.transpose(bank(key)[:, (t * 2 + c) * P:(t * 2 + c + 1) * P],
                                           ev.KW[:, c * 256 + t * P:c * 256 + (t + 1) * P], ident)
                done(ins, key)
                for r in range(2):
                    key = ("ev", "att", r)
                    claim(pe, key)
                    rp = slice(64 * r, 64 * r + 64)
                    for t in range(NT):
                        for c in range(2):
                            cc = slice(c * 256 + t * P, c * 256 + (t + 1) * P)
                            ins = mm(bank(key)[:, (2 * t + c) * P:(2 * t + c + 1) * P], ev.KD[rp, cc], ev.QD[rp, cc], start=True, stop=True)
                    done(ins, key)

            def gla_states():
                await_free_of(pe, ("ev", "kwT"))
                await_free_of(pe, ("ev", "av", 1))
                await_free_of(pe, ("ev", "av", 0))
                for n in range(NCH - 1):
                    key = ("ev", "kv", n)
                    claim(pe, key)
                    rp = slice(64 * (n % 2), 64 * (n % 2) + 64)
                    for c in range(2):
                        ins = mm(bank(key)[:, c * 256:(c + 1) * 256], ev.KWT[rp, n // 2, c * P:(c + 1) * P],
                                 ev.V[rp, n // 2, c * 256:(c + 1) * 256], start=True, stop=True)
                    done(ins, key)

            def gla_out():
                for r in range(2):
                    await_free_of(pe, ("ev", "att", r))
                for t in range(NT):
                    key = ("ev", "o", t)
                    claim(pe, key)
                    for h in range(4):
                        mm(bank(key)[:, h * P:(h + 1) * P], ev.ATT[:, 4 * (h % 2) + 2 * t + h // 2, :], ev.V[:, t, h * P:(h + 1) * P],
                           start=(h == 0), stop=False, skip_group_check=True)
                    for n in (2 * t, 2 * t + 1):
                        if n == 0:
                            continue
                        await_free_of(pe, ("ev", "kv", n - 1))
                        for c in range(2):
                            ins = mm(bank(key)[64 * (n % 2):64 * (n % 2) + 64, c * 256:(c + 1) * 256],
                                     ev.QD[:, c * 256 + n * CH:c * 256 + (n + 1) * CH],
                                     ev.ST[:, n - 1, c].rearrange("p r v -> p (r v)"), start=False, stop=(n == 2 * t + 1 and c == 1),
                                     skip_group_check=True)
                    done(ins, key)

            for j in range(4):
                in_channel(t0 + 7 + j, ("ev", "bqk", j))
                if j:
                    sums(("ev", "ss", j - 1), ev.SQ[:, (j - 1) % 2, :], "ev_sq", j, blk64)
                if j < 3:
                    (gla_scores, gla_states, gla_out)[j]()
            def scores(bk, u, g):
                h, c = u // 2, u % 2
                if u % 4 == 0:
                    for j in (h, h + 1):
                        await_free_of(pe, ("ev", "bqk", j))
                r = slice(64 * c, 64 * c + 64)
                q, k = ev.QK[r, h // 2 * 2, h % 2, :], ev.QK[r, h // 2 * 2 + 1, h % 2, :]
                mm(bk[:, 0:P], q[:, 0:P], k[:, 0:P], start=True, stop=True)
                return mm(bk[:, P:P + 256], q[:, P:256], k[:, 0:256], start=True, stop=True)

            def values(o, h, g, n, kt, first, last):
                b = 0 if n == 0 else 1 + kt
                return mm(o, ev.PT[:, h % 2, 0, b * P:(b + 1) * P], ev.BV[:, kt, h * P:(h + 1) * P], start=first, stop=last)

            da = ("evd", 4, 1, 2, scores, ev.WC, values, 128)
            attn_step(0, *da)
            in_token(t0 + 11, ("ev", "bv", 0))
            sums(("ev", "ss", 3), ev.SQ[:, 1, :], "ev_sq", 4, blk64)
            attn_step(1, *da, parts="s")
            in_token(t0 + 12, ("ev", "bv", 1))
            attn_step(1, *da, parts="t")
            await_free_of(pe, ("ev", "bv", 0))
            await_free_of(pe, ("ev", "bv", 1))
            for i in range(2, 6):
                if i == 4:
                    for t in range(NT):
                        await_free_of(pe, ("ev", "o", t))
                    for j in range(2):
                        transposed("ev", j, (2 * j, 2 * j + 1))
                    for j in range(2):
                        await_free_of(pe, ("ev", "oT", j))
                    out_chunk("ev", 0, 0, 0, first=True)
                attn_step(i, *da)
                if i == 4:
                    out_chunk("ev", 0, 1, 1, used=True)
            out_chunk("ev", 1, 0, 2)
            out_chunk("ev", 1, 1, 3, used=True)
            for t in range(NT):
                await_free_of(pe, ("evd", "o", t))
            for j in range(2, 4):
                transposed("ev", j, (2 * j, 2 * j + 1))
            for j in range(2, 4):
                await_free_of(pe, ("ev", "oT", j))
            for c in (4, 5):
                out_chunk("ev", 2, c - 4, c, used=(c == 5))
            out_last_tile("ev", EV_OUT, (6, 7))

        def odd():
            t0 = BASE["od_in"]
            hT_ready(2)
            pe.wait_ge(s_late, 32)
            for g in range(3):
                for j in range(4):
                    in_channel(t0 + 6 * g + j, ("od", "qk", g, j))
                    if j:
                        sums(("od", "ss", g, j - 1), od.SQ[:, (j - 1) % 2, :], "od_sq", 4 * g + j, ones)
                in_token(t0 + 6 * g + 4, ("od", "v", g, 0))
                sums(("od", "ss", g, 3), od.SQ[:, 1, :], "od_sq", 4 * g + 4, ones)
                in_token(t0 + 6 * g + 5, ("od", "v", g, 1))
            for g in range(3):
                for j in range(4):
                    await_free_of(pe, ("od", "qk", g, j))
                for j in range(2):
                    await_free_of(pe, ("od", "v", g, j))

            def scores(bk, h, g):
                q, k = od.QK[:, g, h // 2, h % 2, :], od.QK[:, g, 2 + h // 2, h % 2, :]
                mm(bk[:, 0:P], q[:, 0:P], k[:, 0:P], start=True, stop=True)
                return mm(bk[:, P:P + 256], q[:, P:256], k[:, 0:256], start=True, stop=True)

            def values(o, h, g, n, kt, first, last):
                b = 0 if n == 0 else 1 + kt
                return mm(o, od.PT[:, h % 2, g, b * P:(b + 1) * P], od.V[:, g, kt, h * P:(h + 1) * P], start=first, stop=last)

            attn("od", 4, 3, 1, scores, od.EX, values, 128)
            out_transposes("od", 4, [("od", "o", 0), ("od", "o", 1)])
            out_proj("od", OD_OUT, 2)

        def mixer2(m, l):
            t0 = BASE[f"{m}_in"]
            hT_ready(4 + 2 * l)
            ab = (m, "ab")
            claim(pe, ab)
            await_tile(t0)
            for j in range(2):
                for k in range(KC):
                    ins = mm(bank(ab)[0:6, j * 256:(j + 1) * 256], in_tile(t0)[:, k, 128 + 6 * j:134 + 6 * j], HT[:, k, :],
                             start=(k == 0), stop=(k == KC - 1))
            done(ins, ab)
            in_channel(t0, (m, "in", 7), units=((0, 128), (140, 6)))
            for j in range(M2_IN - 1):
                jj = j if j < 7 else j + 1
                (in_channel if jj < 8 else in_token)(t0 + 1 + j, (m, "in", jj))
                if jj in M2_SUMS:
                    i = M2_SUMS[jj]
                    k = M2_SUM_ORDER.index(i)
                    hv = M2_SUM_HALVES[i]
                    sums((m, "ss", i), m2.SQ[:, k % 2, :], m + "_sq", k + 1, blk64, 256 * hv[0], 256 * len(hv))
            key = (m, "py")
            claim(pe, key)
            await_free_of(pe, (m, "in", 11))
            pm = cst("pool").rearrange("p (t g n) -> p t g n", t=2, g=4)
            for g in range(4):
                r = slice(64 * (g % 2), 64 * (g % 2) + 64)
                for tt in range(NT):
                    ins = mm(bank(key)[r, (g // 2) * 256:(g // 2 + 1) * 256], m2.XP[:, tt, g * 64:(g + 1) * 64],
                             pm[:, tt, g, :], start=(tt == 0), stop=(tt == NT - 1))
            done(ins, key)
            key = (m, "pz")
            claim(pe, key)
            await_free_of(pe, (m, "py"))
            pw = v3(prm(f"poolw{l}"), 2)
            for g in range(4):
                r = slice(64 * (g % 2), 64 * (g % 2) + 64)
                ins = mm(bank(key)[r, (g // 2) * 256:(g // 2 + 1) * 256], pw[r, g // 2, :], m2.PX[r, g // 2, :],
                         start=True, stop=True)
            done(ins, key)
            key = (m, "rowT")
            claim(pe, key)
            pe.wait_ge(sem(m + "_rows"), 1)
            pe.wait_ge(sem(m + "_ra"), 4)
            G_, GL_, BT_, NG_ = m2.ROW[0:6, 0, :], m2.ROW[0:6, 1, :], m2.ROW[0:6, 2, :], m2.ROW[0:6, 3, :]
            for t in range(NT):
                for j, src in enumerate((G_, GL_, BT_)):
                    ins = pe.transpose(bank(key)[:, (t * 3 + j) * 6:(t * 3 + j) * 6 + 6], src[:, t * P:(t + 1) * P], ident[0:6, 0:6])
            done(ins, key)
            hp = v3(sel("selhp"), 3)
            for name, src in (("gb", G_), ("bb", BT_)):
                for j in range(2):
                    key = (m, name, j)
                    claim(pe, key)
                    for c in range(2 - j):
                        ins = mm(bank(key)[:, c * 256:(c + 1) * 256], hp[0:6, 2 * j + c, :], src, start=True, stop=True)
                    done(ins, key)
            pe.wait_ge(sem(m + "_qk"), 1)
            pe.wait_ge(sem(m + "_v"), 2)
            for t in range(NT):
                key = (m, "kT", t)
                claim(pe, key)
                for c in range(3):
                    ins = pe.transpose(bank(key)[:, c * P:(c + 1) * P], m2.QKN[:, 3 + c, t * P:(t + 1) * P], ident)
                done(ins, key)
            for t in range(NT):
                key = (m, "vT", t)
                claim(pe, key)
                for c in range(3):
                    ins = pe.transpose(bank(key)[:, c * P:(c + 1) * P], m2.Y[:, 6 + c, t * P:(t + 1) * P], ident)
                done(ins, key)
            s6 = v3(sel("sel6"), 6)
            for q in range(3):
                key = (m, "dec", q)
                claim(pe, key)
                for i in range(4):
                    t, h = PAIRS[4 * q + i]
                    o = bank(key)[:, i * P:(i + 1) * P]
                    mm(o, s6[0:6, h, 0:P], G_[:, t * P:(t + 1) * P], start=True, stop=False)
                    mm(o, NG_[:, t * P:(t + 1) * P], s6[0:6, h, 0:P], start=False, stop=False)
                    ins = mm(o, ident, cst("gdneg"), start=False, stop=True)
                done(ins, key)
            for j in range(2):
                await_free_of(pe, (m, "bb", j))
            for name, src, base in (("kk", m2.KB, 0), ("qk", m2.QKN, 0)):
                for q in range(3):
                    key = (m, name, q)
                    claim(pe, key)
                    for i in range(4):
                        t, h = PAIRS[4 * q + i]
                        r = slice(64 * (h % 2), 64 * (h % 2) + 64)
                        if q == 1 and i == 2:
                            fence(ins)
                        ins = mm(bank(key)[:, i * P:(i + 1) * P], m2.QKN[r, 3 + h // 2, t * P:(t + 1) * P],
                                 src[r, h // 2, t * P:(t + 1) * P], start=True, stop=True)
                    done(ins, key)
            for j in (4, 5, 6, 7):
                await_free_of(pe, (m, "in", j))
            pe.wait_ge(sem(m + "_frow"), 1)
            C_, NC_ = m2.ROW2[0:6, 2, :], m2.ROW2[0:6, 3, :]
            await_free_of(pe, (m, "in", 9))
            await_free_of(pe, (m, "in", 10))

            def m2_chunk(c, **flags):
                j = [i for i, cs in enumerate(M2_OUT_CHUNKS) if c in cs][0]
                out_chunk(m, j, M2_OUT_CHUNKS[j].index(c), c, **flags)

            def scores(bk, h, g):
                r = slice(64 * (h % 2), 64 * (h % 2) + 64)
                q, k = m2.FQK[r, h // 2, :], m2.FQK[r, 3 + h // 2, :]
                for n, (o, w) in enumerate(((0, P), (P, 256))):
                    qs = slice(n * P, (n + 1) * P)
                    mm(bk[:, o:o + w], q[:, qs], k[:, 0:w], start=True, stop=False)
                    mm(bk[:, o:o + w], C_[:, qs], s6[0:6, h, 0:w], start=False, stop=False)
                    ins = mm(bk[:, o:o + w], s6[0:6, h, 0:P], NC_[:, 0:w], start=False, stop=True)
                return ins

            def values(o, h, g, n, kt, first, last):
                b = 0 if n == 0 else 1 + kt
                return mm(o, m2.PT[:, h % 2, 0, b * P:(b + 1) * P], m2.FV[:, kt, h * 64:(h + 1) * 64], start=first, stop=last)

            fx = (m + "f", FX_H, 1, 1, scores, m2.EX, values, 64)
            for s in range(GD_STEPS + 1):
                for q in range(3):
                    key = (m, "M", s, q)
                    claim(pe, key)
                    pe.wait_ge(sem(m + "_of"), s + 1)
                    if s == 1:
                        await_free_of(pe, (m, "M", 0, q))
                    elif s:
                        await_free_of(pe, (m, "X", s - 1, q))
                    for i in range(4):
                        z = 4 * q + i
                        ins = mm(bank(key)[:, i * P:(i + 1) * P], m2.OF[:, z, :], ident if s == 0 else m2.DI[:, z, :],
                                 start=True, stop=True)
                    done(ins, key)
                attn_step(s, *fx)
                if s == 0:
                    continue
                for q in range(3):
                    await_free_of(pe, (m, "M", s, q))
                    if s == 1:
                        pe.wait_ge(sem(m + "_ui"), 1)
                    else:
                        await_free_of(pe, (m, "Y", s - 1, q))
                    if s < GD_STEPS:
                        key = (m, "X", s, q)
                        claim(pe, key)
                        for i in range(4):
                            z = 4 * q + i
                            ins = mm(bank(key)[:, i * P:(i + 1) * P], m2.UI[:, z, :], m2.M1[:, z, :], start=True, stop=True)
                        done(ins, key)
                    key = (m, "Y", s, q)
                    claim(pe, key)
                    for i in range(4):
                        z = 4 * q + i
                        ins = mm(bank(key)[:, i * P:(i + 1) * P], m2.M1[:, z, :], m2.UI[:, z, :], start=True, stop=True)
                    done(ins, key)
            for q in range(3):
                await_free_of(pe, (m, "Y", GD_STEPS, q))
            for t in range(NT):
                await_free_of(pe, (m, "kT", t))
                await_free_of(pe, (m, "vT", t))
            for t in range(NT):
                key = (m, "u", t)
                claim(pe, key)
                for h in range(6):
                    ins = mm(bank(key)[:, h * 64:(h + 1) * 64], m2.UI[:, PAIRS.index((t, h)), :], m2.VB[:, t, h * 64:(h + 1) * 64],
                             start=True, stop=True)
                done(ins, key)
                key = (m, "w", t)
                claim(pe, key)
                for h in range(6):
                    ins = mm(bank(key)[64 * (h % 2):64 * (h % 2) + 64, (h // 2) * P:(h // 2 + 1) * P],
                             m2.KBG[:, t, h * 64:(h + 1) * 64], m2.UI[:, PAIRS.index((t, h)), :], start=True, stop=True)
                done(ins, key)
            attn_step(GD_STEPS + 1, *fx)
            pe.wait_ge(sem(m + "_qd"), 1)
            for q in range(3):
                await_free_of(pe, (m, "qk", q))
            for n in range(NCH):
                t, p0 = n // 2, 64 * (n % 2)
                rp = slice(p0, p0 + 64)
                cols = slice(n * CH, (n + 1) * CH)
                await_free_of(pe, (m, "u", t))
                if n == 2:
                    m2_chunk(7, used=True)
                if n == 3:
                    for j in range(2):
                        await_free_of(pe, (m, "oT", j))
                    m2_chunk(4)
                if n:
                    key = (m, "vp", n)
                    claim(pe, key)
                    await_free_of(pe, (m, "kv", n - 1))
                    await_free_of(pe, (m, "w", t))
                    for c in range(3):
                        ins = mm(bank(key)[rp, c * P:(c + 1) * P], m2.WT[:, c, cols], m2.S[:, n % 2, c, :], start=True, stop=True)
                    done(ins, key)
                key = (m, "o", t)
                if p0 == 0:
                    claim(pe, key)
                for c in range(3):
                    mm(bank(key)[rp, c * P:(c + 1) * P], m2.QD[:, c, cols], m2.S[:, n % 2, c, :], start=(c == 0), stop=False,
                       skip_group_check=True)
                if n == 1:
                    await_free_of(pe, (m, "pz"))
                    m2_chunk(6, first=True)
                if n == 2:
                    for k in range(NT):
                        await_free_of(pe, (m + "f", "o", k))
                    for j in range(2):
                        transposed(m, j, M2_OT[j])
                if n == 3:
                    m2_chunk(5, used=True)
                if n:
                    await_free_of(pe, (m, "vp", n))
                if n < NCH - 1:
                    key = (m, "kv", n)
                    claim(pe, key)
                    for c in range(3):
                        ins = mm(bank(key)[:, c * P:(c + 1) * P], m2.KDEC[rp, t, c * P:(c + 1) * P], m2.UU[rp, t, c * P:(c + 1) * P],
                                 start=True, stop=True)
                    done(ins, key)
                if n == 0:
                    attn_step(GD_STEPS + 2, *fx)
                if p0:
                    key = (m, "o", t)
                    for h in range(6):
                        ins = mm(bank(key)[:, h * 64:(h + 1) * 64], m2.ATQ[:, PAIRS.index((t, h)), :], m2.UU[:, t, h * 64:(h + 1) * 64],
                                 start=False, stop=(h == 5), skip_group_check=True)
                    done(ins, key)
            m2_chunk(3)
            for t in range(NT):
                await_free_of(pe, (m, "o", t))
            for j in range(2, 4):
                transposed(m, j, M2_OT[j])
            for j in range(2, 4):
                await_free_of(pe, (m, "oT", j))
            m2_chunk(2, used=True)
            out_last_tile(m, M2_OUT, M2_OUT_CHUNKS[-1])

        def router():
            hT_ready(7)
            key = ("router", "logits")
            claim(pe, key)
            rt = v3(prm("router"), KC)
            for t in range(NT):
                for k in range(KC):
                    ins = mm(bank(key)[:, t * 8:(t + 1) * 8], HT[:, k, t * P:(t + 1) * P], rt[:, k, :],
                             start=(k == 0), stop=(k == KC - 1))
            done(ins, key)
            key = ("router", "place")
            claim(pe, key)
            pe.wait_ge(sem("chosen"), 1)
            m3 = mo.MASK.rearrange("p (t e) -> p t e", t=NT)
            earlier = cst("earlier")
            mm(bank(key)[:, 0:8], earlier, m3[:, 0, :], start=True, stop=True)
            mm(bank(key)[:, 8:16], ones, m3[:, 0, :], start=True, stop=False)
            mm(bank(key)[:, 8:16], earlier, m3[:, 1, :], start=False, stop=True)
            mm(bank(key)[:, 16:24], ones, m3[:, 0, :], start=True, stop=False)
            done(mm(bank(key)[:, 16:24], ones, m3[:, 1, :], start=False, stop=True), key)

        def moe(p):
            name = moe_name[p]
            w0, k0 = BASE["moe"] + p * MOE_TILES, ffn_k0[name]
            pe.wait_ge(sem("hn_lo"), p + 1)
            pe.wait_ge(sem("moe_sel"), p + 1)
            for c in range(KC):
                for hf in range(2):
                    key = ("moe", p, "gx", 2 * c + hf)
                    claim(pe, key)
                    for n, hn in enumerate((HNH, HNL)):
                        for t in range(NT):
                            ins = mm(bank(key)[:, :], hn[:, t, c * P:(c + 1) * P],
                                     SELR[:, t, 4 * hf:4 * hf + 4, :].rearrange("p e s -> p (e s)"),
                                     start=(n == 0 and t == 0), stop=(n == 1 and t == NT - 1))
                    done(ins, key)
            pe.wait_ge(sem("moe_gsel"), p + 1)
            for j in range(4):
                key = ("moe", p, "selT", j)
                claim(pe, key)
                for k in range(2):
                    for t in range(NT):
                        ins = pe.transpose(bank(key)[:, k * 256 + t * P:k * 256 + (t + 1) * P], mo.GSEL[:, t, 2 * j + k, :], ident)
                done(ins, key)
            for b in range(4):
                claim(pe, ("y", name, b))
                mm(PS[b][:, :], ident, X[:, b // 2, (b % 2) * 512:(b % 2 + 1) * 512], start=True, stop=False, skip_group_check=True)
            for j in range(12, 16):
                await_free_of(pe, ("moe", p, "gx", j))
            for j in range(4):
                await_free_of(pe, ("moe", p, "selT", j))

            def await_moe_tile(ts, i):
                pe.wait_ge(w_full[ts % RING], 16 * (ts // RING + 1) + 16 * (3 * G_EXP // RING) * i)

            def up(gs, i, first=False):
                b, e = 6 + gs % 2, gs // G_EXP
                pe.wait_ge(free[b], k0[b] + gs // 2 + (G_EXP // 2) * i)
                for half in range(2):
                    ts = w0 + half if first else w0 + 3 * gs - 1 + half
                    await_moe_tile(ts, i)
                    for c in range(2):
                        for kk in range(KC):
                            x = mo.XG[:, kk, e, :] if isinstance(i, int) else mo.XG[:, kk, bass.ds(i + e, 1), :].rearrange("p e s -> p (e s)")
                            o = half * 256 + c * P
                            ins = mm(PS[b][:, o:o + P], in_tile(ts)[:, kk, c * P:(c + 1) * P], x, start=(kk == 0), stop=(kk == KC - 1))
                    ins.then_inc(w_used, 1)

            def down(gs, i):
                g = MOE_GROUPS * p + gs + 1 + G_EXP * i
                pe.wait_ge(sem("moe_lo"), g)
                pe.wait_ge(sem("moe_gl"), g)
                if gs % G_EXP == 0:
                    for b in (4, 5):
                        pe.wait_ge(free[b], k0[b] + gs // G_EXP + i)
                for c in range(2):
                    for n, (gh, wt) in enumerate(((GRH, DH), (GRH, DL), (GRL, DH))):
                        for hf in range(2):
                            ins = mm(PS[4 + hf][:, :], gh[:, gs % 2, c * P:(c + 1) * P], wt[:, c, hf * 512:(hf + 1) * 512],
                                     start=(gs % G_EXP == 0 and c == 0 and n == 0), stop=(gs % G_EXP == G_EXP - 1 and c == 1 and n == 2),
                                     skip_group_check=True)
                ins.then_inc(w_used, 1)

            def scatter(e, i, last=False):
                for b in (4, 5):
                    pe.wait_ge(free[b], k0[b] + e + 1 + i)
                for t in range(NT):
                    for hf in range(2):
                        ins = mm(PS[2 * t + hf][:, :], mo.GS[:, t * P:(t + 1) * P], mo.YE[:, hf * 512:(hf + 1) * 512], start=False, stop=last, skip_group_check=True)
                        if last:
                            done(ins, ("y", name, 2 * t + hf))
                if not last:
                    ins.then_inc(sem("moe_scattered"), 1)

            up(0, 0, True)
            up(1, 0)
            down(0, 0)
            with pe.Fori(0, N_EXP - 1) as i:
                for u in range(G_EXP):
                    g = 2 + u
                    up(g, i)
                    if g == G_EXP + 1:
                        scatter(0, i)
                    down(g - 1, i)
            for g in range(2 + (N_EXP - 1) * G_EXP, MOE_GROUPS):
                up(g, 0)
                down(g - 1, 0)
            down(MOE_GROUPS - 1, 0)
            scatter(N_EXP - 1, 0, True)

        def ffn(name, groups, kind):
            w0, k0 = BASE[name], ffn_k0[name]
            body = 2

            def await_split(j, i):
                pe.wait_ge(lo_done, split_base[name] + j + 1 + 3 * body * i)

            def up(gs, i, first=False):
                for half in range(2):
                    j = half if first else 3 * gs - 1 + half
                    b, sl = 4 + 2 * (gs % 2) + half, j % SPLIT
                    await_split(j, i)
                    k = k0[b] + gs // 2
                    if not (isinstance(k, int) and k == 0):
                        pe.wait_ge(free[b], k + (body // 2) * i)
                    for c in range(2):
                        for kk in range(KC):
                            o = kk * TW + c * P
                            for n, (wt, ht) in enumerate(((WH, HTH), (WH, HTL), (WL, HTH))):
                                ins = mm(PS[b][:, c * 256:(c + 1) * 256], wt[:, sl, o:o + P], ht[:, kk, :],
                                         start=(kk == 0 and n == 0), stop=(kk == KC - 1 and n == 2))
                    ins.then_inc(w_used, 1)

            def down(gs, i, j):
                sl = j % SPLIT
                await_split(j, i)
                pe.wait_ge(sem(name + "_gl"), gs + 1 + body * i)
                if gs == 0:
                    for b in range(4):
                        claim(pe, ("y", name, b))
                last = isinstance(i, int) and gs == groups - 1
                for tt in range(NT):
                    for c in range(2):
                        for n, (gh, wt) in enumerate(((GHH, WH), (GHH, WL), (GHL, WH))):
                            for hf in range(2):
                                o = c * D + hf * 512
                                ins = mm(PS[2 * tt + hf][:, :], gh[:, gs % 2, c, tt * P:(tt + 1) * P], wt[:, sl, o:o + 512],
                                         start=(gs == 0 and c == 0 and n == 0), stop=(last and c == 1 and n == 2),
                                         skip_group_check=True)
                                if last and c == 1 and n == 2 and 2 * tt + hf < 3:
                                    done(ins, ("y", name, 2 * tt + hf))
                ins.then_inc(w_used, 1)

            hT_ready({"ffn0": 1, "ffn1": 3, "ffn2": 5}[name])
            up(0, 0, True)
            up(1, 0)
            down(0, 0, 4)
            rounds = (groups - 2) // body
            with pe.Fori(0, rounds) as i:
                for u in range(body):
                    g = 2 + u
                    up(g, i)
                    down(g - 1, i, 3 * (g - 1) + 4)
            assert 3 * body % RING == 0 and 3 * body % SPLIT == 0 and body % 2 == 0
            for g in range(2 + rounds * body, groups):
                up(g, 0)
                down(g - 1, 0, 3 * (g - 1) + 4)
            down(groups - 1, 0, 3 * groups - 1)

        pe.wait_ge(s_const, 32)
        for st in order:
            if st[0] == "norm":
                norm(st[1])
            elif st[0] == "even":
                even()
            elif st[0] == "odd":
                odd()
            elif st[0] == "m2":
                mixer2(*st[1:])
            elif st[0] == "router":
                router()
            elif st[0] == "moe":
                moe(0)
                with pe.If(more_tokens(pe) > 0):
                    moe(1)
            else:
                ffn(*st[1:])

    @block.scalar
    def _(act):
        A = act.activation
        chain = [0]
        s_act = sem("act_chain")

        def link(ins):
            chain[0] += 1
            ins.then_inc(s_act, 1)
            act.wait_ge(s_act, chain[0])

        def logs():
            act.preload_act_table_set("natural_log_exp_and_others")

        def norm(n):
            if n in ffn_of_norm:
                act.preload_act_table(ACT.Silu)
            elif n and n < 7:
                logs()
            if n == 0:
                act.wait_ge(s_in, 16)
            for t in range(NT):
                if n:
                    for b in (2 * t, 2 * t + 1):
                        await_free_of(act, ("y", resid_of[n], b))
                A(HT[:, 4 * t:4 * t + 4, :].rearrange("p a b -> p (a b)"), X[:, t, :], ACT.Square, scale=D ** -0.5,
                  accum_out=st_ss[:, t:t + 1]).then_inc(sem("mean_sq"), 1)
            g = prm("norm")
            if n in ffn_of_norm:
                name = ffn_of_norm[n]
                hi(name, 0, 0)
                for b in range(4):
                    await_full(act, ("norm", n, b))
                    for k in range(2):
                        c = 2 * b + k
                        ins = A(HTH[:, c, :], bank(("norm", n, b))[:, k * 256:(k + 1) * 256], ACT.Copy, scale=g[:, n * KC + c:n * KC + c + 1])
                    ins.then_inc(sem("ht_hi"), 1)
                for j in range(1, SPLIT):
                    hi(name, j, 0)
                return
            for b in range(2):
                key = ("norm", n, b)
                await_full(act, key)
                for k in range(2):
                    c = 2 * b + k
                    ins = A(HT[:, c, :], bank(key)[:, k * 256:(k + 1) * 256], ACT.Copy, scale=g[:, n * KC + c:n * KC + c + 1])
                release(ins, key)

        def hi(name, j, i):
            t = BASE[name] + j
            act.wait_ge(w_full[t % RING], 16 * (t // RING + 1) + 16 * i)
            act.wait_ge(w_used, (t - SPLIT + 1 if j >= SPLIT else BASE[name]) + RING * i)
            A(WH[:, j % SPLIT, :], W[:, t % RING, :], ACT.Copy).then_inc(hi_done, 1)

        def squares(src, sq, name):
            A(sq, src, ACT.Square).then_inc(sem(name), 1)

        def rsqrt(key, rs, name, scale, o=0, w=512):
            await_full(act, key)
            release(A(rs[:, o:o + w], bank(key)[:, o:o + w], ACT.Ln, scale=scale, bias=eps), key)
            await_free_of(act, key)
            A(rs[:, o:o + w], rs[:, o:o + w], ACT.Exp, scale=-0.5).then_inc(sem(name), 1)

        def attn_step(i, name, heads, groups, combine, SM, EX, PT, parts="et"):
            if i < heads and "e" in parts:
                for c in range(combine):
                    u = i * combine + c
                    act.wait_ge(sem(name + "_mx"), u + 1)
                    if i >= 2 and c == 0:
                        if combine == 1:
                            for g in range(groups):
                                await_full(act, (name, "t", i - 2, g))
                        else:
                            act.wait_ge(sem(name + "_w"), i - 1)
                    b = u % (2 * combine)
                    for n, sl in enumerate((slice(0, P), slice(P, 384))):
                        j = 2 * u + n
                        ins = A(EX[:, b, :, sl], SM[:, u % 2, :, sl], ACT.Exp, bias=st_mx[:, j:j + 1],
                                accum_out=st_sum[:, j:j + 1])
                    ins.then_inc(sem(name + "_e"), 1)
            if i >= 1 and "t" in parts:
                for g in range(groups):
                    key = (name, "t", i - 1, g)
                    await_full(act, key)
                    release(A(PT[:, (i - 1) % 2, g, :], bank(key)[:, 0:384], ACT.Copy), key)

        def attn(*args):
            for i in range(args[1] + 1):
                attn_step(i, *args)

        def out_norm(name, heads, width, sq, sname):
            for t in range(NT):
                key = (name, "o", t)
                await_full(act, key)
                for h in range(heads):
                    ins = A(sq[:, t, h * width:(h + 1) * width], bank(key)[:, h * width:(h + 1) * width], ACT.Square,
                            accum_out=st_o[:, t * 8 + h:t * 8 + h + 1])
                link(ins)
                o = slice(t * 8, t * 8 + heads)
                link(A(st_or[:, o], st_o[:, o], ACT.Ln, scale=1.0 / width, bias=eps))
                A(st_or[:, o], st_or[:, o], ACT.Exp, scale=-0.5).then_inc(sem(sname), 1)

        def out_T(name, j):
            key = (name, "oT", j)
            await_full(act, key)
            release(A(OT[:, 2 * j:2 * j + 2, :].rearrange("p a b -> p (a b)"), bank(key)[:, :], ACT.Copy), key)

        def m2_out_T(m, j):
            key = (m, "oT", j)
            await_full(act, key)
            c, n = M2_OT[j][0], len(M2_OT[j])
            release(A(OT[:, c:c + n, :].rearrange("p a b -> p (a b)"), bank(key)[:, 0:256 * n], ACT.Copy), key)

        def copy_half(dst, key, j):
            await_full(act, key)
            release(A(dst[:, :, j * 256:(j + 1) * 256], v3(bank(key)[:, :], 2), ACT.Copy), key)

        def even():
            key = ("ev", "ar")
            await_full(act, key)
            release(A(ev.arT[0:16, :], bank(key)[0:16, 0:256], ACT.Copy), key)
            key = ("ev", "la")
            await_full(act, key)
            ba = prm("ba")
            for c in range(2):
                ins = A(ev.T1[:, c * 256:(c + 1) * 256], bank(key)[:, c * 256:(c + 1) * 256], ACT.Abs, bias=ba[:, c:c + 1])
            ins.then_inc(sem("ev_a"), 1)
            act.wait_ge(sem("ev_a"), 1)
            link(A(ev.T1, ev.T1, ACT.Exp, scale=-1.0))
            A(ev.T1, ev.T1, ACT.Ln, bias=one).then_inc(sem("ev_a"), 1)
            act.wait_ge(sem("ev_b"), 1)
            A(ev.EB, ev.B, ACT.Exp, scale=1.0 / 16)
            A(ev.ENB, ev.B, ACT.Exp, scale=-1.0 / 16).then_inc(sem("ev_a"), 1)
            act.wait_ge(sem("ev_b"), 2)
            A(ev.EW, ev.EW, ACT.Exp, scale=1.0 / 16).then_inc(sem("ev_a"), 1)
            for j in range(2):
                copy_half(ev.V, ("ev", "av", j), j)
            for j in range(2):
                key = ("ev", "ag", j)
                await_full(act, key)
                release(A(ev.GG[:, :, j * 256:(j + 1) * 256], v3(bank(key)[:, :], 2), ACT.Silu), key)
            logs()
            for j in range(4):
                key = ("ev", "bqk", j)
                await_full(act, key)
                if j >= 2:
                    await_full(act, ("ev", "ss", j - 2))
                squares(bank(key)[:, :], ev.SQ[:, j % 2, :], "ev_sq")
                if j == 1:
                    kt = ("ev", "kwT")
                    await_full(act, kt)
                    release(A(ev.KWT.rearrange("p a b -> p (a b)"), bank(kt)[:, :], ACT.Copy), kt)
                if j:
                    if j >= 3:
                        await_free_of(act, ("ev", "bqk", j - 3))
                    rsqrt(("ev", "ss", j - 1), ev.RS[:, (j - 1) % 2, :], "ev_rs", 1.0 / 64)
            out_norm("ev", 4, 128, ev.OSQ, "ev_or")
            da = ("evd", 4, 1, 2, ev.SM, ev.EX, ev.PT)
            attn_step(0, *da)
            copy_half(ev.BV, ("ev", "bv", 0), 0)
            await_free_of(act, ("ev", "bqk", 1))
            rsqrt(("ev", "ss", 3), ev.RS[:, 1, :], "ev_rs", 1.0 / 64)
            attn_step(1, *da, parts="e")
            copy_half(ev.BV, ("ev", "bv", 1), 1)
            for i in range(1, 5):
                if i == 4:
                    for j in range(2):
                        out_T("ev", j)
                attn_step(i, *da, parts="t" if i == 1 else "et")
            out_norm("evd", 4, 128, ev.SQ, "ev_or")
            out_T("ev", 2)

        def odd():
            k = 0
            for g in range(3):
                for j in range(4):
                    key = ("od", "qk", g, j)
                    await_full(act, key)
                    if k >= 2:
                        await_full(act, ("od", "ss", (k - 2) // 4, (k - 2) % 4))
                    squares(bank(key)[:, :], od.SQ[:, k % 2, :], "od_sq")
                    if j:
                        od_scale(k - 1)
                    k += 1
                copy_half(od.V[:, g], ("od", "v", g, 0), 0)
                od_scale(k - 1)
                copy_half(od.V[:, g], ("od", "v", g, 1), 1)
            attn("od", 4, 3, 1, od.SM, od.EX, od.PT)
            out_T("od", 0)

        def od_scale(k):
            if k >= 2:
                await_free_of(act, ("od", "qk", (k - 2) // 4, (k - 2) % 4))
            rsqrt(("od", "ss", k // 4, k % 4), od.RS[:, k % 2, :], "od_rs", 1.0 / 128)

        def mixer2(m, l):
            key = (m, "ab")
            ra = sem(m + "_ra")
            await_full(act, key)
            RA = m2.ROW2[0:6, 0, :]
            link(A(RA, bank(key)[0:6, 0:256], ACT.Abs, bias=prm(f"dtb{l}")[0:6, :]))
            link(A(RA, RA, ACT.Exp, scale=-1.0))
            A(RA, RA, ACT.Ln, bias=one[0:6, :]).then_inc(ra, 1)
            BT = m2.ROW[0:6, 2, :]
            A(BT, bank(key)[0:6, 256:512], ACT.Copy).then_inc(ra, 1)
            key = (m, "in", 7)
            RF = m2.ROW2[0:6, 3, :]
            await_full(act, key)
            link(A(RF, bank(key)[0:6, 256:512], ACT.Abs, bias=prm(f"fb{l}")[0:6, :]))
            link(A(RF, RF, ACT.Exp, scale=-1.0))
            A(RF, RF, ACT.Ln, bias=one[0:6, :]).then_inc(ra, 1)
            act.wait_ge(ra, 3)
            A(BT, BT, ACT.Sigmoid).then_inc(ra, 1)
            table = ["other"]
            taps = v3(prm(f"dnconv{l}"), 9)

            def square_of(k):
                j = M2_SUM_ORDER[k]
                if k >= 2:
                    await_full(act, (m, "ss", M2_SUM_ORDER[k - 2]))
                hv = M2_SUM_HALVES[j]
                o, w = 256 * hv[0], 256 * len(hv)
                src = m2.Y[:, 2 * j:2 * j + 2, :].rearrange("p a b -> p (a b)") if j < 3 else bank((m, "in", j))[:, :]
                squares(src[:, o:o + w], m2.SQ[:, k % 2, o:o + w], m + "_sq")

            def scale_of(k):
                j = M2_SUM_ORDER[k]
                if k >= 2:
                    act.wait_ge(sem(m + "_nu"), k - 1)
                hv = M2_SUM_HALVES[j]
                if table[0] != "logs":
                    logs()
                    table[0] = "logs"
                rsqrt((m, "ss", j), m2.RS[:, k % 2, :], m + "_rs", 1.0 if j < 3 else 1.0 / 64, 256 * hv[0], 256 * len(hv))

            square_of(0)
            for j in list(range(7)) + [8, 9, 10, 11]:
                key = (m, "in", j)
                await_full(act, key)
                if j < 5 or j in (8, 9):
                    table[0] = "silu"
                if j < 5:
                    us = [u for u in (2 * j, 2 * j + 1) if u < 9]
                    for u in us:
                        ins = A(m2.Y[:, u, :], bank(key)[:, (u % 2) * 256:(u % 2) * 256 + 256], ACT.Copy, scale=taps[:, u, 3:4])
                    ins.then_inc(sem(m + "_c0"), 1)
                    act.wait_ge(sem(m + "_c1"), j + 1)
                    for u in us:
                        ins = A(m2.Y[:, u, :], m2.Y[:, u, :], ACT.Silu)
                    if j < 3:
                        link(ins)
                    else:
                        ins.then_inc(sem(m + "_v"), 1)
                elif j == 8:
                    release(A(m2.ZG[:, :, 0:256], v3(bank(key)[:, :], 2), ACT.Silu), key)
                elif j == 9:
                    A(m2.ZG[:, :, 256:384], v3(bank(key)[:, :], 2)[:, :, 0:P], ACT.Silu).then_inc(sem(m + "_z"), 1)
                    release(A(m2.FV[:, :, 0:P], v3(bank(key)[:, :], 2)[:, :, P:256], ACT.Copy), key)
                elif j == 10:
                    release(A(m2.FV[:, :, P:384], v3(bank(key)[:, :], 2), ACT.Copy), key)
                elif j == 11:
                    release(A(m2.XP, v3(bank(key)[:, :], 2), ACT.Copy), key)
                if j in M2_SUM_ORDER:
                    square_of(M2_SUM_ORDER.index(j))
                if j in M2_SUMS:
                    scale_of(M2_SUM_ORDER.index(M2_SUMS[j]))
            key = (m, "py")
            await_full(act, key)
            release(A(m2.PX.rearrange("p a b -> p (a b)"), bank(key)[:, :], ACT.Copy), key)
            key = (m, "rowT")
            await_full(act, key)
            rows = bank(key)[:, 0:36].rearrange("p (t j h) -> p t j h", t=2, j=3)
            A(st_tm[:, :, 0:2, :], rows[:, :, 0:2, :], ACT.Exp)
            release(A(st_tm[:, :, 2, :], rows[:, :, 2, :], ACT.Copy), key)
            for j in range(2):
                key = (m, "gb", j)
                w = 2 - j
                await_full(act, key)
                release(A(m2.EGB[:, 2 * j:2 * j + w, :], bank(key)[:, 0:256 * w].rearrange("p (a b) -> p a b", a=w), ACT.Exp), key)
            for q in range(3):
                key = (m, "dec", q)
                await_full(act, key)
                release(A(m2.DEC[:, 4 * q:4 * q + 4, :], bank4(key), ACT.Exp), key)
            fx = (m + "f", FX_H, 1, 1, m2.SM, m2.EX, m2.PT)
            attn_step(0, *fx)
            for s in range(1, GD_STEPS + 1):
                for q in range(3):
                    key = (m, "M", s, q)
                    await_full(act, key)
                    if s > 1:
                        await_full(act, (m, "Y", s - 1, q))
                    else:
                        await_full(act, (m, "pz"))
                    release(A(m2.M1[:, 4 * q:4 * q + 4, :], bank4(key), ACT.Copy), key)
                attn_step(s, *fx)
            for t in range(NT):
                key = (m, "u", t)
                await_full(act, key)
                release(A(m2.UU[:, t, :], bank(key)[:, 0:384], ACT.Copy), key)
            attn_step(GD_STEPS + 1, *fx)
            for j in range(2):
                m2_out_T(m, j)
            for t in range(NT):
                key = (m, "o", t)
                await_full(act, key)
                A(m2.SQ[:, t, 0:384], bank(key)[:, 0:384], ACT.Square).then_inc(sem(m + "_osq"), 1)
                act.wait_ge(sem(m + "_oss"), t + 1)
                o = slice(t * 8, t * 8 + 6)
                link(A(st_or[:, o], st_o[:, o], ACT.Ln, scale=1.0 / 64, bias=eps))
                A(st_or[:, o], st_or[:, o], ACT.Exp, scale=-0.5).then_inc(sem(m + "_ors"), 1)
            m2_out_T(m, 2)

        def router():
            act.wait_ge(sem("r_mx"), 1)
            for t in range(NT):
                ins = A(mo.EX[:, t * 8:t * 8 + 8], mo.LG[:, t * 8:t * 8 + 8], ACT.Exp, bias=st_mx[:, t:t + 1],
                        accum_out=st_sum[:, t:t + 1])
            ins.then_inc(sem("r_e"), 1)

        def moe(p):
            name = moe_name[p]
            w0, k0 = BASE["moe"] + p * MOE_TILES, ffn_k0[name]
            act.preload_act_table(ACT.Silu)
            if p:
                await_full(act, ("y", moe_name[0], 3))
            A(HNH[:, :, :].rearrange("p t d -> p (t d)"), HN[:, :, :].rearrange("p t d -> p (t d)"), ACT.Copy).then_inc(sem("hn_hi"), 1)
            g = prm("norm")
            for c in range(KC):
                key = ("moe", p, "gx", 2 * c)
                await_full(act, key)
                release(A(mo.XG[:, c, 0:4, :].rearrange("p e s -> p (e s)"), bank(key)[:, :], ACT.Copy,
                          scale=g[:, 7 * KC + c:7 * KC + c + 1]), key)
            for j in range(4):
                key = ("moe", p, "selT", j)
                await_full(act, key)
                release(A(mo.SELT[:, 2 * j:2 * j + 2, :].rearrange("p e t -> p (e t)"), bank(key)[:, :], ACT.Copy), key)

            def group(gs, i, first=False):
                hb, b = gs % 2, 6 + gs % 2
                act.wait_ge(w_used, w0 + (1 if first else 3 * gs) + 1 + 3 * G_EXP * i)
                act.wait_ge(free[b], k0[b] + gs // 2 + (G_EXP // 2) * i)
                A(mo.SG[:, hb, :], PS[b][:, 0:256], ACT.Silu).then_inc(sem("moe_silu"), 1)
                act.wait_ge(free[b], k0[b] + gs // 2 + 1 + (G_EXP // 2) * i)
                A(GRH[:, hb, :], mo.GH[:, hb, :], ACT.Copy).then_inc(sem("moe_gh"), 1)
                ts = w0 + (3 * gs + 4 if gs < MOE_GROUPS - 1 else MOE_TILES - 1)
                act.wait_ge(w_full[ts % RING], 16 * (ts // RING + 1) + 16 * (3 * G_EXP // RING) * i)
                if gs:
                    act.wait_ge(w_used, w0 + 3 * gs + 2 + 3 * G_EXP * i)
                else:
                    await_full(act, ("moe", p, "gx", 15))
                A(DH[:, :, :].rearrange("p c n -> p (c n)"), tile_ap(ts), ACT.Copy).then_inc(sem("moe_hi"), 1)

            def expert_out(e, i, tile):
                act.wait_ge(w_used, tile + 1 + 3 * G_EXP * i)
                if p or e or not isinstance(i, int):
                    act.wait_ge(sem("moe_scattered"), (N_EXP - 1) * p + e + i)
                A(mo.YE[:, 0:512], PS[4][:, :], ACT.Copy).then_inc(free[4], 1)

            moe_loop(act, group, expert_out, w0)

        def ffn(name, groups, kind):
            w0, k0 = BASE[name], ffn_k0[name]
            body = 2
            f = lambda ap: ap.rearrange("p c t -> p (c t)")
            sv, sc = sem(name + "_v"), sem(name + "_a")

            def split(j, i):
                if j < 3 * groups:
                    hi(name, j, i)

            def group(gs, i, first=False):
                hb, b = gs % 2, 4 + 2 * (gs % 2)
                j = 0 if first else 3 * gs - 1
                dt, dk = 3 * body * i, (body // 2) * i
                act.wait_ge(w_used, w0 + j + 1 + dt)
                if kind != "conv":
                    act.wait_ge(free[b + 1], k0[b + 1] + gs // 2 + dk)
                    A(f(ff.SG[:, hb]), PS[b][:, :], ACT.Silu).then_inc(free[b], 1)
                    split(j + 3, i)
                    split(j + 4, i)
                    act.wait_ge(free[b + 1], k0[b + 1] + gs // 2 + 1 + dk)
                else:
                    if gs >= 2:
                        act.wait_ge(sv, 7 * (gs - 1) + 7 * body * i)
                    off = PRM["conv0" if name == "ffn0" else "conv1"][0]
                    for half, dst in enumerate((ff.YG, ff.YV)):
                        if half:
                            act.wait_ge(w_used, w0 + j + 2 + dt)
                        for c in range(2):
                            unit = off + 4 * (22 * half + 2 * gs + c)
                            col = lambda k: PR[:, unit + k:unit + k + 1] if isinstance(i, int) else \
                                PR[:, bass.ds(8 * body * i + (unit + k), 1)]
                            ins = A(dst[:, hb, c, :], PS[b + half][:, c * 256:(c + 1) * 256], ACT.Identity, scale=col(2), bias=col(3))
                        ins.then_inc(sc, 1)
                        split(j + 3 + half, i)
                    act.wait_ge(sv, 7 * gs + 3 + 7 * body * i)
                    act.wait_ge(free[b], k0[b] + gs // 2 + 1 + dk)
                    A(f(ff.SG[:, hb]), f(ff.YG[:, hb]), ACT.Silu).then_inc(sc, 1)
                    act.wait_ge(sv, 7 * (gs + 1) + 7 * body * i)
                act.wait_ge(w_used, w0 + j + 2 + dt)
                A(GHH[:, hb].rearrange("p c t -> p (c t)"), f(ff.GH[:, hb]), ACT.Copy).then_inc(sem(name + "_gh"), 1)
                if not first:
                    split(j + 5, i)

            group(0, 0, True)
            group(1, 0)
            rounds = (groups - 2) // body
            with act.Fori(0, rounds) as i:
                for u in range(body):
                    group(2 + u, i)
            for g in range(2 + rounds * body, groups):
                group(g, 0)

        act.wait_ge(s_const, 32)
        act.wait_ge(sem("prep"), 1)
        logs()
        link(A(st_lam, st_lam, ACT.Exp))
        for l in range(2):
            ins = A(st_nea[0:6, l:l + 1], prm(f"alog{l}")[0:6, :], ACT.Exp)
        ins.then_inc(sem("prep_a"), 1)
        for st in order:
            if st[0] == "norm":
                norm(st[1])
            elif st[0] == "even":
                even()
            elif st[0] == "odd":
                odd()
            elif st[0] == "m2":
                mixer2(*st[1:])
            elif st[0] == "router":
                router()
            elif st[0] == "moe":
                moe(0)
                with act.If(more_tokens(act) > 0):
                    moe(1)
            else:
                ffn(*st[1:])

    @block.vector
    def _(dve):
        TT, TS, STT = dve.tensor_tensor, dve.tensor_scalar, dve.scalar_tensor_tensor
        chain = [0]
        s_dve = sem("dve_chain")

        def mark(ins):
            chain[0] += 1
            ins.then_inc(s_dve, 1)
            return chain[0]

        def after(n):
            dve.wait_ge(s_dve, n)

        def link(ins):
            after(mark(ins))

        def prep():
            dve.wait_ge(s_const, 32)
            link(TT(st_lamp, prm("lq"), prm("lk"), MUL))
            dve.tensor_reduce(st_lam, v3(st_lamp, 2), AX.X, ADD).then_inc(sem("prep"), 1)
            TS(st_gain[:, 0:1], prm("dq"), 0.125, None, MUL)
            TS(st_gain[:, 1:2], prm("odq"), 128 ** -0.5, None, MUL)
            for l in range(2):
                TS(st_gain[:, 2 + l:3 + l], prm(f"fxq{l}"), 0.125, None, MUL)
            link(TS(st_dg, prm("diff_gain"), 1.0 - LAMBDA_INIT, None, MUL))
            dve.wait_ge(sem("prep_a"), 1)
            link(TT(st_nlam, st_lam[:, 1:2], st_lam[:, 0:1], SUB))
            link(TS(st_nlam, st_nlam, LAMBDA_INIT, None, SUB))
            link(TS(st_nea[0:6, :], st_nea[0:6, :], -1.0, None, MUL))

        def norm(n):
            for t in range(NT):
                dve.wait_ge(sem("rstd"), NT * n + t + 1)
                TS(HN[:, t, :], X[:, t, :], st_rs[:, t:t + 1], None, MUL).then_inc(sem("hn"), 1)
            g = prm("norm")
            if n in ffn_of_norm:
                name = ffn_of_norm[n]
                lo(name, 0, 0)
                k0 = 4 * list(ffn_of_norm).index(n)
                for b in range(4):
                    dve.wait_ge(sem("ht_hi"), k0 + b + 1)
                    for k in range(2):
                        c = 2 * b + k
                        ins = STT(HTL[:, c, :], bank(("norm", n, b))[:, k * 256:(k + 1) * 256], g[:, n * KC + c:n * KC + c + 1],
                                  HTH[:, c, :].bitcast(F32), MUL, SUB)
                    release(ins, ("norm", n, b))
                for j in range(1, SPLIT):
                    lo(name, j, 0)
                return
            for b in range(2, 4):
                key = ("norm", n, b)
                await_full(dve, key)
                for k in range(2):
                    c = 2 * b + k
                    ins = TS(HT[:, c, :], bank(key)[:, k * 256:(k + 1) * 256], g[:, n * KC + c:n * KC + c + 1], None, MUL)
                release(ins, key)

        def lo(name, j, i):
            t = BASE[name] + j
            dve.wait_ge(hi_done, split_base[name] + j + 1 + RING * i)
            TT(WL[:, j % SPLIT, :], W[:, t % RING, :], WH[:, j % SPLIT, :].bitcast(F32), SUB).then_inc(lo_done, 1)

        def resid(name):
            for b in range(4):
                key = ("y", name, b)
                await_full(dve, key)
                xs = X[:, b // 2, (b % 2) * 512:(b % 2 + 1) * 512]
                release(TT(xs, xs, PS[b][:, :], ADD), key)

        def attn_step(i, name, heads, groups, combine, SM, EX, WC, masks):
            if i < heads:
                for c in range(combine):
                    u = i * combine + c
                    if u >= 2:
                        dve.wait_ge(sem(name + "_e"), u - 1)
                    for g in range(groups):
                        key = (name, "s", u, g)
                        await_full(dve, key)
                        release(TT(SM[:, u % 2, g, :], bank(key)[:, 0:384], masks(g), ADD), key)
                    for g in range(groups):
                        await_free_of(dve, (name, "s", u, g))
                    for n, sl in enumerate((slice(0, P), slice(P, 384))):
                        j = 2 * u + n
                        ins = dve.tensor_reduce(st_mx[:, j:j + 1], SM[:, u % 2, :, sl], AX.XY, MAX, negate=True)
                    ins.then_inc(sem(name + "_mx"), 1)
            if combine > 1 and i >= 1:
                h = i - 1
                dve.wait_ge(sem(name + "_e"), 2 * h + 2)
                if h >= 2:
                    await_full(dve, (name, "t", h - 2, 0))
                link(dve.reciprocal(st_ri[:, 4 * h:4 * h + 4], st_sum[:, 4 * h:4 * h + 4]))
                link(TS(st_rl, st_ri[:, 4 * h + 2:4 * h + 4], st_nlam, None, MUL))
                e = 2 * (h % 2)
                sls = (slice(0, P), slice(P, 384))
                for n, sl in enumerate(sls):
                    ins = TS(EX[:, e + 1, 0, sl], EX[:, e + 1, 0, sl], st_rl[:, n:n + 1], None, MUL)
                link(ins)
                for n, sl in enumerate(sls):
                    ins = STT(WC[:, h % 2, 0, sl], EX[:, e, 0, sl], st_ri[:, 4 * h + n:4 * h + n + 1], EX[:, e + 1, 0, sl], MUL, ADD)
                ins.then_inc(sem(name + "_w"), 1)

        def attn(*args):
            for i in range(args[1] + (args[3] > 1)):
                attn_step(i, *args)

        def attn_out(name, heads, width, col):
            dve.wait_ge(sem(name + "_e"), heads)
            link(dve.reciprocal(st_ri[:, 0:2 * heads], st_sum[:, 0:2 * heads]))
            for n in range(NT):
                key = (name, "o", n)
                await_full(dve, key)
                o = bank(key)[:, 0:heads * width].rearrange("p (h v) -> p h v", h=heads)
                ri = st_ri[:, 0:2 * heads].rearrange("p (h n) -> p h n", n=2)[:, :, n]
                dst = HN[:, n, col:col + heads * width].rearrange("p (h v) -> p h v", h=heads)
                release(TT(dst, o, bc(ri, 2, width), MUL), key)

        def out_T(name, j):
            key = (name, "oT", j)
            await_full(dve, key)
            release(dve.tensor_copy(OT[:, 2 * j:2 * j + 2, :].rearrange("p a b -> p (a b)"), bank(key)[:, :]), key)

        def even():
            key = ("ev", "la")
            await_full(dve, key)
            dve.wait_ge(sem("ev_a"), 1)
            ba = prm("ba")
            for c in range(2):
                ins = TS(ev.MN[:, c * 256:(c + 1) * 256], bank(key)[:, c * 256:(c + 1) * 256], ba[:, c:c + 1], 0.0, ADD, MIN)
            release(ins, key)
            await_free_of(dve, key)
            dve.wait_ge(s_late, 32)
            dve.wait_ge(sem("ev_a"), 2)
            link(TT(ev.MN, ev.MN, ev.T1, SUB))
            dve.tensor_tensor_scan(ev.B, cst("reset"), ev.MN, 0.0, MUL, ADD).then_inc(sem("ev_b"), 1)
            dve.wait_ge(sem("ev_b"), 1)
            b3 = v3(ev.B, 8)
            TT(v3(ev.EW, 8), b3[:, :, CH - 1:CH].broadcast_to([P, 8, CH]), b3, SUB).then_inc(sem("ev_b"), 1)
            dve.wait_ge(sem("ev_a"), 3)
            key = ("ev", "aq")
            await_full(dve, key)
            release(STT(ev.QD, bank(key)[:, :], 0.125, ev.EB, MUL, MUL), key)
            key = ("ev", "ak")
            await_full(dve, key)
            TT(ev.KD, bank(key)[:, :], ev.ENB, MUL)
            dve.wait_ge(sem("ev_a"), 4)
            release(TT(ev.KW, bank(key)[:, :], ev.EW, MUL), key)
            await_free_of(dve, ("ev", "ag", 0))
            await_free_of(dve, ("ev", "ag", 1))
            gg = ev.GG.rearrange("p t (h v) -> p (t h) v", v=P)
            link(TT(gg, gg, bc(prm("gla_gain"), 1, 8), MUL))
            def scaled(j):
                key = ("ev", "bqk", j)
                dve.wait_ge(sem("ev_rs"), j + 1)
                gain = st_gain[:, 0:1] if j % 2 == 0 else prm("dk")
                release(STT(ev.QK[:, j].rearrange("p c t -> p (c t)"), bank(key)[:, :], gain, ev.RS[:, j % 2, :], MUL, MUL), key)
            for r in range(2):
                key = ("ev", "att", r)
                await_full(dve, key)
                release(TT(ev.ATT[:, 4 * r:4 * r + 4, :], bank4(key), bc(cst("glamask"), 1, 4), MUL), key)
            scaled(0)
            own = bc(blk64.rearrange("p (r v) -> p r v", r=2)[:, :, 0], 2, P)
            for n in range(NCH - 1):
                key = ("ev", "kv", n)
                await_full(dve, key)
                for c in range(2):
                    ins = TT(ev.ST[:, n, c], bank(key)[:, c * 256:(c + 1) * 256].rearrange("p (r v) -> p r v", r=2), own, MUL)
                if n:
                    link(ins)
                    for c in range(2):
                        e = c * 256 + n * CH + CH - 1
                        f = lambda k: ev.ST[:, k, c].rearrange("p r v -> p (r v)")
                        ins = STT(f(n), f(n - 1), ev.EB[:, e:e + 1], f(n), MUL, ADD)
                release(ins, key)
                await_free_of(dve, key)
            scaled(1)
            scaled(2)
            da = ("evd", 4, 1, 2, ev.SM, ev.EX, ev.WC, lambda g: cst("cmask"))
            attn_step(0, *da)
            gate(("ev", "ev_or"), lambda t, h: ev.GG[:, t, h * P:(h + 1) * P], 0, 0)
            scaled(3)
            attn_step(1, *da)
            for i in range(2, 5):
                attn_step(i, *da)
            gate(("evd", "ev_or"), lambda t, h: st_dg, 512, 2)
            out_T("ev", 3)
            resid("ev")

        def gate(names, factor, col, count):
            for t in range(NT):
                key = (names[0], "o", t)
                dve.wait_ge(sem(names[1]), count + t + 1)
                for h in range(4):
                    ins = STT(HN[:, t, col + h * P:col + (h + 1) * P], bank(key)[:, h * P:(h + 1) * P],
                              st_or[:, t * 8 + h:t * 8 + h + 1], factor(t, h), MUL, MUL)
                release(ins, key)

        def odd():
            for k in range(12):
                g, j = divmod(k, 4)
                key = ("od", "qk", g, j)
                dve.wait_ge(sem("od_rs"), k + 1)
                gain = st_gain[:, 1:2] if j < 2 else prm("odk")
                release(STT(od.QK[:, g, j].rearrange("p c t -> p (c t)"), bank(key)[:, :], gain, od.RS[:, k % 2, :], MUL, MUL), key)
            dm = cst("dmask").rearrange("p (g k) -> p g k", g=3)
            attn("od", 4, 3, 1, od.SM, od.EX, None, lambda g: dm[:, g, :])
            attn_out("od", 4, 128, 0)
            out_T("od", 1)
            resid("od")

        def mixer2(m, l):
            ra = sem(m + "_ra")
            G_, GL_, BT_, NG_ = [m2.ROW[0:6, r, :] for r in range(4)]
            R0, R1, R2, R3 = [m2.ROW2[0:6, r, :] for r in range(4)]
            key = (m, "ab")
            dve.wait_ge(ra, 2)
            release(TS(R1, bank(key)[0:6, 0:256], prm(f"dtb{l}")[0:6, :], 0.0, ADD, MAX), key)
            await_free_of(dve, key)
            link(TT(R1, R1, R0, ADD))
            link(TS(R1, R1, st_nea[0:6, l:l + 1], None, MUL))
            link(dve.tensor_tensor_scan(G_, cst("reset")[0:6, 0:256], R1, 0.0, MUL, ADD))
            g3 = G_.rearrange("p (n c) -> p n c", c=CH)
            TT(GL_.rearrange("p (n c) -> p n c", c=CH), g3[:, :, CH - 1:CH].broadcast_to([6, NCH, CH]), g3, SUB)
            TS(NG_, G_, -1.0, None, MUL).then_inc(sem(m + "_rows"), 1)
            key = (m, "in", 7)
            await_full(dve, key)
            dve.wait_ge(ra, 3)
            dve.wait_ge(sem(m + "_sq"), 1)
            link(TS(R1, bank(key)[0:6, 256:512], prm(f"fb{l}")[0:6, :], 0.0, ADD, MIN))
            link(TT(R1, R1, R3, SUB))
            link(dve.tensor_tensor_scan(R2, cst("ones")[0:6, :], R1, 0.0, MUL, ADD))
            TS(R3, R2, -1.0, None, MUL).then_inc(sem(m + "_frow"), 1)
            taps = v3(prm(f"dnconv{l}"), 9)

            def normed(k):
                j = M2_SUM_ORDER[k]
                dve.wait_ge(sem(m + "_rs"), k + 1)
                key = (m, "in", j)
                for c in M2_SUM_HALVES[j]:
                    u = 2 * j + c
                    rs = m2.RS[:, k % 2, c * 256:(c + 1) * 256]
                    if j < 3:
                        ins = STT(m2.QKN[:, u, :], m2.Y[:, u, :], 0.125 if u < 3 else 1.0, rs, MUL, MUL)
                    else:
                        gain = st_gain[:, 2 + l:3 + l] if u < 12 else prm(f"fxk{l}")
                        ins = STT(m2.FQK[:, u - 9, :], bank(key)[:, c * 256:(c + 1) * 256], gain, rs, MUL, MUL)
                n = mark(ins)
                after(n)
                dve.sem_inc(sem(m + "_nu"), 1)
                if j >= 3:
                    dve.sem_inc(free[uses[key][0]], 1)

            for j in list(range(7)) + [8, 9]:
                if j < 5:
                    key = (m, "in", j)
                    dve.wait_ge(sem(m + "_c0"), j + 1)
                    us = [u for u in (2 * j, 2 * j + 1) if u < 9]
                    last = {}
                    for s in (1, 2, 3):
                        for u in us:
                            if s > 1:
                                after(last[u])
                            o = (u % 2) * 256
                            ins = STT(m2.Y[:, u, s:256], bank(key)[:, o:o + 256 - s], taps[:, u, 3 - s:4 - s], m2.Y[:, u, s:256], MUL, ADD)
                            if s < 3 or u != us[-1]:
                                last[u] = mark(ins)
                    ins.then_inc(sem(m + "_c1"), 1)
                    if j < 4:
                        dve.wait_ge(sem(m + "_c1"), j + 1)
                        dve.sem_inc(free[uses[key][0]], 1)
                if j in M2_SUMS:
                    normed(M2_SUM_ORDER.index(M2_SUMS[j]))
            dve.sem_inc(sem(m + "_qk"), 1)
            dve.wait_ge(sem(m + "_z"), 1)
            zg = m2.ZG.rearrange("p t (h v) -> p (t h) v", v=64)
            link(TT(zg, zg, bc(prm(f"onorm{l}"), 1, 12), MUL))
            key = (m, "pz")
            await_full(dve, key)
            ps = prm(f"pscale{l}")
            for c in range(2):
                ins = TS(OT[:, 6 + c, :], bank(key)[:, c * 256:(c + 1) * 256], ps[:, c:c + 1], None, MUL)
            release(ins, key)
            await_free_of(dve, (m, "rowT"))
            link(TT(st_beg, st_tm[:, :, 2, :], st_tm[:, :, 0, :], MUL))
            for j in range(2):
                await_free_of(dve, (m, "gb", j))
            dve.memset(m2.S[:, 0], 0.0)
            TT(m2.QD, m2.QKN[:, 0:3, :], m2.EGB, MUL).then_inc(sem(m + "_qd"), 1)
            dve.wait_ge(sem(m + "_qd"), 1)
            for j in range(2):
                key = (m, "bb", j)
                w = 2 - j
                await_full(dve, key)
                release(TT(m2.KB[:, 2 * j:2 * j + w, :], m2.QKN[:, 3 + 2 * j:3 + 2 * j + w, :],
                           bank(key)[:, 0:256 * w].rearrange("p (a b) -> p a b", a=w), MUL), key)
            h3 = lambda ap: ap.rearrange("p (h v) -> p h v", h=6)
            for t in range(NT):
                key = (m, "kT", t)
                await_full(dve, key)
                TT(h3(m2.KBG[:, t, :]), h3(bank(key)[:, 0:384]), bc(st_beg[:, t, :], 2, 64), MUL)
                release(TT(h3(m2.KDEC[:, t, :]), h3(bank(key)[:, 0:384]), bc(st_tm[:, t, 1, :], 2, 64), MUL), key)
            for t in range(NT):
                key = (m, "vT", t)
                await_full(dve, key)
                release(TT(h3(m2.VB[:, t, :]), h3(bank(key)[:, 0:384]), bc(st_tm[:, t, 2, :], 2, 64), MUL), key)
            for name, dst in (("kk", m2.AT), ("qk", m2.ATQ)):
                for q in range(3):
                    key = (m, name, q)
                    await_full(dve, key)
                    await_free_of(dve, (m, "dec", q))
                    release(TT(dst[:, 4 * q:4 * q + 4, :], bank4(key), m2.DEC[:, 4 * q:4 * q + 4, :], MUL), key)
            dve.wait_ge(sem(m + "_of"), 1)
            TT(m2.UI, bc(ident, 1, 12), m2.OF, SUB).then_inc(sem(m + "_ui"), 1)
            for q in range(3):
                key = (m, "M", 0, q)
                await_full(dve, key)
                release(TT(m2.DI[:, 4 * q:4 * q + 4, :], bc(ident, 1, 4), bank4(key), SUB), key)
            fx = (m + "f", FX_H, 1, 1, m2.SM, m2.EX, None, lambda g: cst("cmask"))
            attn_step(0, *fx)
            for s in range(1, GD_STEPS + 1):
                attn_step(s, *fx)
                for q in range(3):
                    for name, dst in (("X", m2.DI), ("Y", m2.UI)):
                        if name == "X" and s == GD_STEPS:
                            continue
                        key = (m, name, s, q)
                        await_full(dve, key)
                        d = dst[:, 4 * q:4 * q + 4, :]
                        release(TT(d, d, bank4(key), SUB), key)
            for t in range(NT):
                key = (m, "w", t)
                await_full(dve, key)
                release(dve.tensor_copy(m2.WT[:, :, t * P:(t + 1) * P], bank4(key, 3)), key)
            for n in range(NCH):
                t, p0 = n // 2, 64 * (n % 2)
                rp = slice(p0, p0 + 64)
                if n:
                    key = (m, "vp", n)
                    await_full(dve, key)
                    await_free_of(dve, (m, "u", t))
                    release(TT(m2.UU[rp, t, :], m2.UU[rp, t, :], bank(key)[rp, 0:384], SUB), key)
                if n < NCH - 1:
                    key = (m, "kv", n)
                    await_full(dve, key)
                    S1, S0 = m2.S[:, (n + 1) % 2], m2.S[:, n % 2]
                    e = n * CH + CH - 1
                    TT(S1, S0, m2.EGB[:, :, e:e + 1].broadcast_to([P, 3, P]), MUL)
                    link(TT(m2.SN, bank4(key, 3), bc(blk64, 1, 3), MUL))
                    release(TT(S1, S1, m2.SN, ADD), key)
                    await_free_of(dve, key)
                if n == 0:
                    attn_out(m + "f", 6, 64, 384)
            for t in range(NT):
                key = (m, "o", t)
                dve.wait_ge(sem(m + "_osq"), t + 1)
                dve.tensor_reduce(st_o[:, t * 8:t * 8 + 6], h3(m2.SQ[:, t, 0:384]), AX.X, ADD).then_inc(sem(m + "_oss"), 1)
                dve.wait_ge(sem(m + "_ors"), t + 1)
                dst = HN[:, t, 0:384]
                link(TT(h3(dst), h3(bank(key)[:, 0:384]), bc(st_or[:, t * 8:t * 8 + 6], 2, 64), MUL))
                link(TT(dst, dst, m2.ZG[:, t, :], MUL))
                dve.sem_inc(free[uses[key][0]], 1)
            key = (m, "oT", 3)
            await_full(dve, key)
            release(dve.tensor_copy(OT[:, M2_OT[3][0], :], bank(key)[:, 0:256]), key)
            resid(m)

        def router():
            key = ("router", "logits")
            await_full(dve, key)
            LG, EX_, PB, MASK = mo.LG, mo.EX, mo.PB, mo.MASK
            t2 = lambda ap: ap.rearrange("p (t e) -> p t e", t=2)
            release(dve.tensor_copy(LG, bank(key)[:, 0:16]), key)
            await_free_of(dve, key)
            dve.tensor_reduce(st_mx[:, 0:2], t2(LG), AX.X, MAX, negate=True).then_inc(sem("r_mx"), 1)
            dve.wait_ge(sem("r_e"), 1)
            link(dve.reciprocal(st_ri[:, 0:2], st_sum[:, 0:2]))
            link(TT(t2(PB), t2(EX_), bc(st_ri[:, 0:2], 2, 8), MUL))
            mine = bc(t2(PB), 3, 8)
            other = bc(t2(PB), 2, 8)
            four = lambda ap: ap.rearrange("p (t e f) -> p t e f", t=2, e=8)
            GTR, EQ = four(mo.GTR), four(mo.EQ)
            TT(GTR, other, mine, ALU.is_gt)
            link(TT(EQ, other, mine, ALU.is_equal))
            link(TT(EQ, EQ, bc(cst("before").rearrange("p (e f) -> p e f", e=8), 1, 2), MUL))
            link(TT(GTR, GTR, EQ, ADD))
            link(dve.tensor_reduce(t2(MASK), GTR, AX.X, ADD))
            TS(MASK, MASK, 1.5, None, ALU.is_lt).then_inc(sem("chosen"), 1)
            split_normed(0)
            dve.wait_ge(sem("chosen"), 1)
            link(TT(PB, PB, MASK, MUL))
            link(dve.tensor_reduce(st_sum[:, 2:4], t2(PB), AX.X, ADD))
            link(dve.reciprocal(st_ri[:, 2:4], st_sum[:, 2:4]))
            link(TT(t2(mo.GATE), t2(PB), bc(st_ri[:, 2:4], 2, 8), MUL))
            key = ("router", "place")
            await_full(dve, key)
            link(TS(mo.EX, MASK, -4.0 * S, 4.0 * S, MUL, ADD))
            TT(mo.POS, mo.EX, bank(key)[:, 0:16], ADD)
            link(dve.tensor_reduce(mo.MOST, bank(key)[:, 16:24], AX.X, MAX))
            release(TS(MORE[0:1, :], mo.MOST[0:1, :], P + 0.5, None, ALU.is_gt), key)
            await_free_of(dve, key)
            dve.sem_inc(sem("more"), 1)

        def split_normed(p):
            dve.wait_ge(sem("hn_hi"), p + 1)
            flat = lambda x: x[:, :, :].rearrange("p t d -> p (t d)")
            TT(flat(HNL), flat(HN), flat(HNH).bitcast(F32), SUB).then_inc(sem("hn_lo"), 1)

        def moe(p):
            name = moe_name[p]
            w0, k0 = BASE["moe"] + p * MOE_TILES, ffn_k0[name]
            if p:
                link(TS(mo.POS, mo.POS, -float(P), None, ADD))
                split_normed(p)
            t3 = lambda ap: ap.rearrange("p t e s -> p (t e) s")
            TT(t3(SELR[:, :, :, :]), bc(cst("iota"), 1, 16), bc(mo.POS, 2, P), ALU.is_equal).then_inc(sem("moe_sel"), 1)
            dve.wait_ge(sem("moe_sel"), p + 1)
            TT(t3(mo.GSEL), t3(SELR[:, :, :, :].bitcast(F32)), bc(mo.GATE, 2, P), MUL).then_inc(sem("moe_gsel"), 1)
            g = prm("norm")
            for c in range(KC):
                key = ("moe", p, "gx", 2 * c + 1)
                await_full(dve, key)
                release(TS(mo.XG[:, c, 4:8, :].rearrange("p e s -> p (e s)"), bank(key)[:, :],
                           g[:, 7 * KC + c:7 * KC + c + 1], None, MUL), key)

            def group(gs, i, first=False):
                hb, b = gs % 2, 6 + gs % 2
                dve.wait_ge(sem("moe_silu"), MOE_GROUPS * p + gs + 1 + G_EXP * i)
                TT(mo.GH[:, hb, :], mo.SG[:, hb, :], PS[b][:, 256:512], MUL).then_inc(free[b], 1)
                n = MOE_GROUPS * p + gs + 1 + G_EXP * i
                dve.wait_ge(sem("moe_gh"), n)
                TT(GRL[:, hb, :], mo.GH[:, hb, :], GRH[:, hb, :].bitcast(F32), SUB).then_inc(sem("moe_gl"), 1)
                ts = w0 + (3 * gs + 4 if gs < MOE_GROUPS - 1 else MOE_TILES - 1)
                dve.wait_ge(sem("moe_hi"), n)
                TT(DL[:, :, :].rearrange("p c n -> p (c n)"), tile_ap(ts), DH[:, :, :].rearrange("p c n -> p (c n)").bitcast(F32),
                   SUB).then_inc(sem("moe_lo"), 1)

            def expert_out(e, i, tile):
                dve.wait_ge(w_used, tile + 1 + 3 * G_EXP * i)
                if p or e or not isinstance(i, int):
                    dve.wait_ge(sem("moe_scattered"), (N_EXP - 1) * p + e + i)
                gs = mo.SELT[:, e, :] if isinstance(i, int) else mo.SELT[:, bass.ds(i + e, 1), :].rearrange("p e t -> p (e t)")
                dve.tensor_copy(mo.GS, gs)
                dve.tensor_copy(mo.YE[:, 512:1024], PS[5][:, :]).then_inc(free[5], 1)

            for j in range(4):
                await_free_of(dve, ("moe", p, "selT", j))
            moe_loop(dve, group, expert_out, w0)
            for b in range(4):
                key = ("y", name, b)
                await_full(dve, key)
                release(dve.tensor_copy(X[:, b // 2, (b % 2) * 512:(b % 2 + 1) * 512], PS[b][:, :]), key)

        def ffn(name, groups, kind):
            w0, k0 = BASE[name], ffn_k0[name]
            body = 2
            f = lambda ap: ap.rearrange("p c t -> p (c t)")
            sv, sc = sem(name + "_v"), sem(name + "_a")

            def split(j, i):
                if j < 3 * groups:
                    lo(name, j, i)

            def group(gs, i, first=False):
                hb, b = gs % 2, 4 + 2 * (gs % 2)
                j = 0 if first else 3 * gs - 1
                dt, dk = 3 * body * i, (body // 2) * i
                if kind != "conv":
                    split(j + 3, i)
                    dve.wait_ge(free[b], k0[b] + gs // 2 + 1 + dk)
                    dve.wait_ge(w_used, w0 + j + 2 + dt)
                    TT(f(ff.GH[:, hb]), f(ff.SG[:, hb]), PS[b + 1][:, :], MUL).then_inc(free[b + 1], 1)
                    split(j + 4, i)
                else:
                    off = PRM["conv0" if name == "ffn0" else "conv1"][0]
                    n0 = 7 * gs + 7 * body * i
                    for half, Y in enumerate((ff.YG, ff.YV)):
                        dve.wait_ge(sc, 3 * gs + 1 + half + 3 * body * i)
                        for s in (1, 2):
                            if s == 2:
                                dve.wait_ge(sv, n0 + 2 + 3 * half)
                            for c in range(2):
                                col = off + 4 * (22 * half + 2 * gs + c) + 2 - s
                                w = PR[:, col:col + 1] if isinstance(i, int) else PR[:, bass.ds(8 * body * i + col, 1)]
                                ins = STT(Y[:, hb, c, s:256], PS[b + half][:, c * 256:c * 256 + 256 - s], w, Y[:, hb, c, s:256], MUL, ADD)
                                if s == 2 and c == 1:
                                    ins.then_inc(free[b + half], 1)
                                else:
                                    ins.then_inc(sv, 1)
                        split(j + 3 + half, i)
                    dve.wait_ge(sv, n0 + 6)
                    dve.wait_ge(free[b + 1], k0[b + 1] + gs // 2 + 1 + dk)
                    dve.wait_ge(sc, 3 * gs + 3 + 3 * body * i)
                    TT(f(ff.GH[:, hb]), f(ff.SG[:, hb]), f(ff.YV[:, hb]), MUL).then_inc(sv, 1)
                dve.wait_ge(sem(name + "_gh"), gs + 1 + body * i)
                TT(GHL[:, hb].rearrange("p c t -> p (c t)"), f(ff.GH[:, hb]), GHH[:, hb].rearrange("p c t -> p (c t)").bitcast(F32),
                   SUB).then_inc(sem(name + "_gl"), 1)
                if not first:
                    split(j + 5, i)

            group(0, 0, True)
            group(1, 0)
            rounds = (groups - 2) // body
            with dve.Fori(0, rounds) as i:
                for u in range(body):
                    group(2 + u, i)
            for g in range(2 + rounds * body, groups):
                group(g, 0)
            resid(name)

        prep()
        for st in order:
            if st[0] == "norm":
                norm(st[1])
            elif st[0] == "even":
                even()
            elif st[0] == "odd":
                odd()
            elif st[0] == "m2":
                mixer2(*st[1:])
            elif st[0] == "router":
                router()
            elif st[0] == "moe":
                moe(0)
                with dve.If(more_tokens(dve) > 0):
                    moe(1)
            else:
                ffn(*st[1:])

    block.__exit__(None, None, None)
    return n_tiles


def pack_params(v):
    prm = np.zeros((P, N_PRM), np.float32)

    def put(name, a):
        o, w = PRM[name]
        a = np.asarray(a).reshape(-1, w)
        prm[:a.shape[0], o:o + w] = a

    def cols(a, n):
        return np.asarray(a).reshape(n, P).transpose(1, 0)

    def rows(a):
        a = np.asarray(a).reshape(1, -1)
        return np.broadcast_to(a, (P, a.shape[1]))

    def column(a, reps):
        return np.concatenate([np.asarray(a).reshape(-1)] * reps).reshape(P, 1)

    norms = [v["norm_mix"][0], v["norm_ffn"][0], v["norm_mix"][1], v["norm_ffn"][1],
             v["norm1_2"][0], v["norm2_2"][0], v["norm1_2"][1], v["norm2_2"][1]]
    put("norm", np.concatenate([cols(g, KC) for g in norms], 1))
    put("ba", cols(v["ev_b_a"][0], 2))
    put("wa2", v["ev_w_a2"][0])
    put("gla_gain", rows(v["ev_gla_gain"][0]))
    put("dq", column(v["ev_dq_gain"][0], 2))
    put("dk", column(v["ev_dk_gain"][0], 2))
    put("lq", rows(np.concatenate([v["ev_lq1"][0], v["ev_lq2"][0]])))
    put("lk", rows(np.concatenate([v["ev_lk1"][0], v["ev_lk2"][0]])))
    put("diff_gain", rows(v["ev_diff_gain"][0]))
    put("odq", column(v["od_q_gain"][0], 1))
    put("odk", column(v["od_k_gain"][0], 1))
    for i in range(2):
        taps = np.concatenate([v["ffn_conv_w"][i][:, 0, :], v["ffn_conv_b"][i][None, :]], 0)
        put(f"conv{i}", taps.reshape(4, 44, P).transpose(2, 1, 0).reshape(P, 176))
        put(f"dnconv{i}", v["dn_conv_2"][i].reshape(4, 9, P).transpose(2, 1, 0).reshape(P, 36))
        put(f"alog{i}", v["dn_a_log_2"][i].reshape(6, 1))
        put(f"dtb{i}", v["dn_dt_bias_2"][i].reshape(6, 1))
        put(f"fb{i}", v["fx_f_bias_2"][i].reshape(6, 1))
        put(f"onorm{i}", rows(v["dn_onorm_2"][i]))
        put(f"fxq{i}", column(v["fx_qnorm_2"][i], 2))
        put(f"fxk{i}", column(v["fx_knorm_2"][i], 2))
        put(f"poolw{i}", v["pool_w_2"][i].reshape(2, P, 64).transpose(1, 0, 2).reshape(P, 128))
        put(f"pscale{i}", cols(v["pool_scale_2"][i], 2))
    put("router", v["router_2"][0].reshape(KC, P, N_EXP).transpose(1, 0, 2).reshape(P, KC * N_EXP))
    return prm


def pack_weights(v):
    w = np.zeros((N_TILES, P, KC * TW), np.float32)

    def put_in(t, mat, cols, at=0):
        a = mat[:, cols]
        w[t].reshape(P, KC, TW)[:, :, at:at + a.shape[1]] = a.reshape(KC, P, a.shape[1]).transpose(1, 0, 2)

    def put_out(t, mat, j):
        w[t].reshape(P, 2, D)[:] = mat[j * TW:(j + 1) * TW].reshape(2, P, D).transpose(1, 0, 2)

    def span(o, n=TW):
        return slice(o, o + n)

    m, b = v["ev_w_in"][0], BASE["ev_in"]
    put_in(b, m, span(1536, 16))
    for j, o in enumerate([0, 256, 512, 768, 1024, 1280, 1552, 2064, 1808, 2320, 2576, 2832]):
        put_in(b + 1 + j, m, span(o))
    for j in range(EV_OUT):
        put_out(BASE["ev_out"] + j, v["ev_w_out"][0], j)
    for j in range(OD_IN):
        put_in(BASE["od_in"] + j, v["od_w_in"][0], span(j * TW))
    for j in range(OD_OUT):
        put_out(BASE["od_out"] + j, v["od_w_out"][0], j)
    for l in range(2):
        m, b = v["w_in_2"][l], BASE[f"m{l}_in"]
        units = [span(o, P) for o in list(range(0, 1152, P)) + list(range(1548, 2316, P))]
        put_in(b, m, units[14])
        put_in(b, m, span(1536, 12), 128)
        put_in(b, m, span(2700, 6), 140)
        for j in range(7):
            put_in(b + 1 + j, m, units[2 * j])
            put_in(b + 1 + j, m, units[2 * j + 1], P)
        put_in(b + 8, m, span(1152))
        put_in(b + 9, m, span(1408, P))
        put_in(b + 9, m, span(2316, P), P)
        put_in(b + 10, m, span(2444))
        put_in(b + 11, m, span(2706))
        for j in range(M2_OUT):
            put_out(BASE[f"m{l}_out"] + j, v["w_out_2"][l], M2_OUT - 1 - j)

    def ffn(base, groups, gate, up, down):
        for g in range(groups):
            t = base + (0 if g == 0 else 3 * g - 1)
            put_in(t, *gate(g))
            put_in(t + 1, *up(g))
            put_out(base + (3 * g + 4 if g < groups - 1 else 3 * groups - 1), *down(g))

    for l in range(2):
        u, d = v["ffn_w_up"][l], v["ffn_w_down"][l]
        ffn(BASE[f"ffn{l}"], G_FFN, lambda g: (u, span(g * TW)), lambda g: (u, span(D_FF + g * TW)), lambda g: (d, g))
    ffn(BASE["ffn2"], G_FFN, lambda g: (v["ffn_gate_2"][0], span(g * TW)), lambda g: (v["ffn_up_2"][0], span(g * TW)),
        lambda g: (v["ffn_down_2"][0], g))
    ffn(BASE["moe"], G_EXP * N_EXP, lambda g: (v["moe_gate_2"][0, g // G_EXP], span(g % G_EXP * TW)),
        lambda g: (v["moe_up_2"][0, g // G_EXP], span(g % G_EXP * TW)), lambda g: (v["moe_down_2"][0, g // G_EXP], g % G_EXP))
    return w


STOP = None


def kernel(**inputs):
    import concourse.bacc as _bacc
    from concourse import mybir as _mybir
    from concourse.bass_utils import run_bass_kernel_spmd as _run
    v = {k: np.asarray(a) for k, a in inputs.items()}
    cst, sel = constants()
    arrays = {"weights": pack_weights(v), "x": v["x"], "params": pack_params(v), "consts": cst, "selectors": sel}
    nc = _bacc.Bacc("TRN2", target_bir_lowering=False, num_devices=1)
    f32 = _mybir.dt.float32
    aps = [nc.dram_tensor(f"in_{k}", a.shape, f32, kind="ExternalInput").ap() for k, a in arrays.items()]
    out = nc.dram_tensor("out", (1, S, D), f32, kind="ExternalOutput").ap()
    build(nc, aps[0], aps[1], aps[2], aps[3], aps[4], out, STOP)
    r = _run(nc, [{f"in_{k}": a for k, a in arrays.items()}], core_ids=[0])
    return r.results[0]["out"]
```

```python
import numpy as np

P = 128
S = 256
NT = S // P
D = 1024
KC = D // P
TW = 256
RING = 6
RAW = 3
SPLIT = 3
HALF = 1024
EPS = 1e-6
NEG = -1e30
D_FF, D_FFE, N_EXP = 2816, 1536, 8
G_FFN = D_FF // TW
G_EXP = D_FFE // TW
PASSES = 2
CH = 64
NCH = S // CH
DN_H, FX_H = 6, 6
LAMBDA_INIT = 0.8 - 0.6
M2_OUT_CHUNKS = (6, 7, 4, 5, 3, 2, 0, 1)
POOL_WINDOWS = (2, 4, 8, 16)

M2_SUMS = {1: 7, 3: 0, 4: 1, 5: 2, 6: 4, 8: 5, 9: 6}
M2_SUM_ORDER = [7, 0, 1, 2, 4, 5, 6]
M2_SUM_HALVES = {7: (0,), 0: (0, 1), 1: (0, 1), 2: (0, 1), 4: (1,), 5: (0, 1), 6: (0, 1)}

EV_IN, EV_OUT = 13, 4
OD_IN, OD_OUT = 18, 2
M2_IN, M2_OUT = 12, 4
SIZES = [("ev_in", EV_IN), ("ev_out", EV_OUT), ("ffn0", 3 * G_FFN), ("od_in", OD_IN), ("od_out", OD_OUT),
         ("ffn1", 3 * G_FFN), ("m0_in", M2_IN), ("m0_out", M2_OUT), ("ffn2", 3 * G_FFN), ("m1_in", M2_IN),
         ("m1_out", M2_OUT), ("moe", 3 * G_EXP * N_EXP)]
BASE = {}
N_TILES = 0
for _n, _k in SIZES:
    BASE[_n] = N_TILES
    N_TILES += _k

PRM_W = [("norm", 8 * KC), ("ba", 2), ("wa2", 256), ("gla_gain", 128), ("dq", 1), ("dk", 1), ("lq", 128), ("lk", 128),
         ("diff_gain", 128), ("odq", 1), ("odk", 1), ("conv0", 44 * 4), ("conv1", 44 * 4), ("router", KC * N_EXP)]
for _l in (0, 1):
    PRM_W += [(f"dnconv{_l}", 9 * 4), (f"alog{_l}", 1), (f"dtb{_l}", 1), (f"fb{_l}", 1), (f"onorm{_l}", 64),
              (f"fxq{_l}", 1), (f"fxk{_l}", 1), (f"poolw{_l}", 128), (f"pscale{_l}", 2)]
PRM = {}
N_PRM = 0
for _n, _k in PRM_W:
    PRM[_n] = (N_PRM, _k)
    N_PRM += _k

N_NORM = PRM["norm"][1]

CST_W = [("ident", 128), ("eps", 1), ("one", 1), ("mhalf", 1), ("blk64", 128), ("ones", 256), ("reset", 512), ("glamask", 128),
         ("cmask", 384), ("dmask", 3 * 384), ("offd", 6 * 128), ("pool", 2 * 4 * 256), ("before", 64),
         ("earlier", 128), ("iota", 128)]
CST = {}
N_CST = 0
for _n, _k in CST_W:
    CST[_n] = (N_CST, _k)
    N_CST += _k
N_FIRST = CST["blk64"][0]
N_SECOND = CST["dmask"][0]
LATE = 5
SEL_W = [("sel6", 6 * 256), ("selhp", 3 * 128)]
SEL = {}
N_SEL = 0
for _n, _k in SEL_W:
    SEL[_n] = (N_SEL, _k)
    N_SEL += _k


def constants():
    c = np.zeros((P, N_CST), np.float32)

    def put(name, a):
        o, w = CST[name]
        c[:, o:o + w] = np.asarray(a, np.float32).reshape(P, w)

    p = np.arange(P)[:, None]
    f = np.arange(P)[None, :]
    put("ident", p == f)
    put("blk64", p // 64 == f // 64)
    put("ones", np.ones((P, 256)))
    put("eps", np.full((P, 1), EPS))
    put("one", np.ones((P, 1)))
    put("mhalf", np.full((P, 1), -0.5))
    causal = np.where(f <= p, 0.0, NEG)
    zero = np.zeros((P, P))
    put("cmask", np.concatenate([causal, zero, causal], 1))
    near = (p - f)
    dm = []
    for dil in (1, 4, 16):
        diag = np.where((near >= 0) & (near % dil == 0), 0.0, NEG)
        far = np.where(((near + P) % dil == 0) & (near + P <= 128 * dil), 0.0, NEG)
        dm.append(np.concatenate([diag, far, diag], 1))
    put("dmask", np.stack(dm, 1))
    same = p // CH == f // CH
    put("glamask", same & (f >= p))
    off = []
    for b in (1, 2, 4, 8, 16, 32):
        off.append((f // (2 * b) == p // (2 * b)) & (f % (2 * b) >= b) & (p % (2 * b) < b))
    put("offd", np.stack(off, 1))
    put("reset", np.broadcast_to(np.arange(512) % CH != 0, (P, 512)))
    pool = np.zeros((P, 2, 4, 256))
    for g, w in enumerate(POOL_WINDOWS):
        for tt in range(2):
            src = tt * P + np.arange(P)[:, None]
            dst = np.arange(256)[None, :]
            pool[:, tt, g] = ((dst - src >= 0) & (dst - src < w)) / np.minimum(dst + 1, w) - (src == dst)
    put("pool", pool)
    put("before", np.broadcast_to((np.arange(8)[None, :] < np.arange(8)[:, None]).reshape(1, 64), (P, 64)))
    put("earlier", p < f)
    put("iota", np.broadcast_to(f, (P, P)))
    s = np.zeros((8, N_SEL), np.float32)
    o = SEL["sel6"][0]
    for h in range(6):
        s[h, o + h * 256:o + (h + 1) * 256] = 1
    o = SEL["selhp"][0]
    for h in range(6):
        s[h, o + (h // 2) * 128 + (h % 2) * 64:o + (h // 2) * 128 + (h % 2) * 64 + 64] = 1
    return c, s


def build(nc, w_dram, x_dram, prm_dram, cst_dram, sel_dram, out_dram, stop=None):
    import concourse.bass as bass
    from concourse import mybir
    F32 = mybir.dt.float32
    F32R = mybir.dt.float32r
    ALU = mybir.AluOpType
    ACT = mybir.ActivationFunctionType
    AX = mybir.AxisListType
    ADD, SUB, MUL, MAX, MIN = ALU.add, ALU.subtract, ALU.mult, ALU.max, ALU.min

    X = nc.alloc_sbuf_tensor("X", [P, NT, D], F32)
    HN = nc.alloc_sbuf_tensor("HN", [P, NT, D], F32)
    HT = nc.alloc_sbuf_tensor("HT", [P, KC, S], F32)
    ht_at = nc.sbuf_base - 4 * KC * S
    HTL = nc.alloc_sbuf_tensor("HTL", [P, KC, S], F32R)
    htl_at = nc.sbuf_base - 4 * KC * S
    W = nc.alloc_sbuf_tensor("W", [P, RING, KC * TW], F32)
    mw_at = nc.sbuf_base - 4 * (RING - RAW) * KC * TW
    PR = nc.alloc_sbuf_tensor("PR", [P, N_PRM], F32)
    CS = nc.alloc_sbuf_tensor("CS", [P, N_CST], F32)
    SL = nc.alloc_sbuf_tensor("SL", [8, N_SEL], F32)
    ST_ = nc.alloc_sbuf_tensor("STAT", [P, 640], F32)
    ARENA_N = 21632
    AR = nc.alloc_sbuf_tensor("ARENA", [P, ARENA_N], F32)
    arena_at = nc.sbuf_base - 4 * ARENA_N
    HTH = nc.alloc_sbuf_tensor_at("HTH", [P, KC, S], F32R, offset=ht_at)
    MWH = nc.alloc_sbuf_tensor_at("MWH", [P, SPLIT, HALF], F32R, offset=mw_at)
    MWL = nc.alloc_sbuf_tensor_at("MWL", [P, SPLIT, HALF], F32R, offset=mw_at + 4 * SPLIT * HALF)
    assert 2 * SPLIT * HALF <= (RING - RAW) * KC * TW
    ff_n = 4 * 2 * 512
    gh_n, wh_n = 2 * 512, SPLIT * KC * TW
    assert ff_n + 2 * gh_n + 2 * wh_n <= ARENA_N
    GHH = nc.alloc_sbuf_tensor_at("GHH", [P, 2, 2, S], F32R, offset=arena_at + 4 * ff_n)
    GHL = nc.alloc_sbuf_tensor_at("GHL", [P, 2, 2, S], F32R, offset=arena_at + 4 * (ff_n + gh_n))
    WH = nc.alloc_sbuf_tensor_at("WH", [P, SPLIT, KC * TW], F32R, offset=arena_at + 4 * (ff_n + 2 * gh_n))
    WL = nc.alloc_sbuf_tensor_at("WL", [P, SPLIT, KC * TW], F32R, offset=arena_at + 4 * (ff_n + 2 * gh_n + wh_n))
    HNH = nc.alloc_sbuf_tensor_at("HNH", [P, NT, D], F32R, offset=ht_at)
    HNL = nc.alloc_sbuf_tensor_at("HNL", [P, NT, D], F32R, offset=htl_at)
    DH = nc.alloc_sbuf_tensor_at("DH", [P, 2, D], F32R, offset=ht_at)
    DL = nc.alloc_sbuf_tensor_at("DL", [P, 2, D], F32R, offset=htl_at)
    sel_n, gr_n = NT * N_EXP * P, 2 * 256
    SELR = nc.alloc_sbuf_tensor_at("SELR", [P, NT, N_EXP, P], F32R, offset=arena_at)
    GRH = nc.alloc_sbuf_tensor_at("GRH", [P, 2, 256], F32R, offset=arena_at + 4 * sel_n)
    GRL = nc.alloc_sbuf_tensor_at("GRL", [P, 2, 256], F32R, offset=arena_at + 4 * (sel_n + gr_n))
    PS = [nc.alloc_psum_tensor(f"PS{b}", [P, 512], F32) for b in range(8)]

    def prm(name):
        o, w = PRM[name]
        return PR[:, o:o + w]

    def cst(name):
        o, w = CST[name]
        return CS[:, o:o + w]

    def sel(name):
        o, w = SEL[name]
        return SL[:, o:o + w]

    class Carve:
        def __init__(self):
            self.at = 0

        def __call__(self, n):
            self.at += n
            assert self.at <= ARENA_N, self.at
            return AR[:, self.at - n:self.at]

    class Stats:
        at = 0

        @classmethod
        def get(cls, n):
            cls.at += n
            assert cls.at <= 640, cls.at
            return ST_[:, cls.at - n:cls.at]

    Stats.at = 0
    ident, ones, blk64 = cst("ident"), cst("ones")[:, 0:P], cst("blk64")
    eps, one, mhalf = cst("eps"), cst("one"), cst("mhalf")

    sems = {}

    def sem(name):
        if name not in sems:
            sems[name] = nc.alloc_semaphore(name)
        return sems[name]

    w_full = [sem(f"w_full{i}") for i in range(RING)]
    w_used = sem("w_used")
    full = [sem(f"bank_full{b}") for b in range(8)]
    free = [sem(f"bank_free{b}") for b in range(8)]
    s_in = [sem(f"x_in{t}") for t in range(NT)]
    s_const, s_prm, s_late, s_out = sem("const_in"), sem("params_in"), sem("late_const_in"), sem("out_done")

    uses = {}
    n_use = [0] * 8
    n_full = [0] * 8

    def plan(key, bank, tile=None):
        if tile is None:
            n_full[bank] += 1
            uses[key] = (bank, n_use[bank], full[bank], n_full[bank])
        else:
            uses[key] = (bank, n_use[bank], w_used, tile + 1)
        n_use[bank] += 1

    class Rot:
        def __init__(self, banks):
            self.banks, self.k = banks, 0

        def __call__(self, key, tile=None):
            plan(key, self.banks[self.k % len(self.banks)], tile)
            self.k += 1

    def bank(key):
        return PS[uses[key][0]]

    def await_full(eng, key):
        eng.wait_ge(uses[key][2], uses[key][3])

    def release(ins, key):
        ins.then_inc(free[uses[key][0]], 1)

    def await_free_of(eng, key):
        eng.wait_ge(free[uses[key][0]], uses[key][1] + 1)

    def claim(pe, key):
        b, k = uses[key][:2]
        if k:
            pe.wait_ge(free[b], k)

    def plan_norm(n):
        for b in range(4):
            plan(("norm", n, b), 4 + b)

    def plan_y(n, tile):
        for b in range(4):
            plan(("y", n, b), b, tile if b == 3 else None)

    def plan_attn_step(i, name, heads, groups, combine, rot, parts="st"):
        if i < heads and "s" in parts:
            for c in range(combine):
                for g in range(groups):
                    rot((name, "s", i * combine + c, g))
        if 1 <= i <= heads and "t" in parts:
            for g in range(groups):
                rot((name, "t", i - 1, g))

    def plan_attn(name, heads, groups, combine, rot):
        for i in range(heads + 2):
            plan_attn_step(i, name, heads, groups, combine, rot)

    def plan_out_t(name, chunks, rot):
        for j in range((chunks + 1) // 2):
            rot((name, "oT", j))

    def plan_even():
        t0 = BASE["ev_in"]
        rot = Rot([0, 1, 2, 3, 4, 5, 6, 7])
        rot(("ev", "ar"), t0)
        rot(("ev", "aq"), t0 + 1)
        rot(("ev", "ak"), t0 + 2)
        rot(("ev", "la"))
        for j in range(2):
            rot(("ev", "av", j), t0 + 3 + j)
        for j in range(2):
            rot(("ev", "ag", j), t0 + 5 + j)
        for j in range(4):
            rot(("ev", "bqk", j), t0 + 7 + j)
            if j:
                rot(("ev", "ss", j - 1))
            if j == 0:
                rot(("ev", "kwT"))
                for r in range(2):
                    rot(("ev", "att", r))
            if j == 1:
                for n in range(NCH - 1):
                    rot(("ev", "kv", n))
            if j == 3:
                for t in range(NT):
                    rot(("ev", "o", t))
        plan_attn_step(0, "evd", 4, 1, 2, rot)
        rot(("ev", "bv", 0), t0 + 11)
        rot(("ev", "ss", 3))
        for c, k in enumerate((("ev", "ss", 2), ("evd", "s", 0, 0))):
            plan(("evd", "s", 2 + c, 0), uses[k][0])
        plan(("ev", "bv", 1), uses[("evd", "s", 1, 0)][0], t0 + 12)
        for n in range(NT):
            plan(("evd", "o", n), 4 + n)
        rot = Rot([0, 1, 2, 3])
        for i in range(1, 6):
            if i == 2:
                for j in range(2):
                    plan(("ev", "oT", j), 6 + j)
            if i == 3:
                rot = Rot([6, 7])
            plan_attn_step(i, "evd", 4, 1, 2, rot, "t" if i == 1 else "st")
        for j in range(2, 4):
            rot(("ev", "oT", j))
        plan_y("ev", BASE["ev_out"] + EV_OUT - 1)

    def plan_odd():
        t0 = BASE["od_in"]
        rot = Rot([0, 1, 2, 3, 4, 5, 6, 7])
        for g in range(3):
            for j in range(4):
                rot(("od", "qk", g, j), t0 + 6 * g + j)
                if j:
                    rot(("od", "ss", g, j - 1))
            rot(("od", "v", g, 0), t0 + 6 * g + 4)
            rot(("od", "ss", g, 3))
            rot(("od", "v", g, 1), t0 + 6 * g + 5)
        for n in range(NT):
            plan(("od", "o", n), n)
        plan_attn("od", 4, 3, 1, Rot([2, 3, 4, 5, 6, 7]))
        plan_out_t("od", 4, Rot([4, 5, 6, 7]))
        plan_y("od", BASE["od_out"] + OD_OUT - 1)

    GD_STEPS = 5
    M2_OT = [(4, 5), (3,), (0, 1), (2,)]
    PAIRS = [(t, h) for r in range(2) for t in range(NT) for h in range(r, 6, 2)]

    def plan_m2(m):
        t0 = BASE[f"{m}_in"]
        rot = Rot([0, 1, 2, 3, 4, 5, 6, 7])
        rot((m, "in", 7), t0)
        for j in range(M2_IN - 1):
            jj = j if j < 7 else j + 1
            rot((m, "in", jj), t0 + 1 + j)
            if jj in M2_SUMS:
                rot((m, "ss", M2_SUMS[jj]))
        rot((m, "py"))
        rot((m, "pz"))
        rot((m, "rowT"))
        for j in range(2):
            rot((m, "gb", j))
        for j in range(2):
            rot((m, "bb", j))
        for t in range(NT):
            rot((m, "kT", t))
        for t in range(NT):
            rot((m, "vT", t))
        for q in range(3):
            rot((m, "dec", q))
        for q in range(3):
            rot((m, "qk", q))
        for q in range(3):
            rot((m, "kk", q))
        fx = (m + "f", FX_H, 1, 1)
        for n in range(NT):
            plan((m + "f", "o", n), 2 + n)
        rot = Rot([0, 1, 4, 5, 6, 7])
        for s in range(GD_STEPS + 1):
            for q in range(3):
                rot((m, "M", s, q))
            plan_attn_step(s, *fx, rot)
            for q in range(3 if s else 0):
                if s < GD_STEPS:
                    rot((m, "X", s, q))
                rot((m, "Y", s, q))
        rot = Rot([6, 7])
        for t in range(NT):
            rot((m, "u", t))
            rot((m, "w", t))
        plan_attn_step(GD_STEPS + 1, *fx, rot)
        for t in range(NT):
            plan((m, "o", t), 4 + t)
        for n in range(NCH):
            if n:
                rot((m, "vp", n))
            if n < NCH - 1:
                rot((m, "kv", n))
            if n == 2:
                for j in range(2):
                    rot((m, "oT", j))
            if n == 0:
                plan_attn_step(GD_STEPS + 2, *fx, rot)
        for j in range(2, 4):
            rot((m, "oT", j))
        plan_y(m, BASE[f"{m}_out"] + M2_OUT - 1)

    ffn_k0 = {}

    def plan_ffn(n, groups):
        ffn_k0[n] = list(n_use)
        for g in range(groups):
            n_use[4 + 2 * (g % 2)] += 1
            n_use[5 + 2 * (g % 2)] += 1
        plan_y(n, BASE[n] + 3 * groups - 1)

    MOE_GROUPS = G_EXP * N_EXP
    MOE_TILES = 3 * MOE_GROUPS
    moe_name = ["moe", "moe_more"]

    def plan_moe(p):
        rot = Rot([4, 5, 6, 7])
        for j in range(16):
            rot(("moe", p, "gx", j))
        for j in range(4):
            rot(("moe", p, "selT", j))
        for b in range(4):
            plan(("y", moe_name[p], b), b)
        ffn_k0[moe_name[p]] = list(n_use)
        for b in (6, 7):
            n_use[b] += MOE_GROUPS // 2
        for b in (4, 5):
            n_use[b] += N_EXP

    order = [("norm", 0), ("even",), ("norm", 1), ("ffn", "ffn0", G_FFN, "conv"),
             ("norm", 2), ("odd",), ("norm", 3), ("ffn", "ffn1", G_FFN, "conv"),
             ("norm", 4), ("m2", "m0", 0), ("norm", 5), ("ffn", "ffn2", G_FFN, "glu"),
             ("norm", 6), ("m2", "m1", 1), ("norm", 7), ("router",), ("moe",)]
    if stop is not None:
        order = order[:stop]
    for st in order:
        if st[0] == "norm":
            plan_norm(st[1])
        elif st[0] == "even":
            plan_even()
        elif st[0] == "odd":
            plan_odd()
        elif st[0] == "m2":
            plan_m2(st[1])
        elif st[0] == "router":
            plan(("router", "logits"), 4)
            plan(("router", "place"), 5)
        elif st[0] == "moe":
            for p in range(PASSES):
                plan_moe(p)
        else:
            plan_ffn(st[1], st[2])
    n_tiles = N_TILES
    last_stage = order[-1]
    if stop is not None and last_stage[0] != "moe":
        n_tiles = {"even": BASE["ffn0"], "odd": BASE["ffn1"]}.get(last_stage[0])
        if n_tiles is None:
            names = [n for n, _ in SIZES]
            if last_stage[0] == "m2":
                n_tiles = BASE[last_stage[1] + "_out"] + M2_OUT
            elif last_stage[0] == "ffn":
                k = names.index(last_stage[1])
                n_tiles = BASE[names[k]] + SIZES[k][1]

    def v3(ap, a):
        return ap.rearrange("p (a b) -> p a b", a=a)

    class NS:
        pass

    ev = NS()
    a = Carve()
    ev.arT = a(256)
    ev.T1, ev.MN, ev.B, ev.EB, ev.ENB, ev.EW, ev.QD, ev.KD, ev.KW = [a(512) for _ in range(9)]
    ev.KWT = v3(a(512), 2)
    ev.V = v3(a(1024), 2)
    ev.GG = v3(a(1024), 2)
    ev.ATT = v3(a(1024), 8)
    ev.ST = a(3 * 512).rearrange("p (n c r v) -> p n c r v", n=3, c=2, r=2)
    ev.SQ = v3(a(1024), 2)
    ev.RS = v3(a(1024), 2)
    ev.QK = a(2048).rearrange("p (j c t) -> p j c t", j=4, c=2)
    ev.BV = v3(a(1024), 2)
    ev.SM = a(2 * 384).rearrange("p (u g k) -> p u g k", u=2, g=1)
    ev.EX = a(4 * 384).rearrange("p (u g k) -> p u g k", u=4, g=1)
    ev.OSQ = v3(a(1024), 2)
    ev.WC = a(2 * 384).rearrange("p (u g k) -> p u g k", u=2, g=1)
    ev.PT = a(2 * 384).rearrange("p (u g k) -> p u g k", u=2, g=1)
    od = NS()
    a = Carve()
    od.QK = a(24 * 256).rearrange("p (g j c t) -> p g j c t", g=3, j=4, c=2)
    od.V = a(3 * 1024).rearrange("p (g t n) -> p g t n", g=3, t=2)
    od.SQ = v3(a(1024), 2)
    od.RS = v3(a(1024), 2)
    od.SM = a(2 * 1152).rearrange("p (u g k) -> p u g k", u=2, g=3)
    od.EX = a(2 * 1152).rearrange("p (u g k) -> p u g k", u=2, g=3)
    od.PT = a(2 * 1152).rearrange("p (u g k) -> p u g k", u=2, g=3)
    m2 = NS()
    a = Carve()
    Yf = a(9 * 256)
    m2.Y = v3(Yf, 9)
    QKNf = a(6 * 256)
    m2.QKN = v3(QKNf, 6)
    m2.QD = v3(a(768), 3)
    KBf = a(768)
    m2.KB = v3(KBf, 3)
    m2.EGB = v3(a(768), 3)
    KBGf = a(768)
    m2.KBG = v3(KBGf, 2)
    m2.KDEC = v3(a(768), 2)
    m2.VB = v3(a(768), 2)
    m2.FQK = v3(a(1536), 6)
    m2.FV = v3(a(768), 2)
    m2.ZG = v3(a(768), 2)
    m2.DEC = v3(a(1536), 12)
    m2.OF = m2.DEC
    m2.AT = v3(a(1536), 12)
    m2.ATQ = v3(a(1536), 12)
    DIf, M1f = a(1536), a(1536)
    m2.DI, m2.M1 = v3(DIf, 12), v3(M1f, 12)
    UIf = a(1536)
    m2.UI = v3(UIf, 12)
    m2.SQ = v3(UIf[:, 0:1024], 2)
    m2.RS = v3(DIf[:, 0:1024], 2)
    m2.S = a(768).rearrange("p (b c v) -> p b c v", b=2, c=3)
    m2.SN = v3(Yf[:, 1536:1920], 3)
    m2.OSQ = v3(KBf, 2)
    m2.XP = v3(KBGf[:, 0:512], 2)
    m2.ROW = HN[0:8, 0, :].rearrange("p (r t) -> p r t", t=256)
    m2.ROW2 = HN[0:8, 1, :].rearrange("p (r t) -> p r t", t=256)
    m2.WT = Yf[:, 0:768].rearrange("p (c t) -> p c t", c=3)
    m2.UU = Yf[:, 768:1536].rearrange("p (t n) -> p t n", t=2)
    m2.PX = M1f[:, 0:512].rearrange("p (c t) -> p c t", c=2)
    m2.SM = QKNf[:, 0:768].rearrange("p (u g k) -> p u g k", u=2, g=1)
    m2.PT = QKNf[:, 768:1536].rearrange("p (u g k) -> p u g k", u=2, g=1)
    m2.EX = KBf.rearrange("p (u g k) -> p u g k", u=2, g=1)
    ff = NS()
    a = Carve()
    ff.GH = a(2 * 512).rearrange("p (b c t) -> p b c t", b=2, c=2)
    ff.SG = a(2 * 512).rearrange("p (b c t) -> p b c t", b=2, c=2)
    ff.YG = a(2 * 512).rearrange("p (b c t) -> p b c t", b=2, c=2)
    ff.YV = a(2 * 512).rearrange("p (b c t) -> p b c t", b=2, c=2)
    mo = NS()
    a = Carve()
    a(sel_n + 2 * gr_n)
    mo.GH = a(2 * 256).rearrange("p (b n) -> p b n", b=2)
    mo.SG = a(2 * 256).rearrange("p (b n) -> p b n", b=2)
    mo.YE = a(D)
    mo.XG = a(KC * N_EXP * P).rearrange("p (k e s) -> p k e s", k=KC, e=N_EXP)
    mo.GSEL = a(NT * N_EXP * P).rearrange("p (t e s) -> p t e s", t=NT, e=N_EXP)
    mo.SELT = a(N_EXP * S).rearrange("p (e t) -> p e t", e=N_EXP)
    mo.GS = a(S)
    mo.LG, mo.EX, mo.PB, mo.MASK, mo.GATE, mo.POS = [a(16) for _ in range(6)]
    mo.GTR, mo.EQ = a(128), a(128)
    mo.MOST = a(1)

    MORE = nc.alloc_sbuf_tensor("MORE", [1, 1], mybir.dt.int32)

    st_ss, st_rs = Stats.get(2), Stats.get(2)
    st_gain = Stats.get(4)
    st_lam, st_nlam = Stats.get(2), Stats.get(1)
    st_lamp, st_dg = Stats.get(128), Stats.get(128)
    st_nea = Stats.get(2)
    st_o, st_or = Stats.get(16), Stats.get(16)
    st_mx, st_sum, st_ri = Stats.get(24), Stats.get(24), Stats.get(24)
    st_rl = Stats.get(2)
    st_tm = Stats.get(36).rearrange("p (t j h) -> p t j h", t=2, j=3)
    st_gc = Stats.get(24).rearrange("p (t j h) -> p t j h", t=2, j=2)
    st_beg = Stats.get(12).rearrange("p (t h) -> p t h", t=2)

    def bc(ap, axis, n):
        ap = ap.unsqueeze(axis)
        shape = list(ap.shape)
        shape[axis] = n
        return ap.broadcast_to(shape)

    def bank4(key, n=4):
        return bank(key)[:, 0:n * P].rearrange("p (a b) -> p a b", a=n)

    y_names = {"even": "ev", "odd": "od"}
    resid_of = {}
    prev = None
    for st in order:
        if st[0] == "norm":
            resid_of[st[1]] = prev
        elif st[0] != "router":
            prev = y_names.get(st[0], st[1] if len(st) > 1 else st[0])
    last_resid = prev

    ffn_of_norm = {1: "ffn0", 3: "ffn1", 5: "ffn2"}
    mixer_of_norm = {0: "ev", 2: "od", 4: "m0", 6: "m1"}
    norm_after = {"ev": 1, "ffn0": 2, "od": 3, "ffn1": 4, "m0": 5, "ffn2": 6, "m1": 7}
    prev_mixer = {"ffn0": "ev", "ffn1": "od", "ffn2": "m0"}
    EARLY = 2
    MOE0 = BASE["moe"]
    MOE_SLOTS = [(MOE0 + k) % RAW for k in range(RAW)] + [k for k in range(RAW, RING)]

    def raw_slot(t):
        return t % RAW if t < MOE0 else MOE_SLOTS[(t - MOE0) % RING]

    def raw_count(t):
        if t < MOE0:
            return t // RAW + 1
        sl = raw_slot(t)
        return (len(range(sl, MOE0, RAW)) if sl < RAW else 0) + (t - MOE0) // RING + 1

    def await_raw(eng, t, more=0):
        eng.wait_ge(w_full[raw_slot(t)], 16 * raw_count(t) + 16 * more)

    mixer_tiles = {"ev": EV_IN + EV_OUT, "od": OD_IN + OD_OUT, "m0": M2_IN + M2_OUT, "m1": M2_IN + M2_OUT}
    firsts_before = {}
    _n = 0
    for _name in ("ev", "od", "m0", "m1"):
        firsts_before[_name] = _n
        _n += mixer_tiles[_name]
    half_used = sem("half_used")

    class Feeder:
        def __init__(self, name, emit):
            self.name, self.emit, self.h = name, emit, 0

        def __call__(self, upto):
            while self.h <= min(upto, 2 * mixer_tiles[self.name] - 1):
                self.emit(self.name, self.h)
                self.h += 1

    hi_done, lo_done = sem("hi_done"), sem("lo_done")

    def half_ap(name, h):
        t = BASE[name + "_in"] + h // 2
        return W[:, raw_slot(t), (h % 2) * HALF:(h % 2 + 1) * HALF]

    def tile_ap(t):
        return W[:, raw_slot(t), :]

    def in_tile(t):
        return tile_ap(t).rearrange("p (k n) -> p k n", k=KC)

    def out_tile(t):
        return tile_ap(t).rearrange("p (c n) -> p c n", c=2)

    def more_tokens(eng):
        eng.wait_ge(sem("more"), 1)
        return eng.value_load(MORE[0:1, 0:1], min_val=0, max_val=1)

    def moe_loop(eng, group, expert_out, w0):
        group(0, 0, True)
        group(1, 0)
        with eng.Fori(0, N_EXP - 1) as i:
            for gs in range(2, 2 + G_EXP):
                group(gs, i)
                if gs == G_EXP:
                    expert_out(0, i, w0 + 3 * (G_EXP - 1) + 4)
        for gs in range(2 + (N_EXP - 1) * G_EXP, MOE_GROUPS):
            group(gs, 0)
        expert_out(N_EXP - 1, 0, w0 + MOE_TILES - 1)

    block = nc.Block()
    block.__enter__()

    @block.sync
    def _(sp):
        x_tiles = x_dram.rearrange("b (t p) d -> p (b t) d", p=P)
        for t in range(NT):
            sp.dma_start(X[:, t, :], x_tiles[:, t, :]).then_inc(s_in[t], 16)
        sp.dma_start(CS[:, 0:N_FIRST], cst_dram[:, 0:N_FIRST]).then_inc(s_const, 16)
        sp.dma_start(PR[:, 0:N_NORM], prm_dram[:, 0:N_NORM]).then_inc(s_const, 16)

        def load(t, slot):
            src = w_dram[t] if isinstance(t, int) else w_dram[bass.ds(t, 1), :, :].rearrange("a p n -> (a p) n")
            sp.dma_start(W[:, slot, :], src).then_inc(w_full[slot], 16)

        for t in range(RAW):
            load(t, t)
            if t == 0:
                sp.dma_start(PR[:, N_NORM:N_PRM], prm_dram[:, N_NORM:N_PRM]).then_inc(s_prm, 16)
                sp.dma_start(CS[:, N_FIRST:N_SECOND], cst_dram[:, N_FIRST:N_SECOND]).then_inc(s_prm, 16)
        n_split = min(n_tiles, MOE0)
        rounds = (n_split - RAW) // RAW
        with sp.Fori(0, rounds) as i:
            for u in range(RAW):
                sp.wait_ge(lo_done, 2 * RAW * i + 2 * (u + 1))
                load(RAW * i + (RAW + u), u)
        for t in range(RAW * (rounds + 1), n_split):
            sp.wait_ge(lo_done, 2 * (t - RAW + 1))
            load(t, raw_slot(t))

        def load_experts(p):
            t0 = MOE0 + p * MOE_TILES
            for t in range(t0, t0 + RING if not p else t0):
                if raw_slot(t) < RAW:
                    sp.wait_ge(lo_done, 2 * (t - RAW + 1))
                else:
                    sp.wait_ge(w_used, MOE0)
                load(t, raw_slot(t))
            first = 0 if p else RING
            with sp.Fori(0, (MOE_TILES - first) // RING) as i:
                for u in range(RING):
                    sp.wait_ge(w_used, RING * i + (t0 + first + u - RING + 1))
                    load(RING * i + (MOE0 + first + u), raw_slot(t0 + first + u))

        if n_tiles > MOE0:
            load_experts(0)
        for b in range(4):
            await_free_of(sp, ("y", last_resid, b))
        if last_resid == "moe":
            with sp.If(more_tokens(sp) > 0):
                load_experts(1)
                for b in range(4):
                    await_free_of(sp, ("y", moe_name[1], b))
        sp.dma_start(out_dram.rearrange("b (t p) d -> p (b t) d", p=P), X[:, :, :]).then_inc(s_out, 16)
        sp.wait_ge(s_out, 16)

    @block.gpsimd
    def _(pool):
        offd = v3(cst("offd"), 6)

        def norm(n):
            if n == 0:
                pool.wait_ge(s_const, 32)
            for t in range(NT):
                pool.wait_ge(sem("mean_sq"), NT * n + t + 1)
                if n:
                    pool.wait_ge(sem("hn"), NT * (n - 1) + t + 1)
                pool.tensor_tensor(st_ss[:, t:t + 1], st_ss[:, t:t + 1], eps, ADD).then_inc(sem("mean_eps"), 1)
                pool.wait_ge(sem("mean_eps"), NT * n + t + 1)
                pool.tensor_tensor(st_rs[:, t:t + 1], st_ss[:, t:t + 1], mhalf, ALU.pow).then_inc(sem("rstd"), 1)

        def late_constants():
            cut = [N_SECOND + (N_CST - N_SECOND) * k // LATE for k in range(LATE + 1)]
            for k in range(LATE):
                pool.wait_ge(w_used, 2 * (k + 1))
                pool.dma_start(CS[:, cut[k]:cut[k + 1]], cst_dram[:, cut[k]:cut[k + 1]]).then_inc(s_late, 16)
            pool.dma_start(SL[:, :], sel_dram).then_inc(s_late, 16)
            pool.wait_ge(s_late, 16 * (LATE + 1))

        def mixer2(m):
            for s in range(1, GD_STEPS + 1):
                if s == 1:
                    pool.wait_ge(sem(m + "_ui"), 1)
                for q in range(3):
                    await_full(pool, (m, "M", s - 1, q))
                    z = slice(4 * q, 4 * q + 4)
                    pool.tensor_tensor(m2.OF[:, z, :], m2.AT[:, z, :], bc(offd[:, s, :], 1, 4), MUL).then_inc(sem(m + "_of"), 1)
                for q in range(3 if s == 1 else 0):
                    await_free_of(pool, (m, "qk", q))
                    z = slice(4 * q, 4 * q + 4)
                    pool.tensor_tensor(m2.ATQ[:, z, :], m2.ATQ[:, z, :], bc(cst("glamask"), 1, 4), MUL).then_inc(sem(m + "_atq"), 1)

        for st in order:
            if st[0] == "norm":
                norm(st[1])
                if st[1] == 0:
                    late_constants()
            elif st[0] == "m2":
                mixer2(st[1])

    @block.tensor
    def _(pe):
        mm = pe.matmul

        fences = [0]

        def fence(ins):
            fences[0] += 1
            ins.then_inc(sem("pe_fence"), 1)
            pe.wait_ge(sem("pe_fence"), fences[0])

        def products(out, wt_first, name, h, wc, act, ac, start, stop):
            for n, (wt, ht) in enumerate(((MWH, HTH), (MWH, HTL), (MWL, HTH)) if wt_first else ((MWH, HTH), (MWL, HTH), (MWH, HTL))):
                w, a = wt[:, h % SPLIT, wc], ht[:, act, ac]
                ins = mm(out, w if wt_first else a, a if wt_first else w, start=(start and n == 0), stop=(stop and n == 2),
                         skip_group_check=True)
            return ins

        def await_half(name, h):
            pe.wait_ge(lo_done, 2 * BASE[name + "_in"] + h + 1)

        def norm(n):
            for b in range(4):
                claim(pe, ("norm", n, b))
            for t in range(NT):
                pe.wait_ge(sem("hn"), NT * n + t + 1)
                for b in range(4):
                    for k in range(2):
                        c = 2 * b + k
                        ins = pe.transpose(bank(("norm", n, b))[:, k * 256 + t * P:k * 256 + (t + 1) * P],
                                           HN[:, t, c * P:(c + 1) * P], ident)
                    if t == NT - 1:
                        done(ins, ("norm", n, b))

        def hT_ready(n):
            for b in range(4):
                await_free_of(pe, ("norm", n, b))

        def in_channel(name, j, key, units=2):
            claim(pe, key)
            for hf in range(2):
                h = 2 * j + hf
                if j == 0:
                    n = [n for n in mixer_of_norm if mixer_of_norm[n] == name][0]
                    for b in (2 * hf, 2 * hf + 1):
                        await_free_of(pe, ("norm", n, b))
                await_half(name, h)
                for c in range(units):
                    for k in range(KC // 2):
                        o = k * TW + c * P
                        ins = products(bank(key)[:, c * 256:(c + 1) * 256], True, name, h, slice(o, o + P), 4 * hf + k, slice(0, S),
                                       hf == 0 and c == 0 and k == 0, hf == 1 and k == KC // 2 - 1)
                ins.then_inc(w_used if hf else half_used, 1)

        def in_token(name, j, key):
            claim(pe, key)
            for hf in range(2):
                h = 2 * j + hf
                await_half(name, h)
                for tt in range(NT):
                    for k in range(KC // 2):
                        ins = products(bank(key)[:, tt * 256:(tt + 1) * 256], False, name, h, slice(k * TW, (k + 1) * TW), 4 * hf + k,
                                       slice(tt * P, (tt + 1) * P), hf == 0 and tt == 0 and k == 0, hf == 1 and k == KC // 2 - 1)
                ins.then_inc(w_used if hf else half_used, 1)

        def done(ins, key):
            ins.then_inc(uses[key][2], 1)

        def sums(key, sq, sqname, n, mat, o=0, w=512):
            claim(pe, key)
            pe.wait_ge(sem(sqname), n)
            done(mm(bank(key)[:, o:o + w], mat, sq[:, o:o + w], start=True, stop=True), key)

        def attn_step(i, name, heads, groups, combine, scores, src, values, dv, parts="stv"):
            if i < heads and "s" in parts:
                for c in range(combine):
                    u = i * combine + c
                    for g in range(groups):
                        key = (name, "s", u, g)
                        claim(pe, key)
                        done(scores(bank(key), u, g), key)
            if 1 <= i <= heads and "t" in parts:
                h = i - 1
                pe.wait_ge(sem(name + ("_w" if combine > 1 else "_e")), h + 1)
                for g in range(groups):
                    key = (name, "t", h, g)
                    claim(pe, key)
                    for b in range(3):
                        ins = pe.transpose(bank(key)[:, b * P:(b + 1) * P], src[:, h % 2, g, b * P:(b + 1) * P], ident)
                    done(ins, key)
            if i >= 2 and "v" in parts:
                h = i - 2
                for g in range(groups):
                    await_free_of(pe, (name, "t", h, g))
                if h == 0:
                    for n in range(NT):
                        claim(pe, (name, "o", n))
                for n in range(NT):
                    o = bank((name, "o", n))[:, h * dv:(h + 1) * dv]
                    steps = [(g, kt) for g in range(groups) for kt in range(n + 1)]
                    for j, (g, kt) in enumerate(steps):
                        ins = values(o, h, g, n, kt, j == 0, j == len(steps) - 1)
                    if h == heads - 1:
                        done(ins, (name, "o", n))

        def attn(*args):
            for i in range(args[1] + 2):
                attn_step(i, *args)

        def transposed(name, j, chunks):
            key = (name, "oT", j)
            claim(pe, key)
            for k, c in enumerate(chunks):
                for t in range(NT):
                    ins = pe.transpose(bank(key)[:, k * 256 + t * P:k * 256 + (t + 1) * P], HN[:, t, c * P:(c + 1) * P], ident)
            done(ins, key)

        def out_chunk(name, i, c, first=False):
            h = 2 * (BASE[name + "_out"] - BASE[name + "_in"]) + i
            await_half(name, h)
            if first:
                for b in range(4):
                    claim(pe, ("y", name, b))
            for tt in range(NT):
                for hf in range(2):
                    ins = products(PS[2 * tt + hf][:, :], False, name, h, slice(hf * 512, (hf + 1) * 512), c,
                                   slice(tt * P, (tt + 1) * P), first, False)
            ins.then_inc(w_used if i % 2 else half_used, 1)

        def out_last_tile(name, tiles, chunks):
            h = 2 * (BASE[name + "_out"] - BASE[name + "_in"]) + 2 * tiles - 2
            await_half(name, h + 1)
            for tt in range(NT):
                for k, c in enumerate(chunks):
                    for hf in range(2):
                        ins = products(PS[2 * tt + hf][:, :], False, name, h + k, slice(hf * 512, (hf + 1) * 512), c,
                                       slice(tt * P, (tt + 1) * P), False, k == 1)
                        if k == 1 and 2 * tt + hf < 3:
                            done(ins, ("y", name, 2 * tt + hf))
                    if tt == NT - 1:
                        ins.then_inc(w_used if k else half_used, 1)

        def even():
            t0 = BASE["ev_in"]
            in_channel("ev", 0, ("ev", "ar"), units=1)
            in_channel("ev", 1, ("ev", "aq"))
            in_channel("ev", 2, ("ev", "ak"))
            claim(pe, ("ev", "la"))
            pe.wait_ge(s_prm, 32)
            await_free_of(pe, ("ev", "ar"))
            wa2 = prm("wa2")
            for c in range(2):
                ins = mm(bank(("ev", "la"))[:, c * 256:(c + 1) * 256], wa2[0:16, c * P:(c + 1) * P], ev.arT[0:16, :],
                         start=True, stop=True)
            done(ins, ("ev", "la"))
            for j in range(2):
                in_token("ev", 3 + j, ("ev", "av", j))
            for j in range(2):
                in_token("ev", 5 + j, ("ev", "ag", j))
            def gla_scores():
                key = ("ev", "kwT")
                claim(pe, key)
                await_free_of(pe, ("ev", "ak"))
                await_free_of(pe, ("ev", "aq"))
                for t in range(NT):
                    for c in range(2):
                        ins = pe.transpose(bank(key)[:, (t * 2 + c) * P:(t * 2 + c + 1) * P],
                                           ev.KW[:, c * 256 + t * P:c * 256 + (t + 1) * P], ident)
                done(ins, key)
                for r in range(2):
                    key = ("ev", "att", r)
                    claim(pe, key)
                    rp = slice(64 * r, 64 * r + 64)
                    for t in range(NT):
                        for c in range(2):
                            cc = slice(c * 256 + t * P, c * 256 + (t + 1) * P)
                            ins = mm(bank(key)[:, (2 * t + c) * P:(2 * t + c + 1) * P], ev.KD[rp, cc], ev.QD[rp, cc], start=True, stop=True)
                    done(ins, key)

            def gla_states():
                await_free_of(pe, ("ev", "kwT"))
                await_free_of(pe, ("ev", "av", 1))
                await_free_of(pe, ("ev", "av", 0))
                for n in range(NCH - 1):
                    key = ("ev", "kv", n)
                    claim(pe, key)
                    rp = slice(64 * (n % 2), 64 * (n % 2) + 64)
                    for c in range(2):
                        ins = mm(bank(key)[:, c * 256:(c + 1) * 256], ev.KWT[rp, n // 2, c * P:(c + 1) * P],
                                 ev.V[rp, n // 2, c * 256:(c + 1) * 256], start=True, stop=True)
                    done(ins, key)

            def gla_out():
                for r in range(2):
                    await_free_of(pe, ("ev", "att", r))
                for t in range(NT):
                    key = ("ev", "o", t)
                    claim(pe, key)
                    for h in range(4):
                        mm(bank(key)[:, h * P:(h + 1) * P], ev.ATT[:, 4 * (h % 2) + 2 * t + h // 2, :], ev.V[:, t, h * P:(h + 1) * P],
                           start=(h == 0), stop=False, skip_group_check=True)
                    for n in (2 * t, 2 * t + 1):
                        if n == 0:
                            continue
                        await_free_of(pe, ("ev", "kv", n - 1))
                        for c in range(2):
                            ins = mm(bank(key)[64 * (n % 2):64 * (n % 2) + 64, c * 256:(c + 1) * 256],
                                     ev.QD[:, c * 256 + n * CH:c * 256 + (n + 1) * CH],
                                     ev.ST[:, n - 1, c].rearrange("p r v -> p (r v)"), start=False, stop=(n == 2 * t + 1 and c == 1),
                                     skip_group_check=True)
                    done(ins, key)

            for j in range(4):
                in_channel("ev", 7 + j, ("ev", "bqk", j))
                if j:
                    sums(("ev", "ss", j - 1), ev.SQ[:, (j - 1) % 2, :], "ev_sq", j, blk64)
                if j != 2:
                    {0: gla_scores, 1: gla_states, 3: gla_out}[j]()
            def scores(bk, u, g):
                h, c = u // 2, u % 2
                if u % 4 == 0:
                    for j in (h, h + 1):
                        await_free_of(pe, ("ev", "bqk", j))
                r = slice(64 * c, 64 * c + 64)
                q, k = ev.QK[r, h // 2 * 2, h % 2, :], ev.QK[r, h // 2 * 2 + 1, h % 2, :]
                mm(bk[:, 0:P], q[:, 0:P], k[:, 0:P], start=True, stop=True)
                return mm(bk[:, P:P + 256], q[:, P:256], k[:, 0:256], start=True, stop=True)

            def values(o, h, g, n, kt, first, last):
                b = 0 if n == 0 else 1 + kt
                return mm(o, ev.PT[:, h % 2, 0, b * P:(b + 1) * P], ev.BV[:, kt, h * P:(h + 1) * P], start=first, stop=last)

            da = ("evd", 4, 1, 2, scores, ev.WC, values, 128)
            attn_step(0, *da)
            in_token("ev", 11, ("ev", "bv", 0))
            sums(("ev", "ss", 3), ev.SQ[:, 1, :], "ev_sq", 4, blk64)
            attn_step(1, *da, parts="s")
            in_token("ev", 12, ("ev", "bv", 1))
            attn_step(1, *da, parts="t")
            await_free_of(pe, ("ev", "bv", 0))
            await_free_of(pe, ("ev", "bv", 1))
            for t in range(NT):
                await_free_of(pe, ("ev", "o", t))
            for j in range(2):
                transposed("ev", j, (2 * j, 2 * j + 1))
            attn_step(2, *da)
            for j in range(2):
                await_free_of(pe, ("ev", "oT", j))
            for i in range(3, 6):
                attn_step(i, *da, parts="s")
                out_chunk("ev", i - 3, i - 3, first=(i == 3))
                attn_step(i, *da, parts="tv")
            out_chunk("ev", 3, 3)
            for t in range(NT):
                await_free_of(pe, ("evd", "o", t))
            for j in range(2, 4):
                transposed("ev", j, (2 * j, 2 * j + 1))
            for j in range(2, 4):
                await_free_of(pe, ("ev", "oT", j))
            for c in (4, 5):
                out_chunk("ev", c, c)
            out_last_tile("ev", EV_OUT, (6, 7))

        def odd():
            t0 = BASE["od_in"]
            pe.wait_ge(s_late, 16 * (LATE + 1))
            for g in range(3):
                for j in range(4):
                    in_channel("od", 6 * g + j, ("od", "qk", g, j))
                    if j:
                        sums(("od", "ss", g, j - 1), od.SQ[:, (j - 1) % 2, :], "od_sq", 4 * g + j, ones)
                in_token("od", 6 * g + 4, ("od", "v", g, 0))
                sums(("od", "ss", g, 3), od.SQ[:, 1, :], "od_sq", 4 * g + 4, ones)
                in_token("od", 6 * g + 5, ("od", "v", g, 1))
            for g in range(3):
                for j in range(4):
                    await_free_of(pe, ("od", "qk", g, j))
                for j in range(2):
                    await_free_of(pe, ("od", "v", g, j))

            def scores(bk, h, g):
                q, k = od.QK[:, g, h // 2, h % 2, :], od.QK[:, g, 2 + h // 2, h % 2, :]
                mm(bk[:, 0:P], q[:, 0:P], k[:, 0:P], start=True, stop=True)
                return mm(bk[:, P:P + 256], q[:, P:256], k[:, 0:256], start=True, stop=True)

            def values(o, h, g, n, kt, first, last):
                b = 0 if n == 0 else 1 + kt
                return mm(o, od.PT[:, h % 2, g, b * P:(b + 1) * P], od.V[:, g, kt, h * P:(h + 1) * P], start=first, stop=last)

            attn("od", 4, 3, 1, scores, od.EX, values, 128)
            for t in range(NT):
                await_free_of(pe, ("od", "o", t))
            for j in range(2):
                transposed("od", j, (2 * j, 2 * j + 1))
            for j in range(2):
                await_free_of(pe, ("od", "oT", j))
            out_chunk("od", 0, 0, first=True)
            out_chunk("od", 1, 1)
            out_last_tile("od", OD_OUT, (2, 3))

        def mixer2(m, l):
            t0 = BASE[f"{m}_in"]
            in_channel(m, 0, (m, "in", 7))
            for j in range(M2_IN - 1):
                jj = j if j < 7 else j + 1
                (in_channel if jj < 8 else in_token)(m, 1 + j, (m, "in", jj))
                if jj in M2_SUMS:
                    i = M2_SUMS[jj]
                    k = M2_SUM_ORDER.index(i)
                    hv = M2_SUM_HALVES[i]
                    sums((m, "ss", i), m2.SQ[:, k % 2, :], m + "_sq", k + 1, blk64, 256 * hv[0], 256 * len(hv))
            key = (m, "py")
            claim(pe, key)
            await_free_of(pe, (m, "in", 11))
            pm = cst("pool").rearrange("p (t g n) -> p t g n", t=2, g=4)
            for g in range(4):
                r = slice(64 * (g % 2), 64 * (g % 2) + 64)
                for tt in range(NT):
                    ins = mm(bank(key)[r, (g // 2) * 256:(g // 2 + 1) * 256], m2.XP[:, tt, g * 64:(g + 1) * 64],
                             pm[:, tt, g, :], start=(tt == 0), stop=(tt == NT - 1))
            done(ins, key)
            key = (m, "pz")
            claim(pe, key)
            await_free_of(pe, (m, "py"))
            pw = v3(prm(f"poolw{l}"), 2)
            for g in range(4):
                r = slice(64 * (g % 2), 64 * (g % 2) + 64)
                ins = mm(bank(key)[r, (g // 2) * 256:(g // 2 + 1) * 256], pw[r, g // 2, :], m2.PX[r, g // 2, :],
                         start=True, stop=True)
            done(ins, key)
            key = (m, "rowT")
            claim(pe, key)
            pe.wait_ge(sem(m + "_rows"), 1)
            pe.wait_ge(sem(m + "_frow"), 1)
            pe.wait_ge(sem(m + "_ra"), 4)
            G_, GL_, BT_ = m2.ROW[0:6, 0, :], m2.ROW[0:6, 1, :], m2.ROW[0:6, 2, :]
            C_, NC_ = m2.ROW2[0:6, 2, :], m2.ROW2[0:6, 3, :]
            for t in range(NT):
                for j, src in enumerate((G_, GL_, BT_, C_)):
                    ins = pe.transpose(bank(key)[:, (t * 4 + j) * 6:(t * 4 + j) * 6 + 6], src[:, t * P:(t + 1) * P], ident[0:6, 0:6])
            done(ins, key)
            hp = v3(sel("selhp"), 3)
            for name, src in (("gb", G_), ("bb", BT_)):
                for j in range(2):
                    key = (m, name, j)
                    claim(pe, key)
                    for c in range(2 - j):
                        ins = mm(bank(key)[:, c * 256:(c + 1) * 256], hp[0:6, 2 * j + c, :], src, start=True, stop=True)
                    done(ins, key)
            pe.wait_ge(sem(m + "_qk"), 1)
            pe.wait_ge(sem(m + "_v"), 2)
            for t in range(NT):
                key = (m, "kT", t)
                claim(pe, key)
                for c in range(3):
                    ins = pe.transpose(bank(key)[:, c * P:(c + 1) * P], m2.QKN[:, 3 + c, t * P:(t + 1) * P], ident)
                done(ins, key)
            for t in range(NT):
                key = (m, "vT", t)
                claim(pe, key)
                for c in range(3):
                    ins = pe.transpose(bank(key)[:, c * P:(c + 1) * P], m2.Y[:, 6 + c, t * P:(t + 1) * P], ident)
                done(ins, key)
            s6 = v3(sel("sel6"), 6)
            for q in range(3):
                key = (m, "dec", q)
                claim(pe, key)
                for i in range(4):
                    t, h = PAIRS[4 * q + i]
                    o = bank(key)[:, i * P:(i + 1) * P]
                    ins = mm(o, s6[0:6, h, 0:P], G_[:, t * P:(t + 1) * P], start=True, stop=True)
                done(ins, key)
            for name, src in (("qk", m2.QKN), ("kk", m2.KB)):
                for j in range(2 if name == "kk" else 0):
                    await_free_of(pe, (m, "bb", j))
                for q in range(3):
                    key = (m, name, q)
                    claim(pe, key)
                    for i in range(4):
                        t, h = PAIRS[4 * q + i]
                        r = slice(64 * (h % 2), 64 * (h % 2) + 64)
                        if q == 1 and i == 2:
                            fence(ins)
                        ins = mm(bank(key)[:, i * P:(i + 1) * P], m2.QKN[r, 3 + h // 2, t * P:(t + 1) * P],
                                 src[r, h // 2, t * P:(t + 1) * P], start=True, stop=True)
                    done(ins, key)
            for j in (4, 5, 6, 7):
                await_free_of(pe, (m, "in", j))
            await_free_of(pe, (m, "in", 9))
            await_free_of(pe, (m, "in", 10))

            def m2_chunk(c, **flags):
                out_chunk(m, M2_OUT_CHUNKS.index(c), c, **flags)

            def scores(bk, h, g):
                r = slice(64 * (h % 2), 64 * (h % 2) + 64)
                q, k = m2.FQK[r, h // 2, :], m2.FQK[r, 3 + h // 2, :]
                for n, (o, w) in enumerate(((0, P), (P, 256))):
                    qs = slice(n * P, (n + 1) * P)
                    mm(bk[:, o:o + w], q[:, qs], k[:, 0:w], start=True, stop=False)
                    ins = mm(bk[:, o:o + w], s6[0:6, h, 0:P], NC_[:, 0:w], start=False, stop=True)
                return ins

            def values(o, h, g, n, kt, first, last):
                b = 0 if n == 0 else 1 + kt
                return mm(o, m2.PT[:, h % 2, 0, b * P:(b + 1) * P], m2.FV[:, kt, h * 64:(h + 1) * 64], start=first, stop=last)

            fx = (m + "f", FX_H, 1, 1, scores, m2.EX, values, 64)
            for s in range(GD_STEPS + 1):
                for q in range(3):
                    key = (m, "M", s, q)
                    claim(pe, key)
                    pe.wait_ge(*((sem(m + "_of"), 3 * (s - 1) + q + 1) if s else (sem(m + "_of2"), q + 1)))
                    if s == 1:
                        await_free_of(pe, (m, "M", 0, q))
                    elif s:
                        await_free_of(pe, (m, "X", s - 1, q))
                    for i in range(4):
                        z = 4 * q + i
                        ins = mm(bank(key)[:, i * P:(i + 1) * P], m2.OF[:, z, :], ident if s == 0 else m2.DI[:, z, :],
                                 start=True, stop=True)
                    done(ins, key)
                attn_step(s, *fx)
                if s == 0:
                    continue
                for q in range(3):
                    await_free_of(pe, (m, "M", s, q))
                    if s == 1:
                        pe.wait_ge(sem(m + "_ui"), 1)
                    else:
                        await_free_of(pe, (m, "Y", s - 1, q))
                    if s < GD_STEPS:
                        key = (m, "X", s, q)
                        claim(pe, key)
                        for i in range(4):
                            z = 4 * q + i
                            ins = mm(bank(key)[:, i * P:(i + 1) * P], m2.UI[:, z, :], m2.M1[:, z, :], start=True, stop=True)
                        done(ins, key)
                    key = (m, "Y", s, q)
                    claim(pe, key)
                    for i in range(4):
                        z = 4 * q + i
                        ins = mm(bank(key)[:, i * P:(i + 1) * P], m2.M1[:, z, :], m2.UI[:, z, :], start=True, stop=True)
                    done(ins, key)
            for q in range(3):
                await_free_of(pe, (m, "Y", GD_STEPS, q))
            for t in range(NT):
                await_free_of(pe, (m, "kT", t))
                await_free_of(pe, (m, "vT", t))
            for t in range(NT):
                key = (m, "u", t)
                claim(pe, key)
                for h in range(6):
                    ins = mm(bank(key)[:, h * 64:(h + 1) * 64], m2.UI[:, PAIRS.index((t, h)), :], m2.VB[:, t, h * 64:(h + 1) * 64],
                             start=True, stop=True)
                done(ins, key)
                key = (m, "w", t)
                claim(pe, key)
                for h in range(6):
                    ins = mm(bank(key)[64 * (h % 2):64 * (h % 2) + 64, (h // 2) * P:(h // 2 + 1) * P],
                             m2.KBG[:, t, h * 64:(h + 1) * 64], m2.UI[:, PAIRS.index((t, h)), :], start=True, stop=True)
                done(ins, key)
            attn_step(GD_STEPS + 1, *fx)
            pe.wait_ge(sem(m + "_qd"), 1)
            pe.wait_ge(sem(m + "_atq"), 3)
            for n in range(NCH):
                t, p0 = n // 2, 64 * (n % 2)
                rp = slice(p0, p0 + 64)
                cols = slice(n * CH, (n + 1) * CH)
                await_free_of(pe, (m, "u", t))
                if n == 2:
                    m2_chunk(7)
                if n:
                    key = (m, "vp", n)
                    claim(pe, key)
                    await_free_of(pe, (m, "kv", n - 1))
                    await_free_of(pe, (m, "w", t))
                    for c in range(3):
                        ins = mm(bank(key)[rp, c * P:(c + 1) * P], m2.WT[:, c, cols], m2.S[:, n % 2, c, :], start=True, stop=True)
                    done(ins, key)
                key = (m, "o", t)
                if p0 == 0:
                    claim(pe, key)
                for c in range(3):
                    mm(bank(key)[rp, c * P:(c + 1) * P], m2.QD[:, c, cols], m2.S[:, n % 2, c, :], start=(c == 0), stop=False,
                       skip_group_check=True)
                if n == 1:
                    await_free_of(pe, (m, "pz"))
                    m2_chunk(6, first=True)
                if n == 3:
                    for j in range(2):
                        await_free_of(pe, (m, "oT", j))
                    m2_chunk(4)
                if n:
                    await_free_of(pe, (m, "vp", n))
                if n < NCH - 1:
                    key = (m, "kv", n)
                    claim(pe, key)
                    for c in range(3):
                        ins = mm(bank(key)[:, c * P:(c + 1) * P], m2.KDEC[rp, t, c * P:(c + 1) * P], m2.UU[rp, t, c * P:(c + 1) * P],
                                 start=True, stop=True)
                    done(ins, key)
                if n == 0:
                    attn_step(GD_STEPS + 2, *fx)
                if n == 2:
                    for k in range(NT):
                        await_free_of(pe, (m + "f", "o", k))
                    for j in range(2):
                        transposed(m, j, M2_OT[j])
                if p0:
                    key = (m, "o", t)
                    for h in range(6):
                        ins = mm(bank(key)[:, h * 64:(h + 1) * 64], m2.ATQ[:, PAIRS.index((t, h)), :], m2.UU[:, t, h * 64:(h + 1) * 64],
                                 start=False, stop=(h == 5), skip_group_check=True)
                    done(ins, key)
            m2_chunk(5)
            m2_chunk(3)
            for t in range(NT):
                await_free_of(pe, (m, "o", t))
            for j in range(2, 4):
                transposed(m, j, M2_OT[j])
            for j in range(2, 4):
                await_free_of(pe, (m, "oT", j))
            m2_chunk(2)
            out_last_tile(m, M2_OUT, M2_OUT_CHUNKS[-2:])

        def router():
            hT_ready(7)
            key = ("router", "logits")
            claim(pe, key)
            rt = v3(prm("router"), KC)
            for t in range(NT):
                for k in range(KC):
                    ins = mm(bank(key)[:, t * 8:(t + 1) * 8], HT[:, k, t * P:(t + 1) * P], rt[:, k, :],
                             start=(k == 0), stop=(k == KC - 1))
            done(ins, key)
            key = ("router", "place")
            claim(pe, key)
            pe.wait_ge(sem("chosen"), 1)
            m3 = mo.MASK.rearrange("p (t e) -> p t e", t=NT)
            earlier = cst("earlier")
            mm(bank(key)[:, 0:8], earlier, m3[:, 0, :], start=True, stop=True)
            mm(bank(key)[:, 8:16], ones, m3[:, 0, :], start=True, stop=False)
            mm(bank(key)[:, 8:16], earlier, m3[:, 1, :], start=False, stop=True)
            mm(bank(key)[:, 16:24], ones, m3[:, 0, :], start=True, stop=False)
            done(mm(bank(key)[:, 16:24], ones, m3[:, 1, :], start=False, stop=True), key)

        def moe(p):
            name = moe_name[p]
            w0, k0 = BASE["moe"] + p * MOE_TILES, ffn_k0[name]
            pe.wait_ge(sem("hn_lo"), p + 1)
            pe.wait_ge(sem("moe_sel"), p + 1)
            for c in range(KC):
                for hf in range(2):
                    key = ("moe", p, "gx", 2 * c + hf)
                    claim(pe, key)
                    for n, hn in enumerate((HNH, HNL)):
                        for t in range(NT):
                            ins = mm(bank(key)[:, :], hn[:, t, c * P:(c + 1) * P],
                                     SELR[:, t, 4 * hf:4 * hf + 4, :].rearrange("p e s -> p (e s)"),
                                     start=(n == 0 and t == 0), stop=(n == 1 and t == NT - 1))
                    done(ins, key)
            pe.wait_ge(sem("moe_gsel"), p + 1)
            for j in range(4):
                key = ("moe", p, "selT", j)
                claim(pe, key)
                for k in range(2):
                    for t in range(NT):
                        ins = pe.transpose(bank(key)[:, k * 256 + t * P:k * 256 + (t + 1) * P], mo.GSEL[:, t, 2 * j + k, :], ident)
                done(ins, key)
            for b in range(4):
                claim(pe, ("y", name, b))
                mm(PS[b][:, :], ident, X[:, b // 2, (b % 2) * 512:(b % 2 + 1) * 512], start=True, stop=False, skip_group_check=True)
            for j in range(12, 16):
                await_free_of(pe, ("moe", p, "gx", j))
            for j in range(4):
                await_free_of(pe, ("moe", p, "selT", j))

            def await_moe_tile(ts, i):
                await_raw(pe, ts, 3 * G_EXP // RING * i)

            def up(gs, i, first=False):
                b, e = 6 + gs % 2, gs // G_EXP
                pe.wait_ge(free[b], k0[b] + gs // 2 + (G_EXP // 2) * i)
                for half in range(2):
                    ts = w0 + half if first else w0 + 3 * gs - 1 + half
                    await_moe_tile(ts, i)
                    for c in range(2):
                        for kk in range(KC):
                            x = mo.XG[:, kk, e, :] if isinstance(i, int) else mo.XG[:, kk, bass.ds(i + e, 1), :].rearrange("p e s -> p (e s)")
                            o = half * 256 + c * P
                            ins = mm(PS[b][:, o:o + P], in_tile(ts)[:, kk, c * P:(c + 1) * P], x, start=(kk == 0), stop=(kk == KC - 1))
                    ins.then_inc(w_used, 1)

            def down(gs, i):
                g = MOE_GROUPS * p + gs + 1 + G_EXP * i
                pe.wait_ge(sem("moe_lo"), g)
                pe.wait_ge(sem("moe_gl"), g)
                if gs % G_EXP == 0:
                    for b in (4, 5):
                        pe.wait_ge(free[b], k0[b] + gs // G_EXP + i)
                for c in range(2):
                    for n, (gh, wt) in enumerate(((GRH, DH), (GRH, DL), (GRL, DH))):
                        for hf in range(2):
                            ins = mm(PS[4 + hf][:, :], gh[:, gs % 2, c * P:(c + 1) * P], wt[:, c, hf * 512:(hf + 1) * 512],
                                     start=(gs % G_EXP == 0 and c == 0 and n == 0), stop=(gs % G_EXP == G_EXP - 1 and c == 1 and n == 2),
                                     skip_group_check=True)
                ins.then_inc(w_used, 1)

            def scatter(e, i, last=False):
                for b in (4, 5):
                    pe.wait_ge(free[b], k0[b] + e + 1 + i)
                for t in range(NT):
                    for hf in range(2):
                        ins = mm(PS[2 * t + hf][:, :], mo.GS[:, t * P:(t + 1) * P], mo.YE[:, hf * 512:(hf + 1) * 512], start=False, stop=last, skip_group_check=True)
                        if last:
                            done(ins, ("y", name, 2 * t + hf))
                if not last:
                    ins.then_inc(sem("moe_scattered"), 1)

            up(0, 0, True)
            up(1, 0)
            down(0, 0)
            with pe.Fori(0, N_EXP - 1) as i:
                for u in range(G_EXP):
                    g = 2 + u
                    up(g, i)
                    if g == G_EXP + 1:
                        scatter(0, i)
                    down(g - 1, i)
            for g in range(2 + (N_EXP - 1) * G_EXP, MOE_GROUPS):
                up(g, 0)
                down(g - 1, 0)
            down(MOE_GROUPS - 1, 0)
            scatter(N_EXP - 1, 0, True)

        def ffn(name, groups, kind):
            w0, k0 = BASE[name], ffn_k0[name]
            body = 2

            def await_split(j, i):
                pe.wait_ge(lo_done, 2 * (w0 + j + 1) + 2 * 3 * body * i)

            def up(gs, i, first=False):
                for half in range(2):
                    j = half if first else 3 * gs - 1 + half
                    b, sl = 4 + 2 * (gs % 2) + half, j % SPLIT
                    await_split(j, i)
                    k = k0[b] + gs // 2
                    if not (isinstance(k, int) and k == 0):
                        pe.wait_ge(free[b], k + (body // 2) * i)
                    for c in range(2):
                        for kk in range(KC):
                            if first and half == 0 and c == 0 and kk % 2 == 0:
                                await_free_of(pe, ("norm", {"ffn0": 1, "ffn1": 3, "ffn2": 5}[name], kk // 2))
                            o = kk * TW + c * P
                            for n, (wt, ht) in enumerate(((WH, HTH), (WH, HTL), (WL, HTH))):
                                ins = mm(PS[b][:, c * 256:(c + 1) * 256], wt[:, sl, o:o + P], ht[:, kk, :],
                                         start=(kk == 0 and n == 0), stop=(kk == KC - 1 and n == 2))
                    ins.then_inc(w_used, 1)

            def down(gs, i, j):
                sl = j % SPLIT
                await_split(j, i)
                pe.wait_ge(sem(name + "_gl"), gs + 1 + body * i)
                if gs == 0:
                    for b in range(4):
                        claim(pe, ("y", name, b))
                last = isinstance(i, int) and gs == groups - 1
                for tt in range(NT):
                    for c in range(2):
                        for n, (gh, wt) in enumerate(((GHH, WH), (GHH, WL), (GHL, WH))):
                            for hf in range(2):
                                o = c * D + hf * 512
                                ins = mm(PS[2 * tt + hf][:, :], gh[:, gs % 2, c, tt * P:(tt + 1) * P], wt[:, sl, o:o + 512],
                                         start=(gs == 0 and c == 0 and n == 0), stop=(last and c == 1 and n == 2),
                                         skip_group_check=True)
                                if last and c == 1 and n == 2 and 2 * tt + hf < 3:
                                    done(ins, ("y", name, 2 * tt + hf))
                ins.then_inc(w_used, 1)

            up(0, 0, True)
            up(1, 0)
            down(0, 0, 4)
            rounds = (groups - 2) // body
            with pe.Fori(0, rounds) as i:
                for u in range(body):
                    g = 2 + u
                    up(g, i)
                    down(g - 1, i, 3 * (g - 1) + 4)
            assert 3 * body % RAW == 0 and 3 * body % SPLIT == 0 and body % 2 == 0
            for g in range(2 + rounds * body, groups):
                up(g, 0)
                down(g - 1, 0, 3 * (g - 1) + 4)
            down(groups - 1, 0, 3 * groups - 1)

        pe.wait_ge(s_const, 32)
        for st in order:
            if st[0] == "norm":
                norm(st[1])
            elif st[0] == "even":
                even()
            elif st[0] == "odd":
                odd()
            elif st[0] == "m2":
                mixer2(*st[1:])
            elif st[0] == "router":
                router()
            elif st[0] == "moe":
                moe(0)
                with pe.If(more_tokens(pe) > 0):
                    moe(1)
            else:
                ffn(*st[1:])

    @block.scalar
    def _(act):
        A = act.activation
        chain = [0]
        s_act = sem("act_chain")

        def link(ins):
            chain[0] += 1
            ins.then_inc(s_act, 1)
            act.wait_ge(s_act, chain[0])

        def logs():
            act.preload_act_table_set("natural_log_exp_and_others")

        def norm(n):
            if n in ffn_of_norm:
                act.preload_act_table(ACT.Silu)
            elif n < 7:
                if n:
                    logs()
                    feed(n)(SPLIT - 1)
            for t in range(NT):
                if n == 0:
                    act.wait_ge(s_in[t], 16)
                else:
                    for b in (2 * t, 2 * t + 1):
                        await_free_of(act, ("y", resid_of[n], b))
                A(HN[:, t, :], X[:, t, :], ACT.Square, scale=D ** -0.5,
                  accum_out=st_ss[:, t:t + 1]).then_inc(sem("mean_sq"), 1)
            g = prm("norm")
            if n == 0:
                act.wait_ge(s_const, 32)
                feed(n)(0)
            if n < 7:
                for b in range(4):
                    await_full(act, ("norm", n, b))
                    if n == 0 and b == 2:
                        feed(n)(1)
                    for k in range(2):
                        c = 2 * b + k
                        ins = A(HTH[:, c, :], bank(("norm", n, b))[:, k * 256:(k + 1) * 256], ACT.Copy, scale=g[:, n * KC + c:n * KC + c + 1])
                    ins.then_inc(sem("ht_hi"), 1)
                if n == 0:
                    feed(n)(SPLIT - 1)
                if n in ffn_of_norm:
                    for k in range(EARLY, SPLIT):
                        hi(ffn_of_norm[n], k, 0)
                return
            for b in range(2):
                key = ("norm", n, b)
                await_full(act, key)
                for k in range(2):
                    c = 2 * b + k
                    ins = A(HT[:, c, :], bank(key)[:, k * 256:(k + 1) * 256], ACT.Copy, scale=g[:, n * KC + c:n * KC + c + 1])
                release(ins, key)

        def hi(name, j, i):
            t = BASE[name] + j
            await_raw(act, t, 2 * i)
            if j >= SPLIT:
                act.wait_ge(w_used, t - SPLIT + 1 + 2 * RAW * i)
            else:
                await_full(act, (prev_mixer[name], "oT", 3 if prev_mixer[name] != "od" else 1))
            A(WH[:, j % SPLIT, :], tile_ap(t), ACT.Copy).then_inc(hi_done, 2)

        def ffn_ahead(mixer):
            n = norm_after[mixer]
            for k in range(EARLY if n in ffn_of_norm else 0):
                hi(ffn_of_norm[n], k, 0)

        def hi_half(name, h):
            t0 = BASE[name + "_in"]
            await_raw(act, t0 + h // 2)
            if h >= SPLIT:
                u = h - SPLIT
                if u % 2:
                    act.wait_ge(w_used, t0 + u // 2 + 1)
                else:
                    act.wait_ge(half_used, firsts_before[name] + u // 2 + 1)
            A(MWH[:, h % SPLIT, :], half_ap(name, h), ACT.Copy).then_inc(hi_done, 1)

        feeders = {n: Feeder(name, hi_half) for n, name in mixer_of_norm.items()}
        feed = feeders.get

        def squares(src, sq, name):
            A(sq, src, ACT.Square).then_inc(sem(name), 1)

        def rsqrt(key, rs, name, scale, o=0, w=512):
            await_full(act, key)
            release(A(rs[:, o:o + w], bank(key)[:, o:o + w], ACT.Ln, scale=scale, bias=eps), key)
            await_free_of(act, key)
            A(rs[:, o:o + w], rs[:, o:o + w], ACT.Exp, scale=-0.5).then_inc(sem(name), 1)

        def attn_step(i, name, heads, groups, combine, SM, EX, PT, parts="et"):
            if i < heads and "e" in parts:
                for c in range(combine):
                    u = i * combine + c
                    act.wait_ge(sem(name + "_mx"), u + 1)
                    if i >= 2 and c == 0:
                        if combine == 1:
                            for g in range(groups):
                                await_full(act, (name, "t", i - 2, g))
                        else:
                            act.wait_ge(sem(name + "_w"), i - 1)
                    b = u % (2 * combine)
                    for n, sl in enumerate((slice(0, P), slice(P, 384))):
                        j = 2 * u + n
                        ins = A(EX[:, b, :, sl], SM[:, u % 2, :, sl], ACT.Exp, bias=st_mx[:, j:j + 1],
                                accum_out=st_sum[:, j:j + 1])
                    ins.then_inc(sem(name + "_e"), 1)
            if i >= 1 and "t" in parts:
                for g in range(groups):
                    key = (name, "t", i - 1, g)
                    await_full(act, key)
                    release(A(PT[:, (i - 1) % 2, g, :], bank(key)[:, 0:384], ACT.Copy), key)

        def attn(*args):
            for i in range(args[1] + 1):
                attn_step(i, *args)

        def out_norm(name, heads, width, sq, sname):
            for t in range(NT):
                key = (name, "o", t)
                await_full(act, key)
                for h in range(heads):
                    ins = A(sq[:, t, h * width:(h + 1) * width], bank(key)[:, h * width:(h + 1) * width], ACT.Square,
                            accum_out=st_o[:, t * 8 + h:t * 8 + h + 1])
                link(ins)
                o = slice(t * 8, t * 8 + heads)
                link(A(st_or[:, o], st_o[:, o], ACT.Ln, scale=1.0 / width, bias=eps))
                A(st_or[:, o], st_or[:, o], ACT.Exp, scale=-0.5).then_inc(sem(sname), 1)

        def out_hi(ins):
            ins.then_inc(sem("out_hi"), 1)

        def out_T(name, j):
            key = (name, "oT", j)
            await_full(act, key)
            out_hi(A(HTH[:, 2 * j:2 * j + 2, :].rearrange("p a b -> p (a b)"), bank(key)[:, :], ACT.Copy))

        def m2_out_T(m, j):
            key = (m, "oT", j)
            await_full(act, key)
            c, n = M2_OT[j][0], len(M2_OT[j])
            out_hi(A(HTH[:, c:c + n, :].rearrange("p a b -> p (a b)"), bank(key)[:, 0:256 * n], ACT.Copy))

        def copy_half(dst, key, j):
            await_full(act, key)
            release(A(dst[:, :, j * 256:(j + 1) * 256], v3(bank(key)[:, :], 2), ACT.Copy), key)

        def even():
            fd = feed(0)
            fd(3)
            key = ("ev", "ar")
            await_full(act, key)
            fd(4)
            release(A(ev.arT[0:16, :], bank(key)[0:16, 0:256], ACT.Copy), key)
            fd(5)
            act.wait_ge(s_prm, 32)
            act.wait_ge(sem("prep"), 1)
            link(A(st_lam, st_lam, ACT.Exp))
            for l in range(2):
                ins = A(st_nea[0:6, l:l + 1], prm(f"alog{l}")[0:6, :], ACT.Exp)
            ins.then_inc(sem("prep_a"), 1)
            key = ("ev", "la")
            await_full(act, key)
            fd(8)
            ba = prm("ba")
            for c in range(2):
                ins = A(ev.T1[:, c * 256:(c + 1) * 256], bank(key)[:, c * 256:(c + 1) * 256], ACT.Abs, bias=ba[:, c:c + 1])
            ins.then_inc(sem("ev_a"), 1)
            act.wait_ge(sem("ev_a"), 1)
            link(A(ev.T1, ev.T1, ACT.Exp, scale=-1.0))
            A(ev.T1, ev.T1, ACT.Ln, bias=one).then_inc(sem("ev_a"), 1)
            fd(9)
            act.wait_ge(sem("ev_b"), 1)
            A(ev.EB, ev.B, ACT.Exp, scale=1.0 / 16)
            A(ev.ENB, ev.B, ACT.Exp, scale=-1.0 / 16).then_inc(sem("ev_a"), 1)
            act.wait_ge(sem("ev_b"), 2)
            A(ev.EW, ev.EW, ACT.Exp, scale=1.0 / 16).then_inc(sem("ev_a"), 1)
            for j in range(2):
                await_full(act, ("ev", "av", j))
                fd(2 * (3 + j) + 4)
                copy_half(ev.V, ("ev", "av", j), j)
                fd(2 * (3 + j) + 5)
            for j in range(2):
                key = ("ev", "ag", j)
                await_full(act, key)
                fd(2 * (5 + j) + 4)
                release(A(ev.GG[:, :, j * 256:(j + 1) * 256], v3(bank(key)[:, :], 2), ACT.Silu), key)
                fd(2 * (5 + j) + 5)
            logs()
            for j in range(4):
                key = ("ev", "bqk", j)
                await_full(act, key)
                fd(2 * (7 + j) + 4)
                if j >= 2:
                    await_full(act, ("ev", "ss", j - 2))
                squares(bank(key)[:, :], ev.SQ[:, j % 2, :], "ev_sq")
                if j == 0:
                    kt = ("ev", "kwT")
                    await_full(act, kt)
                    release(A(ev.KWT.rearrange("p a b -> p (a b)"), bank(kt)[:, :], ACT.Copy), kt)
                if j:
                    if j >= 3:
                        await_free_of(act, ("ev", "bqk", j - 3))
                    rsqrt(("ev", "ss", j - 1), ev.RS[:, (j - 1) % 2, :], "ev_rs", 1.0 / 64)
                fd(2 * (7 + j) + 5)
            da = ("evd", 4, 1, 2, ev.SM, ev.EX, ev.PT)
            attn_step(0, *da)
            out_norm("ev", 4, 128, ev.OSQ, "ev_or")
            await_full(act, ("ev", "bv", 0))
            fd(26)
            copy_half(ev.BV, ("ev", "bv", 0), 0)
            await_free_of(act, ("ev", "bqk", 1))
            rsqrt(("ev", "ss", 3), ev.RS[:, 1, :], "ev_rs", 1.0 / 64)
            fd(27)
            attn_step(1, *da, parts="e")
            await_full(act, ("ev", "bv", 1))
            fd(28)
            copy_half(ev.BV, ("ev", "bv", 1), 1)
            for i in range(1, 5):
                if i == 2:
                    for j in range(2):
                        out_T("ev", j)
                attn_step(i, *da, parts="t" if i == 1 else "et")
                if i > 2:
                    fd(26 + i)
            out_norm("evd", 4, 128, ev.SQ, "ev_or")
            fd(32)
            for j in range(2, 4):
                out_T("ev", j)
            fd(33)
            ffn_ahead("ev")

        def odd():
            fd = feed(2)
            fd(3)
            k = 0
            for g in range(3):
                for j in range(4):
                    key = ("od", "qk", g, j)
                    await_full(act, key)
                    fd(2 * (6 * g + j) + 4)
                    if k >= 2:
                        await_full(act, ("od", "ss", (k - 2) // 4, (k - 2) % 4))
                    squares(bank(key)[:, :], od.SQ[:, k % 2, :], "od_sq")
                    if j:
                        od_scale(k - 1)
                    fd(2 * (6 * g + j) + 5)
                    k += 1
                for j in range(2):
                    await_full(act, ("od", "v", g, j))
                    if (g, j) != (2, 1):
                        fd(2 * (6 * g + 4 + j) + 4)
                    copy_half(od.V[:, g], ("od", "v", g, j), j)
                    if j == 0:
                        od_scale(k - 1)
                    if (g, j) != (2, 1):
                        fd(2 * (6 * g + 4 + j) + 5)
            fd(38)
            attn("od", 4, 3, 1, od.SM, od.EX, od.PT)
            for j in range(2):
                out_T("od", j)
            fd(39)
            ffn_ahead("od")

        def od_scale(k):
            if k >= 2:
                await_free_of(act, ("od", "qk", (k - 2) // 4, (k - 2) % 4))
            rsqrt(("od", "ss", k // 4, k % 4), od.RS[:, k % 2, :], "od_rs", 1.0 / 128)

        def mixer2(m, l):
            fd = feed(4 + 2 * l)
            fd(3)
            key = (m, "in", 7)
            ra = sem(m + "_ra")
            await_full(act, key)
            fd(4)
            abf = bank(key)[:, 256:512]
            RA, RX, RC, RF = [m2.ROW2[0:6, r, :] for r in range(4)]
            BT = m2.ROW[0:6, 2, :]
            A(RX, abf[0:6, :], ACT.Copy)
            link(A(RA, abf[0:6, :], ACT.Abs, bias=prm(f"dtb{l}")[0:6, :]))
            link(A(RA, RA, ACT.Exp, scale=-1.0))
            A(RA, RA, ACT.Ln, bias=one[0:6, :]).then_inc(ra, 1)
            A(BT, abf[32:38, :], ACT.Copy).then_inc(ra, 1)
            link(A(RC, abf[64:70, :], ACT.Copy))
            link(A(RF, RC, ACT.Abs, bias=prm(f"fb{l}")[0:6, :]))
            link(A(RF, RF, ACT.Exp, scale=-1.0))
            A(RF, RF, ACT.Ln, bias=one[0:6, :]).then_inc(ra, 1)
            act.wait_ge(ra, 3)
            A(BT, BT, ACT.Sigmoid).then_inc(ra, 1)
            table = ["other"]
            taps = v3(prm(f"dnconv{l}"), 9)

            def square_of(k):
                j = M2_SUM_ORDER[k]
                if k >= 2:
                    await_full(act, (m, "ss", M2_SUM_ORDER[k - 2]))
                hv = M2_SUM_HALVES[j]
                o, w = 256 * hv[0], 256 * len(hv)
                src = m2.Y[:, 2 * j:2 * j + 2, :].rearrange("p a b -> p (a b)") if j < 3 else bank((m, "in", j))[:, :]
                squares(src[:, o:o + w], m2.SQ[:, k % 2, o:o + w], m + "_sq")

            def scale_of(k):
                j = M2_SUM_ORDER[k]
                if k >= 2:
                    act.wait_ge(sem(m + "_nu"), k - 1)
                hv = M2_SUM_HALVES[j]
                if table[0] != "logs":
                    logs()
                    table[0] = "logs"
                rsqrt((m, "ss", j), m2.RS[:, k % 2, :], m + "_rs", 1.0 if j < 3 else 1.0 / 64, 256 * hv[0], 256 * len(hv))

            square_of(0)
            fd(5)
            for J, j in enumerate(list(range(7)) + [8, 9, 10, 11], 1):
                key = (m, "in", j)
                await_full(act, key)
                fd(2 * J + 4)
                if 1 <= j <= 5 or j in (8, 9):
                    table[0] = "silu"
                if j == 4:
                    square_of(M2_SUM_ORDER.index(j))
                if j < 5:
                    us = [u for u in (2 * j, 2 * j + 1) if u < 9]
                    for u in us:
                        ins = A(m2.Y[:, u, :], bank(key)[:, (u % 2) * 256:(u % 2) * 256 + 256], ACT.Copy, scale=taps[:, u, 3:4])
                    ins.then_inc(sem(m + "_c0"), 1)
                elif j == 8:
                    release(A(m2.ZG[:, :, 0:256], v3(bank(key)[:, :], 2), ACT.Silu), key)
                elif j == 9:
                    A(m2.ZG[:, :, 256:384], v3(bank(key)[:, :], 2)[:, :, 0:P], ACT.Silu).then_inc(sem(m + "_z"), 1)
                    release(A(m2.FV[:, :, 0:P], v3(bank(key)[:, :], 2)[:, :, P:256], ACT.Copy), key)
                elif j == 10:
                    release(A(m2.FV[:, :, P:384], v3(bank(key)[:, :], 2), ACT.Copy), key)
                elif j == 11:
                    release(A(m2.XP, v3(bank(key)[:, :], 2), ACT.Copy), key)
                if 1 <= j <= 5:
                    act.wait_ge(sem(m + "_c1"), j)
                    for u in [u for u in (2 * j - 2, 2 * j - 1) if u < 9]:
                        ins = A(m2.Y[:, u, :], m2.Y[:, u, :], ACT.Silu)
                    if j - 1 < 3:
                        link(ins)
                        square_of(M2_SUM_ORDER.index(j - 1))
                    else:
                        ins.then_inc(sem(m + "_v"), 1)
                if j in (5, 6):
                    square_of(M2_SUM_ORDER.index(j))
                if j in M2_SUMS:
                    scale_of(M2_SUM_ORDER.index(M2_SUMS[j]))
                if J < M2_IN - 1:
                    fd(2 * J + 5)
            key = (m, "py")
            await_full(act, key)
            release(A(m2.PX.rearrange("p a b -> p (a b)"), bank(key)[:, :], ACT.Copy), key)
            key = (m, "pz")
            await_full(act, key)
            ps = prm(f"pscale{l}")
            for c in range(2):
                ins = A(HTH[:, 6 + c, :], bank(key)[:, c * 256:(c + 1) * 256], ACT.Copy, scale=ps[:, c:c + 1])
            out_hi(ins)
            key = (m, "rowT")
            await_full(act, key)
            rows = bank(key)[:, 0:48].rearrange("p (t j h) -> p t j h", t=2, j=4)
            A(st_gc[:, :, 0, :], rows[:, :, 0, :], ACT.Copy)
            A(st_gc[:, :, 1, :], rows[:, :, 3, :], ACT.Copy)
            A(st_tm[:, :, 0:2, :], rows[:, :, 0:2, :], ACT.Exp)
            release(A(st_tm[:, :, 2, :], rows[:, :, 2, :], ACT.Copy), key)
            for j in range(2):
                key = (m, "gb", j)
                w = 2 - j
                await_full(act, key)
                release(A(m2.EGB[:, 2 * j:2 * j + w, :], bank(key)[:, 0:256 * w].rearrange("p (a b) -> p a b", a=w), ACT.Exp), key)
            for q in range(3):
                await_free_of(act, (m, "dec", q))
                z = slice(4 * q, 4 * q + 4)
                A(m2.DEC[:, z, :], m2.DEC[:, z, :], ACT.Exp).then_inc(sem(m + "_dec"), 1)
            fx = (m + "f", FX_H, 1, 1, m2.SM, m2.EX, m2.PT)
            attn_step(0, *fx)
            for s in range(1, GD_STEPS + 1):
                for q in range(3):
                    key = (m, "M", s, q)
                    await_full(act, key)
                    if s > 1:
                        await_full(act, (m, "Y", s - 1, q))
                    else:
                        await_full(act, (m, "pz"))
                    release(A(m2.M1[:, 4 * q:4 * q + 4, :], bank4(key), ACT.Copy), key)
                attn_step(s, *fx)
            for t in range(NT):
                key = (m, "u", t)
                await_full(act, key)
                release(A(m2.UU[:, t, :], bank(key)[:, 0:384], ACT.Copy), key)
            attn_step(GD_STEPS + 1, *fx)
            fd(28)
            for j in range(2):
                m2_out_T(m, j)
            fd(29)
            for t in range(NT):
                key = (m, "o", t)
                await_full(act, key)
                A(m2.OSQ[:, t, :], bank(key)[:, 0:384], ACT.Square).then_inc(sem(m + "_osq"), 1)
                act.wait_ge(sem(m + "_oss"), t + 1)
                o = slice(t * 8, t * 8 + 6)
                link(A(st_or[:, o], st_o[:, o], ACT.Ln, scale=1.0 / 64, bias=eps))
                A(st_or[:, o], st_or[:, o], ACT.Exp, scale=-0.5).then_inc(sem(m + "_ors"), 1)
            fd(31)
            for j in range(2, 4):
                m2_out_T(m, j)
            ffn_ahead(m)

        def router():
            act.wait_ge(sem("r_mx"), 1)
            for t in range(NT):
                ins = A(mo.EX[:, t * 8:t * 8 + 8], mo.LG[:, t * 8:t * 8 + 8], ACT.Exp, bias=st_mx[:, t:t + 1],
                        accum_out=st_sum[:, t:t + 1])
            ins.then_inc(sem("r_e"), 1)

        def moe(p):
            name = moe_name[p]
            w0, k0 = BASE["moe"] + p * MOE_TILES, ffn_k0[name]
            act.preload_act_table(ACT.Silu)
            if p:
                await_full(act, ("y", moe_name[0], 3))
            A(HNH[:, :, :].rearrange("p t d -> p (t d)"), HN[:, :, :].rearrange("p t d -> p (t d)"), ACT.Copy).then_inc(sem("hn_hi"), 1)
            g = prm("norm")
            for c in range(KC):
                key = ("moe", p, "gx", 2 * c)
                await_full(act, key)
                release(A(mo.XG[:, c, 0:4, :].rearrange("p e s -> p (e s)"), bank(key)[:, :], ACT.Copy,
                          scale=g[:, 7 * KC + c:7 * KC + c + 1]), key)
            for j in range(4):
                key = ("moe", p, "selT", j)
                await_full(act, key)
                release(A(mo.SELT[:, 2 * j:2 * j + 2, :].rearrange("p e t -> p (e t)"), bank(key)[:, :], ACT.Copy), key)

            def group(gs, i, first=False):
                hb, b = gs % 2, 6 + gs % 2
                act.wait_ge(w_used, w0 + (1 if first else 3 * gs) + 1 + 3 * G_EXP * i)
                act.wait_ge(free[b], k0[b] + gs // 2 + (G_EXP // 2) * i)
                A(mo.SG[:, hb, :], PS[b][:, 0:256], ACT.Silu).then_inc(sem("moe_silu"), 1)
                act.wait_ge(free[b], k0[b] + gs // 2 + 1 + (G_EXP // 2) * i)
                A(GRH[:, hb, :], mo.GH[:, hb, :], ACT.Copy).then_inc(sem("moe_gh"), 1)
                ts = w0 + (3 * gs + 4 if gs < MOE_GROUPS - 1 else MOE_TILES - 1)
                await_raw(act, ts, 3 * G_EXP // RING * i)
                if gs:
                    act.wait_ge(w_used, w0 + 3 * gs + 2 + 3 * G_EXP * i)
                else:
                    await_full(act, ("moe", p, "gx", 15))
                A(DH[:, :, :].rearrange("p c n -> p (c n)"), tile_ap(ts), ACT.Copy).then_inc(sem("moe_hi"), 1)

            def expert_out(e, i, tile):
                act.wait_ge(w_used, tile + 1 + 3 * G_EXP * i)
                if p or e or not isinstance(i, int):
                    act.wait_ge(sem("moe_scattered"), (N_EXP - 1) * p + e + i)
                A(mo.YE[:, 0:512], PS[4][:, :], ACT.Copy).then_inc(free[4], 1)

            moe_loop(act, group, expert_out, w0)

        def ffn(name, groups, kind):
            w0, k0 = BASE[name], ffn_k0[name]
            body = 2
            f = lambda ap: ap.rearrange("p c t -> p (c t)")
            sv, sc = sem(name + "_v"), sem(name + "_a")

            def split(j, i):
                if j < 3 * groups:
                    hi(name, j, i)

            def group(gs, i, first=False):
                hb, b = gs % 2, 4 + 2 * (gs % 2)
                j = 0 if first else 3 * gs - 1
                dt, dk = 3 * body * i, (body // 2) * i
                act.wait_ge(w_used, w0 + j + 1 + dt)
                if kind != "conv":
                    act.wait_ge(free[b + 1], k0[b + 1] + gs // 2 + dk)
                    A(f(ff.SG[:, hb]), PS[b][:, :], ACT.Silu).then_inc(free[b], 1)
                    split(j + 3, i)
                    split(j + 4, i)
                    act.wait_ge(free[b + 1], k0[b + 1] + gs // 2 + 1 + dk)
                else:
                    if gs >= 2:
                        act.wait_ge(sv, 7 * (gs - 1) + 7 * body * i)
                    off = PRM["conv0" if name == "ffn0" else "conv1"][0]
                    for half, dst in enumerate((ff.YG, ff.YV)):
                        if half:
                            act.wait_ge(w_used, w0 + j + 2 + dt)
                        for c in range(2):
                            unit = off + 4 * (22 * half + 2 * gs + c)
                            col = lambda k: PR[:, unit + k:unit + k + 1] if isinstance(i, int) else \
                                PR[:, bass.ds(8 * body * i + (unit + k), 1)]
                            ins = A(dst[:, hb, c, :], PS[b + half][:, c * 256:(c + 1) * 256], ACT.Identity, scale=col(2), bias=col(3))
                        ins.then_inc(sc, 1)
                        split(j + 3 + half, i)
                    act.wait_ge(sv, 7 * gs + 3 + 7 * body * i)
                    act.wait_ge(free[b], k0[b] + gs // 2 + 1 + dk)
                    A(f(ff.SG[:, hb]), f(ff.YG[:, hb]), ACT.Silu).then_inc(sc, 1)
                    act.wait_ge(sv, 7 * (gs + 1) + 7 * body * i)
                act.wait_ge(w_used, w0 + j + 2 + dt)
                A(GHH[:, hb].rearrange("p c t -> p (c t)"), f(ff.GH[:, hb]), ACT.Copy).then_inc(sem(name + "_gh"), 1)
                if not first:
                    split(j + 5, i)

            group(0, 0, True)
            group(1, 0)
            rounds = (groups - 2) // body
            with act.Fori(0, rounds) as i:
                for u in range(body):
                    group(2 + u, i)
            for g in range(2 + rounds * body, groups):
                group(g, 0)

        logs()
        for st in order:
            if st[0] == "norm":
                norm(st[1])
            elif st[0] == "even":
                even()
            elif st[0] == "odd":
                odd()
            elif st[0] == "m2":
                mixer2(*st[1:])
            elif st[0] == "router":
                router()
            elif st[0] == "moe":
                moe(0)
                with act.If(more_tokens(act) > 0):
                    moe(1)
            else:
                ffn(*st[1:])

    @block.vector
    def _(dve):
        TT, TS, STT = dve.tensor_tensor, dve.tensor_scalar, dve.scalar_tensor_tensor
        chain = [0]
        s_dve = sem("dve_chain")

        def mark(ins):
            chain[0] += 1
            ins.then_inc(s_dve, 1)
            return chain[0]

        def after(n):
            dve.wait_ge(s_dve, n)

        def link(ins):
            after(mark(ins))

        def prep():
            dve.wait_ge(s_prm, 32)
            link(TT(st_lamp, prm("lq"), prm("lk"), MUL))
            dve.tensor_reduce(st_lam, v3(st_lamp, 2), AX.X, ADD).then_inc(sem("prep"), 1)
            TS(st_gain[:, 0:1], prm("dq"), 0.125, None, MUL)
            TS(st_gain[:, 1:2], prm("odq"), 128 ** -0.5, None, MUL)
            for l in range(2):
                TS(st_gain[:, 2 + l:3 + l], prm(f"fxq{l}"), 0.125, None, MUL)
            link(TS(st_dg, prm("diff_gain"), 1.0 - LAMBDA_INIT, None, MUL))

        def prep_exp():
            dve.wait_ge(sem("prep_a"), 1)
            link(TT(st_nlam, st_lam[:, 1:2], st_lam[:, 0:1], SUB))
            link(TS(st_nlam, st_nlam, LAMBDA_INIT, None, SUB))
            link(TS(st_nea[0:6, :], st_nea[0:6, :], -1.0, None, MUL))

        def norm(n):
            for t in range(NT):
                dve.wait_ge(sem("rstd"), NT * n + t + 1)
                TS(HN[:, t, :], X[:, t, :], st_rs[:, t:t + 1], None, MUL).then_inc(sem("hn"), 1)
            g = prm("norm")
            if n == 0:
                dve.wait_ge(s_const, 32)
                feed(n)(0)
            if n < 7:
                for b in range(4):
                    if n == 0 and b == 2:
                        feed(n)(1)
                    dve.wait_ge(sem("ht_hi"), 4 * n + b + 1)
                    for k in range(2):
                        c = 2 * b + k
                        ins = STT(HTL[:, c, :], bank(("norm", n, b))[:, k * 256:(k + 1) * 256], g[:, n * KC + c:n * KC + c + 1],
                                  HTH[:, c, :].bitcast(F32), MUL, SUB)
                    release(ins, ("norm", n, b))
                if n == 0:
                    feed(n)(SPLIT - 1)
                if n in ffn_of_norm:
                    for k in range(EARLY, SPLIT):
                        lo(ffn_of_norm[n], k, 0)
                return
            for b in range(2, 4):
                key = ("norm", n, b)
                await_full(dve, key)
                for k in range(2):
                    c = 2 * b + k
                    ins = TS(HT[:, c, :], bank(key)[:, k * 256:(k + 1) * 256], g[:, n * KC + c:n * KC + c + 1], None, MUL)
                release(ins, key)

        def lo(name, j, i):
            t = BASE[name] + j
            dve.wait_ge(hi_done, 2 * (t + 1) + 4 * RAW * i)
            TT(WL[:, j % SPLIT, :], tile_ap(t), WH[:, j % SPLIT, :].bitcast(F32), SUB).then_inc(lo_done, 2)

        def lo_half(name, h):
            dve.wait_ge(hi_done, 2 * BASE[name + "_in"] + h + 1)
            TT(MWL[:, h % SPLIT, :], half_ap(name, h), MWH[:, h % SPLIT, :].bitcast(F32), SUB).then_inc(lo_done, 1)

        feeders = {n: Feeder(name, lo_half) for n, name in mixer_of_norm.items()}
        feed = feeders.get
        out_parts = [0]

        def await_out_hi():
            out_parts[0] += 1
            dve.wait_ge(sem("out_hi"), out_parts[0])

        def resid(name):
            n = norm_after.get(name)
            if n in ffn_of_norm:
                for k in range(EARLY):
                    lo(ffn_of_norm[n], k, 0)
            elif n in mixer_of_norm:
                feed(n)(SPLIT - 1)
            for b in range(4):
                key = ("y", name, b)
                await_full(dve, key)
                xs = X[:, b // 2, (b % 2) * 512:(b % 2 + 1) * 512]
                release(TT(xs, xs, PS[b][:, :], ADD), key)

        def attn_step(i, name, heads, groups, combine, SM, EX, WC, masks, row=None):
            if i < heads:
                for c in range(combine):
                    u = i * combine + c
                    if u >= 2:
                        dve.wait_ge(sem(name + "_e"), u - 1)
                    for g in range(groups):
                        key = (name, "s", u, g)
                        await_full(dve, key)
                        if row is None:
                            ins = TT(SM[:, u % 2, g, :], bank(key)[:, 0:384], masks(g), ADD)
                        else:
                            for n, sl in enumerate((slice(0, P), slice(P, 384))):
                                ins = STT(SM[:, u % 2, g, sl], bank(key)[:, sl], row(n, u), masks(g)[:, sl], ADD, ADD)
                        release(ins, key)
                    for g in range(groups):
                        await_free_of(dve, (name, "s", u, g))
                    for n, sl in enumerate((slice(0, P), slice(P, 384))):
                        j = 2 * u + n
                        ins = dve.tensor_reduce(st_mx[:, j:j + 1], SM[:, u % 2, :, sl], AX.XY, MAX, negate=True)
                    ins.then_inc(sem(name + "_mx"), 1)
            if combine > 1 and i >= 1:
                h = i - 1
                dve.wait_ge(sem(name + "_e"), 2 * h + 2)
                if h >= 2:
                    await_full(dve, (name, "t", h - 2, 0))
                link(dve.reciprocal(st_ri[:, 4 * h:4 * h + 4], st_sum[:, 4 * h:4 * h + 4]))
                link(TS(st_rl, st_ri[:, 4 * h + 2:4 * h + 4], st_nlam, None, MUL))
                e = 2 * (h % 2)
                sls = (slice(0, P), slice(P, 384))
                for n, sl in enumerate(sls):
                    ins = TS(EX[:, e + 1, 0, sl], EX[:, e + 1, 0, sl], st_rl[:, n:n + 1], None, MUL)
                link(ins)
                for n, sl in enumerate(sls):
                    ins = STT(WC[:, h % 2, 0, sl], EX[:, e, 0, sl], st_ri[:, 4 * h + n:4 * h + n + 1], EX[:, e + 1, 0, sl], MUL, ADD)
                ins.then_inc(sem(name + "_w"), 1)

        def attn(*args):
            for i in range(args[1] + (args[3] > 1)):
                attn_step(i, *args)

        def attn_out(name, heads, width, col):
            dve.wait_ge(sem(name + "_e"), heads)
            link(dve.reciprocal(st_ri[:, 0:2 * heads], st_sum[:, 0:2 * heads]))
            for n in range(NT):
                key = (name, "o", n)
                await_full(dve, key)
                o = bank(key)[:, 0:heads * width].rearrange("p (h v) -> p h v", h=heads)
                ri = st_ri[:, 0:2 * heads].rearrange("p (h n) -> p h n", n=2)[:, :, n]
                dst = HN[:, n, col:col + heads * width].rearrange("p (h v) -> p h v", h=heads)
                release(TT(dst, o, bc(ri, 2, width), MUL), key)

        def out_lo(key, c, n):
            await_out_hi()
            flat = lambda x: x[:, c:c + n, :].rearrange("p a b -> p (a b)")
            release(TT(flat(HTL), bank(key)[:, 0:256 * n], flat(HTH).bitcast(F32), SUB), key)

        def out_T(name, j):
            out_lo((name, "oT", j), 2 * j, 2)

        def even():
            fd = feed(0)
            fd(3)
            prep()
            fd(5)
            prep_exp()
            key = ("ev", "la")
            await_full(dve, key)
            dve.wait_ge(sem("ev_a"), 1)
            ba = prm("ba")
            for c in range(2):
                ins = TS(ev.MN[:, c * 256:(c + 1) * 256], bank(key)[:, c * 256:(c + 1) * 256], ba[:, c:c + 1], 0.0, ADD, MIN)
            release(ins, key)
            fd(8)
            await_free_of(dve, key)
            dve.wait_ge(sem("ev_a"), 2)
            link(TT(ev.MN, ev.MN, ev.T1, SUB))
            dve.tensor_tensor_scan(ev.B, cst("reset"), ev.MN, 0.0, MUL, ADD).then_inc(sem("ev_b"), 1)
            dve.wait_ge(sem("ev_b"), 1)
            b3 = v3(ev.B, 8)
            TT(v3(ev.EW, 8), b3[:, :, CH - 1:CH].broadcast_to([P, 8, CH]), b3, SUB).then_inc(sem("ev_b"), 1)
            fd(9)
            dve.wait_ge(sem("ev_a"), 3)
            key = ("ev", "aq")
            await_full(dve, key)
            release(STT(ev.QD, bank(key)[:, :], 0.125, ev.EB, MUL, MUL), key)
            key = ("ev", "ak")
            await_full(dve, key)
            TT(ev.KD, bank(key)[:, :], ev.ENB, MUL)
            dve.wait_ge(sem("ev_a"), 4)
            release(TT(ev.KW, bank(key)[:, :], ev.EW, MUL), key)
            fd(13)
            await_free_of(dve, ("ev", "ag", 0))
            fd(15)
            await_free_of(dve, ("ev", "ag", 1))
            fd(17)
            gg = ev.GG.rearrange("p t (h v) -> p (t h) v", v=P)
            link(TT(gg, gg, bc(prm("gla_gain"), 1, 8), MUL))
            def scaled(j):
                key = ("ev", "bqk", j)
                dve.wait_ge(sem("ev_rs"), j + 1)
                gain = st_gain[:, 0:1] if j % 2 == 0 else prm("dk")
                release(STT(ev.QK[:, j].rearrange("p c t -> p (c t)"), bank(key)[:, :], gain, ev.RS[:, j % 2, :], MUL, MUL), key)
            for r in range(2):
                key = ("ev", "att", r)
                await_full(dve, key)
                release(TT(ev.ATT[:, 4 * r:4 * r + 4, :], bank4(key), bc(cst("glamask"), 1, 4), MUL), key)
            fd(19)
            fd(20)
            scaled(0)
            fd(21)
            own = bc(blk64.rearrange("p (r v) -> p r v", r=2)[:, :, 0], 2, P)
            for n in range(NCH - 1):
                key = ("ev", "kv", n)
                await_full(dve, key)
                for c in range(2):
                    ins = TT(ev.ST[:, n, c], bank(key)[:, c * 256:(c + 1) * 256].rearrange("p (r v) -> p r v", r=2), own, MUL)
                if n:
                    link(ins)
                    for c in range(2):
                        e = c * 256 + n * CH + CH - 1
                        f = lambda k: ev.ST[:, k, c].rearrange("p r v -> p (r v)")
                        ins = STT(f(n), f(n - 1), ev.EB[:, e:e + 1], f(n), MUL, ADD)
                release(ins, key)
                await_free_of(dve, key)
            fd(22)
            scaled(1)
            fd(24)
            scaled(2)
            fd(25)
            da = ("evd", 4, 1, 2, ev.SM, ev.EX, ev.WC, lambda g: cst("cmask"))
            attn_step(0, *da)
            fd(26)
            scaled(3)
            fd(27)
            attn_step(1, *da)
            gate(("ev", "ev_or"), lambda t, h: ev.GG[:, t, h * P:(h + 1) * P], 0, 0)
            fd(28)
            for i in range(2, 5):
                attn_step(i, *da)
                if i == 2:
                    for j in range(2):
                        out_T("ev", j)
                else:
                    fd(26 + i)
            gate(("evd", "ev_or"), lambda t, h: st_dg, 512, 2)
            fd(32)
            for j in range(2, 4):
                out_T("ev", j)
            fd(33)
            resid("ev")

        def gate(names, factor, col, count):
            for t in range(NT):
                key = (names[0], "o", t)
                dve.wait_ge(sem(names[1]), count + t + 1)
                for h in range(4):
                    ins = STT(HN[:, t, col + h * P:col + (h + 1) * P], bank(key)[:, h * P:(h + 1) * P],
                              st_or[:, t * 8 + h:t * 8 + h + 1], factor(t, h), MUL, MUL)
                release(ins, key)

        def odd():
            fd = feed(2)
            fd(5)
            for k in range(12):
                g, j = divmod(k, 4)
                key = ("od", "qk", g, j)
                J = 6 * g + j + 1
                fd(2 * J + 4)
                dve.wait_ge(sem("od_rs"), k + 1)
                gain = st_gain[:, 1:2] if j < 2 else prm("odk")
                release(STT(od.QK[:, g, j].rearrange("p c t -> p (c t)"), bank(key)[:, :], gain, od.RS[:, k % 2, :], MUL, MUL), key)
                fd(2 * J + 5)
                if j == 3:
                    fd(min(2 * J + 7, 38))
            dve.wait_ge(s_late, 16 * (LATE + 1))
            dm = cst("dmask").rearrange("p (g k) -> p g k", g=3)
            attn("od", 4, 3, 1, od.SM, od.EX, None, lambda g: dm[:, g, :])
            attn_out("od", 4, 128, 0)
            for j in range(2):
                out_T("od", j)
            fd(39)
            resid("od")

        def mixer2(m, l):
            ra = sem(m + "_ra")
            G_, GL_, BT_ = [m2.ROW[0:6, r, :] for r in range(3)]
            R0, R1, R2, R3 = [m2.ROW2[0:6, r, :] for r in range(4)]
            fd = feed(4 + 2 * l)
            fd(4)
            dve.wait_ge(ra, 1)
            link(TS(R1, R1, prm(f"dtb{l}")[0:6, :], 0.0, ADD, MAX))
            link(TT(R1, R1, R0, ADD))
            link(TS(R1, R1, st_nea[0:6, l:l + 1], None, MUL))
            link(dve.tensor_tensor_scan(G_, cst("reset")[0:6, 0:256], R1, 0.0, MUL, ADD))
            g3 = G_.rearrange("p (n c) -> p n c", c=CH)
            TT(GL_.rearrange("p (n c) -> p n c", c=CH), g3[:, :, CH - 1:CH].broadcast_to([6, NCH, CH]), g3, SUB).then_inc(
                sem(m + "_rows"), 1)
            dve.wait_ge(ra, 3)
            link(TS(R1, R2, prm(f"fb{l}")[0:6, :], 0.0, ADD, MIN))
            link(TT(R1, R1, R3, SUB))
            link(dve.tensor_tensor_scan(R2, cst("ones")[0:6, :], R1, 0.0, MUL, ADD))
            TS(R3, R2, -1.0, None, MUL).then_inc(sem(m + "_frow"), 1)
            taps = v3(prm(f"dnconv{l}"), 9)

            def normed(k):
                j = M2_SUM_ORDER[k]
                dve.wait_ge(sem(m + "_rs"), k + 1)
                key = (m, "in", j)
                for c in M2_SUM_HALVES[j]:
                    u = 2 * j + c
                    rs = m2.RS[:, k % 2, c * 256:(c + 1) * 256]
                    if j < 3:
                        ins = STT(m2.QKN[:, u, :], m2.Y[:, u, :], 0.125 if u < 3 else 1.0, rs, MUL, MUL)
                    else:
                        gain = st_gain[:, 2 + l:3 + l] if u < 12 else prm(f"fxk{l}")
                        ins = STT(m2.FQK[:, u - 9, :], bank(key)[:, c * 256:(c + 1) * 256], gain, rs, MUL, MUL)
                n = mark(ins)
                after(n)
                dve.sem_inc(sem(m + "_nu"), 1)
                if j >= 3:
                    dve.sem_inc(free[uses[key][0]], 1)

            fd(5)
            for J, j in enumerate(list(range(7)) + [8, 9], 1):
                fd(2 * J + 4)
                if j < 5:
                    key = (m, "in", j)
                    dve.wait_ge(sem(m + "_c0"), j + 1)
                    us = [u for u in (2 * j, 2 * j + 1) if u < 9]
                    last = {}
                    for s in (1, 2, 3):
                        for u in us:
                            if s > 1:
                                after(last[u])
                            o = (u % 2) * 256
                            ins = STT(m2.Y[:, u, s:256], bank(key)[:, o:o + 256 - s], taps[:, u, 3 - s:4 - s], m2.Y[:, u, s:256], MUL, ADD)
                            if s < 3 or u != us[-1]:
                                last[u] = mark(ins)
                    ins.then_inc(sem(m + "_c1"), 1)
                    if j < 4:
                        dve.wait_ge(sem(m + "_c1"), j + 1)
                        dve.sem_inc(free[uses[key][0]], 1)
                if j in M2_SUMS:
                    normed(M2_SUM_ORDER.index(M2_SUMS[j]))
                fd(2 * J + 5)
            fd(26)
            dve.sem_inc(sem(m + "_qk"), 1)
            dve.wait_ge(sem(m + "_z"), 1)
            zg = m2.ZG.rearrange("p t (h v) -> p (t h) v", v=64)
            link(TT(zg, zg, bc(prm(f"onorm{l}"), 1, 12), MUL))
            key = (m, "pz")
            await_out_hi()
            ps = prm(f"pscale{l}")
            for c in range(2):
                ins = STT(HTL[:, 6 + c, :], bank(key)[:, c * 256:(c + 1) * 256], ps[:, c:c + 1], HTH[:, 6 + c, :].bitcast(F32), MUL, SUB)
            release(ins, key)
            await_free_of(dve, (m, "rowT"))
            link(TT(st_beg, st_tm[:, :, 2, :], st_tm[:, :, 0, :], MUL))
            for j in range(2):
                await_free_of(dve, (m, "gb", j))
            dve.memset(m2.S[:, 0], 0.0)
            TT(m2.QD, m2.QKN[:, 0:3, :], m2.EGB, MUL).then_inc(sem(m + "_qd"), 1)
            dve.wait_ge(sem(m + "_qd"), 1)
            for j in range(2):
                key = (m, "bb", j)
                w = 2 - j
                await_full(dve, key)
                release(TT(m2.KB[:, 2 * j:2 * j + w, :], m2.QKN[:, 3 + 2 * j:3 + 2 * j + w, :],
                           bank(key)[:, 0:256 * w].rearrange("p (a b) -> p a b", a=w), MUL), key)
            h3 = lambda ap: ap.rearrange("p (h v) -> p h v", h=6)
            for t in range(NT):
                key = (m, "kT", t)
                await_full(dve, key)
                TT(h3(m2.KBG[:, t, :]), h3(bank(key)[:, 0:384]), bc(st_beg[:, t, :], 2, 64), MUL)
                release(TT(h3(m2.KDEC[:, t, :]), h3(bank(key)[:, 0:384]), bc(st_tm[:, t, 1, :], 2, 64), MUL), key)
            for t in range(NT):
                key = (m, "vT", t)
                await_full(dve, key)
                release(TT(h3(m2.VB[:, t, :]), h3(bank(key)[:, 0:384]), bc(st_tm[:, t, 2, :], 2, 64), MUL), key)
            for q in range(3):
                key = (m, "dec", q)
                await_full(dve, key)
                for i in range(4):
                    t, h = PAIRS[4 * q + i]
                    ins = TS(m2.DEC[:, 4 * q + i, :], bank(key)[:, i * P:(i + 1) * P], st_gc[:, t, 0, h:h + 1], 0.0, SUB, MIN)
                release(ins, key)
            for name, dst in (("qk", m2.ATQ), ("kk", m2.AT)):
                for q in range(3):
                    key = (m, name, q)
                    await_full(dve, key)
                    dve.wait_ge(sem(m + "_dec"), q + 1)
                    z = slice(4 * q, 4 * q + 4)
                    release(TT(dst[:, z, :], bank4(key), m2.DEC[:, z, :], MUL), key)
                    if name == "kk":
                        await_free_of(dve, (m, "qk", q))
                        await_free_of(dve, key)
                        TT(m2.OF[:, z, :], m2.AT[:, z, :], bc(v3(cst("offd"), 6)[:, 0, :], 1, 4), MUL).then_inc(sem(m + "_of2"), 1)
            dve.wait_ge(sem(m + "_of2"), 3)
            TT(m2.UI, bc(ident, 1, 12), m2.OF, SUB).then_inc(sem(m + "_ui"), 1)
            for q in range(3):
                key = (m, "M", 0, q)
                await_full(dve, key)
                release(TT(m2.DI[:, 4 * q:4 * q + 4, :], bc(ident, 1, 4), bank4(key), SUB), key)
            fx = (m + "f", FX_H, 1, 1, m2.SM, m2.EX, None, lambda g: cst("cmask"), lambda n, h: st_gc[:, n, 1, h:h + 1])
            attn_step(0, *fx)
            for s in range(1, GD_STEPS + 1):
                attn_step(s, *fx)
                for q in range(3):
                    for name, dst in (("X", m2.DI), ("Y", m2.UI)):
                        if name == "X" and s == GD_STEPS:
                            continue
                        key = (m, name, s, q)
                        await_full(dve, key)
                        d = dst[:, 4 * q:4 * q + 4, :]
                        release(TT(d, d, bank4(key), SUB), key)
            for t in range(NT):
                key = (m, "w", t)
                await_full(dve, key)
                release(dve.tensor_copy(m2.WT[:, :, t * P:(t + 1) * P], bank4(key, 3)), key)
            for n in range(NCH):
                t, p0 = n // 2, 64 * (n % 2)
                rp = slice(p0, p0 + 64)
                if n:
                    key = (m, "vp", n)
                    await_full(dve, key)
                    await_free_of(dve, (m, "u", t))
                    release(TT(m2.UU[rp, t, :], m2.UU[rp, t, :], bank(key)[rp, 0:384], SUB), key)
                if n < NCH - 1:
                    key = (m, "kv", n)
                    await_full(dve, key)
                    S1, S0 = m2.S[:, (n + 1) % 2], m2.S[:, n % 2]
                    e = n * CH + CH - 1
                    TT(S1, S0, m2.EGB[:, :, e:e + 1].broadcast_to([P, 3, P]), MUL)
                    link(TT(m2.SN, bank4(key, 3), bc(blk64, 1, 3), MUL))
                    release(TT(S1, S1, m2.SN, ADD), key)
                    await_free_of(dve, key)
                if n == 0:
                    attn_out(m + "f", 6, 64, 384)
                if n == 1:
                    fd(27)
                if n == 2:
                    fd(28)
                    for j in range(2):
                        out_lo((m, "oT", j), M2_OT[j][0], len(M2_OT[j]))
            fd(29)
            for t in range(NT):
                key = (m, "o", t)
                dve.wait_ge(sem(m + "_osq"), t + 1)
                dve.tensor_reduce(st_o[:, t * 8:t * 8 + 6], h3(m2.OSQ[:, t, :]), AX.X, ADD).then_inc(sem(m + "_oss"), 1)
                dve.wait_ge(sem(m + "_ors"), t + 1)
                dst = HN[:, t, 0:384]
                link(TT(h3(dst), h3(bank(key)[:, 0:384]), bc(st_or[:, t * 8:t * 8 + 6], 2, 64), MUL))
                link(TT(dst, dst, m2.ZG[:, t, :], MUL))
                dve.sem_inc(free[uses[key][0]], 1)
            fd(31)
            for j in range(2, 4):
                out_lo((m, "oT", j), M2_OT[j][0], len(M2_OT[j]))
            resid(m)

        def router():
            key = ("router", "logits")
            await_full(dve, key)
            LG, EX_, PB, MASK = mo.LG, mo.EX, mo.PB, mo.MASK
            t2 = lambda ap: ap.rearrange("p (t e) -> p t e", t=2)
            release(dve.tensor_copy(LG, bank(key)[:, 0:16]), key)
            await_free_of(dve, key)
            dve.tensor_reduce(st_mx[:, 0:2], t2(LG), AX.X, MAX, negate=True).then_inc(sem("r_mx"), 1)
            dve.wait_ge(sem("r_e"), 1)
            link(dve.reciprocal(st_ri[:, 0:2], st_sum[:, 0:2]))
            link(TT(t2(PB), t2(EX_), bc(st_ri[:, 0:2], 2, 8), MUL))
            mine = bc(t2(PB), 3, 8)
            other = bc(t2(PB), 2, 8)
            four = lambda ap: ap.rearrange("p (t e f) -> p t e f", t=2, e=8)
            GTR, EQ = four(mo.GTR), four(mo.EQ)
            TT(GTR, other, mine, ALU.is_gt)
            link(TT(EQ, other, mine, ALU.is_equal))
            link(TT(EQ, EQ, bc(cst("before").rearrange("p (e f) -> p e f", e=8), 1, 2), MUL))
            link(TT(GTR, GTR, EQ, ADD))
            link(dve.tensor_reduce(t2(MASK), GTR, AX.X, ADD))
            TS(MASK, MASK, 1.5, None, ALU.is_lt).then_inc(sem("chosen"), 1)
            split_normed(0)
            dve.wait_ge(sem("chosen"), 1)
            link(TT(PB, PB, MASK, MUL))
            link(dve.tensor_reduce(st_sum[:, 2:4], t2(PB), AX.X, ADD))
            link(dve.reciprocal(st_ri[:, 2:4], st_sum[:, 2:4]))
            link(TT(t2(mo.GATE), t2(PB), bc(st_ri[:, 2:4], 2, 8), MUL))
            key = ("router", "place")
            await_full(dve, key)
            link(TS(mo.EX, MASK, -4.0 * S, 4.0 * S, MUL, ADD))
            TT(mo.POS, mo.EX, bank(key)[:, 0:16], ADD)
            link(dve.tensor_reduce(mo.MOST, bank(key)[:, 16:24], AX.X, MAX))
            release(TS(MORE[0:1, :], mo.MOST[0:1, :], P + 0.5, None, ALU.is_gt), key)
            await_free_of(dve, key)
            dve.sem_inc(sem("more"), 1)

        def split_normed(p):
            dve.wait_ge(sem("hn_hi"), p + 1)
            flat = lambda x: x[:, :, :].rearrange("p t d -> p (t d)")
            TT(flat(HNL), flat(HN), flat(HNH).bitcast(F32), SUB).then_inc(sem("hn_lo"), 1)

        def moe(p):
            name = moe_name[p]
            w0, k0 = BASE["moe"] + p * MOE_TILES, ffn_k0[name]
            if p:
                link(TS(mo.POS, mo.POS, -float(P), None, ADD))
                split_normed(p)
            t3 = lambda ap: ap.rearrange("p t e s -> p (t e) s")
            TT(t3(SELR[:, :, :, :]), bc(cst("iota"), 1, 16), bc(mo.POS, 2, P), ALU.is_equal).then_inc(sem("moe_sel"), 1)
            dve.wait_ge(sem("moe_sel"), p + 1)
            TT(t3(mo.GSEL), t3(SELR[:, :, :, :].bitcast(F32)), bc(mo.GATE, 2, P), MUL).then_inc(sem("moe_gsel"), 1)
            g = prm("norm")
            for c in range(KC):
                key = ("moe", p, "gx", 2 * c + 1)
                await_full(dve, key)
                release(TS(mo.XG[:, c, 4:8, :].rearrange("p e s -> p (e s)"), bank(key)[:, :],
                           g[:, 7 * KC + c:7 * KC + c + 1], None, MUL), key)

            def group(gs, i, first=False):
                hb, b = gs % 2, 6 + gs % 2
                dve.wait_ge(sem("moe_silu"), MOE_GROUPS * p + gs + 1 + G_EXP * i)
                TT(mo.GH[:, hb, :], mo.SG[:, hb, :], PS[b][:, 256:512], MUL).then_inc(free[b], 1)
                n = MOE_GROUPS * p + gs + 1 + G_EXP * i
                dve.wait_ge(sem("moe_gh"), n)
                TT(GRL[:, hb, :], mo.GH[:, hb, :], GRH[:, hb, :].bitcast(F32), SUB).then_inc(sem("moe_gl"), 1)
                ts = w0 + (3 * gs + 4 if gs < MOE_GROUPS - 1 else MOE_TILES - 1)
                dve.wait_ge(sem("moe_hi"), n)
                TT(DL[:, :, :].rearrange("p c n -> p (c n)"), tile_ap(ts), DH[:, :, :].rearrange("p c n -> p (c n)").bitcast(F32),
                   SUB).then_inc(sem("moe_lo"), 1)

            def expert_out(e, i, tile):
                dve.wait_ge(w_used, tile + 1 + 3 * G_EXP * i)
                if p or e or not isinstance(i, int):
                    dve.wait_ge(sem("moe_scattered"), (N_EXP - 1) * p + e + i)
                gs = mo.SELT[:, e, :] if isinstance(i, int) else mo.SELT[:, bass.ds(i + e, 1), :].rearrange("p e t -> p (e t)")
                dve.tensor_copy(mo.GS, gs)
                dve.tensor_copy(mo.YE[:, 512:1024], PS[5][:, :]).then_inc(free[5], 1)

            for j in range(4):
                await_free_of(dve, ("moe", p, "selT", j))
            moe_loop(dve, group, expert_out, w0)
            for b in range(4):
                key = ("y", name, b)
                await_full(dve, key)
                release(dve.tensor_copy(X[:, b // 2, (b % 2) * 512:(b % 2 + 1) * 512], PS[b][:, :]), key)

        def ffn(name, groups, kind):
            w0, k0 = BASE[name], ffn_k0[name]
            body = 2
            f = lambda ap: ap.rearrange("p c t -> p (c t)")
            sv, sc = sem(name + "_v"), sem(name + "_a")

            def split(j, i):
                if j < 3 * groups:
                    lo(name, j, i)

            def group(gs, i, first=False):
                hb, b = gs % 2, 4 + 2 * (gs % 2)
                j = 0 if first else 3 * gs - 1
                dt, dk = 3 * body * i, (body // 2) * i
                if kind != "conv":
                    split(j + 3, i)
                    dve.wait_ge(free[b], k0[b] + gs // 2 + 1 + dk)
                    dve.wait_ge(w_used, w0 + j + 2 + dt)
                    TT(f(ff.GH[:, hb]), f(ff.SG[:, hb]), PS[b + 1][:, :], MUL).then_inc(free[b + 1], 1)
                    split(j + 4, i)
                else:
                    off = PRM["conv0" if name == "ffn0" else "conv1"][0]
                    n0 = 7 * gs + 7 * body * i
                    for half, Y in enumerate((ff.YG, ff.YV)):
                        dve.wait_ge(sc, 3 * gs + 1 + half + 3 * body * i)
                        for s in (1, 2):
                            if s == 2:
                                dve.wait_ge(sv, n0 + 2 + 3 * half)
                            for c in range(2):
                                col = off + 4 * (22 * half + 2 * gs + c) + 2 - s
                                w = PR[:, col:col + 1] if isinstance(i, int) else PR[:, bass.ds(8 * body * i + col, 1)]
                                ins = STT(Y[:, hb, c, s:256], PS[b + half][:, c * 256:c * 256 + 256 - s], w, Y[:, hb, c, s:256], MUL, ADD)
                                if s == 2 and c == 1:
                                    ins.then_inc(free[b + half], 1)
                                else:
                                    ins.then_inc(sv, 1)
                        split(j + 3 + half, i)
                    dve.wait_ge(sv, n0 + 6)
                    dve.wait_ge(free[b + 1], k0[b + 1] + gs // 2 + 1 + dk)
                    dve.wait_ge(sc, 3 * gs + 3 + 3 * body * i)
                    TT(f(ff.GH[:, hb]), f(ff.SG[:, hb]), f(ff.YV[:, hb]), MUL).then_inc(sv, 1)
                dve.wait_ge(sem(name + "_gh"), gs + 1 + body * i)
                TT(GHL[:, hb].rearrange("p c t -> p (c t)"), f(ff.GH[:, hb]), GHH[:, hb].rearrange("p c t -> p (c t)").bitcast(F32),
                   SUB).then_inc(sem(name + "_gl"), 1)
                if not first:
                    split(j + 5, i)

            group(0, 0, True)
            group(1, 0)
            rounds = (groups - 2) // body
            with dve.Fori(0, rounds) as i:
                for u in range(body):
                    group(2 + u, i)
            for g in range(2 + rounds * body, groups):
                group(g, 0)
            resid(name)

        for st in order:
            if st[0] == "norm":
                norm(st[1])
            elif st[0] == "even":
                even()
            elif st[0] == "odd":
                odd()
            elif st[0] == "m2":
                mixer2(*st[1:])
            elif st[0] == "router":
                router()
            elif st[0] == "moe":
                moe(0)
                with dve.If(more_tokens(dve) > 0):
                    moe(1)
            else:
                ffn(*st[1:])

    block.__exit__(None, None, None)
    return n_tiles


def pack_params(v):
    prm = np.zeros((P, N_PRM), np.float32)

    def put(name, a):
        o, w = PRM[name]
        a = np.asarray(a).reshape(-1, w)
        prm[:a.shape[0], o:o + w] = a

    def cols(a, n):
        return np.asarray(a).reshape(n, P).transpose(1, 0)

    def rows(a):
        a = np.asarray(a).reshape(1, -1)
        return np.broadcast_to(a, (P, a.shape[1]))

    def column(a, reps):
        return np.concatenate([np.asarray(a).reshape(-1)] * reps).reshape(P, 1)

    norms = [v["norm_mix"][0], v["norm_ffn"][0], v["norm_mix"][1], v["norm_ffn"][1],
             v["norm1_2"][0], v["norm2_2"][0], v["norm1_2"][1], v["norm2_2"][1]]
    put("norm", np.concatenate([cols(g, KC) for g in norms], 1))
    put("ba", cols(v["ev_b_a"][0], 2))
    put("wa2", v["ev_w_a2"][0])
    put("gla_gain", rows(v["ev_gla_gain"][0]))
    put("dq", column(v["ev_dq_gain"][0], 2))
    put("dk", column(v["ev_dk_gain"][0], 2))
    put("lq", rows(np.concatenate([v["ev_lq1"][0], v["ev_lq2"][0]])))
    put("lk", rows(np.concatenate([v["ev_lk1"][0], v["ev_lk2"][0]])))
    put("diff_gain", rows(v["ev_diff_gain"][0]))
    put("odq", column(v["od_q_gain"][0], 1))
    put("odk", column(v["od_k_gain"][0], 1))
    for i in range(2):
        taps = np.concatenate([v["ffn_conv_w"][i][:, 0, :], v["ffn_conv_b"][i][None, :]], 0)
        put(f"conv{i}", taps.reshape(4, 44, P).transpose(2, 1, 0).reshape(P, 176))
        put(f"dnconv{i}", v["dn_conv_2"][i].reshape(4, 9, P).transpose(2, 1, 0).reshape(P, 36))
        put(f"alog{i}", v["dn_a_log_2"][i].reshape(6, 1))
        put(f"dtb{i}", v["dn_dt_bias_2"][i].reshape(6, 1))
        put(f"fb{i}", v["fx_f_bias_2"][i].reshape(6, 1))
        put(f"onorm{i}", rows(v["dn_onorm_2"][i]))
        put(f"fxq{i}", column(v["fx_qnorm_2"][i], 2))
        put(f"fxk{i}", column(v["fx_knorm_2"][i], 2))
        put(f"poolw{i}", v["pool_w_2"][i].reshape(2, P, 64).transpose(1, 0, 2).reshape(P, 128))
        put(f"pscale{i}", cols(v["pool_scale_2"][i], 2))
    put("router", v["router_2"][0].reshape(KC, P, N_EXP).transpose(1, 0, 2).reshape(P, KC * N_EXP))
    return prm


def pack_weights(v):
    w = np.zeros((N_TILES, P, KC * TW), np.float32)

    def put_in(t, mat, cols, at=0):
        a = mat[:, cols]
        w[t].reshape(P, KC, TW)[:, :, at:at + a.shape[1]] = a.reshape(KC, P, a.shape[1]).transpose(1, 0, 2)

    def put_out(t, mat, chunks):
        for k, c in enumerate(chunks):
            w[t].reshape(P, 2, D)[:, k] = mat[c * P:(c + 1) * P]

    def span(o, n=TW):
        return slice(o, o + n)

    m, b = v["ev_w_in"][0], BASE["ev_in"]
    put_in(b, m, span(1536, 16))
    for j, o in enumerate([0, 256, 512, 768, 1024, 1280, 1552, 2064, 1808, 2320, 2576, 2832]):
        put_in(b + 1 + j, m, span(o))
    for j in range(EV_OUT):
        put_out(BASE["ev_out"] + j, v["ev_w_out"][0], (2 * j, 2 * j + 1))
    for j in range(OD_IN):
        put_in(BASE["od_in"] + j, v["od_w_in"][0], span(j * TW))
    for j in range(OD_OUT):
        put_out(BASE["od_out"] + j, v["od_w_out"][0], (2 * j, 2 * j + 1))
    for l in range(2):
        m, b = v["w_in_2"][l], BASE[f"m{l}_in"]
        units = [span(o, P) for o in list(range(0, 1152, P)) + list(range(1548, 2316, P))]
        put_in(b, m, units[14])
        for k, o in enumerate((1536, 1542, 2700)):
            put_in(b, m, span(o, 6), P + 32 * k)
        for j in range(7):
            put_in(b + 1 + j, m, units[2 * j])
            put_in(b + 1 + j, m, units[2 * j + 1], P)
        put_in(b + 8, m, span(1152))
        put_in(b + 9, m, span(1408, P))
        put_in(b + 9, m, span(2316, P), P)
        put_in(b + 10, m, span(2444))
        put_in(b + 11, m, span(2706))
        for j in range(M2_OUT):
            put_out(BASE[f"m{l}_out"] + j, v["w_out_2"][l], M2_OUT_CHUNKS[2 * j:2 * j + 2])

    def ffn(base, groups, gate, up, down):
        for g in range(groups):
            t = base + (0 if g == 0 else 3 * g - 1)
            put_in(t, *gate(g))
            put_in(t + 1, *up(g))
            mat, j = down(g)
            put_out(base + (3 * g + 4 if g < groups - 1 else 3 * groups - 1), mat, (2 * j, 2 * j + 1))

    for l in range(2):
        u, d = v["ffn_w_up"][l], v["ffn_w_down"][l]
        ffn(BASE[f"ffn{l}"], G_FFN, lambda g: (u, span(g * TW)), lambda g: (u, span(D_FF + g * TW)), lambda g: (d, g))
    ffn(BASE["ffn2"], G_FFN, lambda g: (v["ffn_gate_2"][0], span(g * TW)), lambda g: (v["ffn_up_2"][0], span(g * TW)),
        lambda g: (v["ffn_down_2"][0], g))
    ffn(BASE["moe"], G_EXP * N_EXP, lambda g: (v["moe_gate_2"][0, g // G_EXP], span(g % G_EXP * TW)),
        lambda g: (v["moe_up_2"][0, g // G_EXP], span(g % G_EXP * TW)), lambda g: (v["moe_down_2"][0, g // G_EXP], g % G_EXP))
    return w


STOP = None


def kernel(**inputs):
    import concourse.bacc as _bacc
    from concourse import mybir as _mybir
    from concourse.bass_utils import run_bass_kernel_spmd as _run
    v = {k: np.asarray(a) for k, a in inputs.items()}
    cst, sel = constants()
    arrays = {"weights": pack_weights(v), "x": v["x"], "params": pack_params(v), "consts": cst, "selectors": sel}
    nc = _bacc.Bacc("TRN2", target_bir_lowering=False, num_devices=1)
    f32 = _mybir.dt.float32
    aps = [nc.dram_tensor(f"in_{k}", a.shape, f32, kind="ExternalInput").ap() for k, a in arrays.items()]
    out = nc.dram_tensor("out", (1, S, D), f32, kind="ExternalOutput").ap()
    build(nc, aps[0], aps[1], aps[2], aps[3], aps[4], out, STOP)
    r = _run(nc, [{f"in_{k}": a for k, a in arrays.items()}], core_ids=[0])
    return r.results[0]["out"]
```
